# Optimizing a Trainium2 kernel written in Bass

```python
import jax, jax.numpy as jnp
from jax import lax
import numpy as np

D_MODEL = 1024
BATCH = 1
SEQ = 2048
DEPTH = 1

CONV_WIDTH = D_MODEL
CONV_K = 3
MLA_HEADS = 8
QK_NOPE = 128
QK_ROPE = 64
V_HEAD = 128
Q_LORA = 384
KV_LORA = 256
MLA_WIDTH = MLA_HEADS * V_HEAD
ROPE_THETA = 10000.0
Q_BLOCK = 128
EPS = 1e-6

_SEGMENTS = [CONV_WIDTH, CONV_WIDTH, CONV_WIDTH, CONV_WIDTH,
             Q_LORA, KV_LORA, QK_ROPE, MLA_WIDTH,
             D_MODEL, D_MODEL]
N_IN = int(sum(_SEGMENTS))
SPLIT_POINTS = [int(v) for v in np.cumsum(_SEGMENTS)[:-1]]

kernel_name = "hybrid_conv_mla_gated_merge"

def rms_norm(t, g):
    t32 = t.astype(jnp.float32)
    out = t32 * lax.rsqrt(jnp.mean(t32 * t32, axis=-1, keepdims=True) + EPS) * g.astype(jnp.float32)
    return out.astype(t.dtype)

def rope_tables(positions):
    inv_freq = ROPE_THETA ** (-jnp.arange(0, QK_ROPE, 2, dtype=jnp.float32) / QK_ROPE)
    ang = positions.astype(jnp.float32)[..., None] * inv_freq
    return jnp.cos(ang), jnp.sin(ang)

def apply_rope(t, cos, sin):
    half = t.shape[-1] // 2
    t1, t2 = t[..., :half], t[..., half:]
    cos = cos.astype(t.dtype)
    sin = sin.astype(t.dtype)
    return jnp.concatenate([t1 * cos - t2 * sin, t1 * sin + t2 * cos], axis=-1)

def causal_depthwise_conv(u, w):
    k = w.shape[0]
    s = u.shape[1]
    up = jnp.pad(u, ((0, 0), (k - 1, 0), (0, 0)))
    out = up[:, 0:s] * w[0]
    for j in range(1, k):
        out = out + up[:, j:j + s] * w[j]
    return out

def short_conv_branch(a_v, a_b, a_c, a_z, conv_w, w_conv_out):
    y = a_b * causal_depthwise_conv(a_c * a_v, conv_w)
    y = y * jax.nn.silu(a_z)
    return y @ w_conv_out

def causal_mla_attention(q_nope, q_pe, k_nope, k_pe, v):
    s_len = q_nope.shape[1]
    scale = (QK_NOPE + QK_ROPE) ** -0.5
    outs = []
    for i in range(s_len // Q_BLOCK):
        q0, q1 = i * Q_BLOCK, (i + 1) * Q_BLOCK
        sc = (jnp.einsum('bqhd,bkhd->bhqk', q_nope[:, q0:q1], k_nope[:, :q1])
              + jnp.einsum('bqhr,bkr->bhqk', q_pe[:, q0:q1], k_pe[:, :q1]))
        sc = sc.astype(jnp.float32) * scale
        qpos = jnp.arange(q0, q1)[:, None]
        kpos = jnp.arange(q1)[None, :]
        sc = jnp.where(kpos <= qpos, sc, -jnp.inf)
        p = jax.nn.softmax(sc, axis=-1).astype(v.dtype)
        outs.append(jnp.einsum('bhqk,bkhd->bqhd', p, v[:, :q1]))
    return jnp.concatenate(outs, axis=1)

def mla_branch(q_lat, kv_lat, k_rope, b_z, cos, sin, g_q, w_uq, g_kv, w_ukv, w_mla_out):
    bsz, s_len = q_lat.shape[0], q_lat.shape[1]
    q = (rms_norm(q_lat, g_q) @ w_uq).reshape(bsz, s_len, MLA_HEADS, QK_NOPE + QK_ROPE)
    q_nope = q[..., :QK_NOPE]
    q_pe = apply_rope(q[..., QK_NOPE:], cos[:, :, None, :], sin[:, :, None, :])
    kv = (rms_norm(kv_lat, g_kv) @ w_ukv).reshape(bsz, s_len, MLA_HEADS, QK_NOPE + V_HEAD)
    k_nope = kv[..., :QK_NOPE]
    v = kv[..., QK_NOPE:]
    k_pe = apply_rope(k_rope, cos, sin)
    o = causal_mla_attention(q_nope, q_pe, k_nope, k_pe, v).reshape(bsz, s_len, MLA_WIDTH)
    o = o * jax.nn.silu(b_z)
    return o @ w_mla_out

def setup_inputs(seed: int = 0) -> dict:
    key = jax.random.key(seed)
    ks = jax.random.split(key, 20)
    f32 = jnp.float32

    def w(k, shape, fan_in):
        return jax.random.normal(k, shape, f32) * (fan_in ** -0.5)

    def gain(k, shape):
        return 1.0 + 0.01 * jax.random.normal(k, shape, f32)

    x = jax.random.normal(ks[0], (BATCH, SEQ, D_MODEL), f32)
    c = jax.random.normal(ks[1], (BATCH, D_MODEL), f32)
    positions = jnp.broadcast_to(jnp.arange(SEQ, dtype=jnp.int32)[None, :], (BATCH, SEQ))
    return {
        "x": x,
        "c": c,
        "positions": positions,
        "w_ada": w(ks[2], (DEPTH, D_MODEL, 3 * D_MODEL), D_MODEL) * 0.1,
        "b_ada": 0.01 * jax.random.normal(ks[3], (DEPTH, 3 * D_MODEL), f32),
        "g_pre": gain(ks[4], (DEPTH, D_MODEL)),
        "w_in": w(ks[5], (DEPTH, D_MODEL, N_IN), D_MODEL),
        "conv_w": w(ks[6], (DEPTH, CONV_K, CONV_WIDTH), CONV_K),
        "w_conv_out": w(ks[7], (DEPTH, CONV_WIDTH, D_MODEL), CONV_WIDTH),
        "g_q": gain(ks[8], (DEPTH, Q_LORA)),
        "w_uq": w(ks[9], (DEPTH, Q_LORA, MLA_HEADS * (QK_NOPE + QK_ROPE)), Q_LORA),
        "g_kv": gain(ks[10], (DEPTH, KV_LORA)),
        "w_ukv": w(ks[11], (DEPTH, KV_LORA, MLA_HEADS * (QK_NOPE + V_HEAD)), KV_LORA),
        "w_mla_out": w(ks[12], (DEPTH, MLA_WIDTH, D_MODEL), MLA_WIDTH),
        "w_out": w(ks[13], (DEPTH, D_MODEL, D_MODEL), D_MODEL),
        "g_post": gain(ks[14], (DEPTH, D_MODEL)),
    }

def reference(x, c, positions, w_ada, b_ada, g_pre, w_in, conv_w, w_conv_out,
              g_q, w_uq, g_kv, w_ukv, w_mla_out, w_out, g_post):
    cos, sin = rope_tables(positions)
    for l in range(DEPTH):
        mod = c @ w_ada[l] + b_ada[l]
        shift, scale, gate = jnp.split(mod, 3, axis=-1)
        h = rms_norm(x, g_pre[l]) * (1.0 + scale[:, None, :]) + shift[:, None, :]
        proj = h @ w_in[l]
        (a_v, a_b, a_c, a_z, q_lat, kv_lat, k_rope, b_z,
         gate_a, gate_b) = jnp.split(proj, SPLIT_POINTS, axis=-1)
        y_a = short_conv_branch(a_v, a_b, a_c, a_z, conv_w[l], w_conv_out[l])
        y_b = mla_branch(q_lat, kv_lat, k_rope, b_z, cos, sin,
                         g_q[l], w_uq[l], g_kv[l], w_ukv[l], w_mla_out[l])
        m = jax.nn.sigmoid(gate_a) * y_a + jax.nn.sigmoid(gate_b) * y_b
        o = m @ w_out[l]
        x = x + gate[:, None, :] * rms_norm(o, g_post[l])
    return x


_drawn_inputs = setup_inputs


def setup_inputs(seed=0):
    import zlib

    import numpy as np

    out = dict(_drawn_inputs(seed))
    spreads = {}
    factors = {'b_ada': 5.474,
     'g_pre': 8.0,
     'g_q': 22.993,
     'w_uq': 6.15,
     'g_kv': 24.445,
     'w_ukv': 3.416,
     'w_mla_out': 3.444,
     'g_post': 64.0}
    for name, (base, spread) in spreads.items():
        noise = np.random.default_rng([zlib.crc32(name.encode()), seed]).standard_normal(out[name].shape)
        drawn = base * np.exp(spread * noise) if base else spread * noise
        out[name] = __import__('jax').numpy.asarray(drawn.astype(out[name].dtype))
    for name, factor in factors.items():
        out[name] = (out[name] * factor).astype(out[name].dtype)
    return out
```

```python
from contextlib import ExitStack

import numpy as np

import concourse.bass as bass
from concourse import mybir

P = 128
SEQ, D = 2048, 1024
KD = D // P
CH = 512
NCH = SEQ // CH
SB = SEQ // P
HEADS, NOPE, ROPE, VD = 8, 128, 64, 128
Q_LORA, KV_LORA = 384, 256
KQ, KKV = Q_LORA // P, KV_LORA // P
CONV_K = 3
EPS = 1e-6
ROPE_THETA = 10000.0
SCALE = float((NOPE + ROPE) ** -0.5)
HALF = ROPE // 2
MASKED = -3.0e38

N_LAT = 6
N_CONV = 4 * KD
N_GATES = 3 * KD
N_PROJ = N_LAT + N_CONV + N_GATES
T_ADA = N_PROJ
T_QR = T_ADA + KD
T_V = T_QR + HEADS // 2
T_K = T_V + KKV
T_Q = T_K + HEADS
T_MERGE = T_Q + HEADS
PER_CHUNK = 3 * KD
RAW = 4

C_C = 0
C_BADA = C_C + KD
C_GPRE = C_BADA + 2 * KD
C_GQ = C_GPRE + KD
C_GKV = C_GQ + KQ
C_CONV = C_GKV + KKV
C_INV = C_CONV + CONV_K * KD
N_CST = C_INV + 1

ROUND = 12582912.0


def _parts(x, bits, n):
    out = []
    for _ in range(n - 1):
        e = np.floor(np.log2(x))
        step = 2.0 ** (e - bits + 1)
        p = np.floor(x / step) * step
        out.append(float(p))
        x = x - p
    return out + [float(np.float32(x))]


TWO_PI = _parts(2.0 * np.pi, 8, 5)

F32 = mybir.dt.float32
F32R = mybir.dt.float32r
BF16 = mybir.dt.bfloat16
I32 = mybir.dt.int32
ACT = mybir.ActivationFunctionType
ALU = mybir.AluOpType
AX = mybir.AxisListType


def chunk(s):
    return slice(s * CH, (s + 1) * CH)


def block(i):
    return slice(i * P, (i + 1) * P)


SPREAD = [[0, 1, 1, 2], [1, 2, 2, 3], [2, 2, 3, 5], [4, 4, 8, 0]]
STEPS = [4 * (g + 1) for g in range(4)]
STEP0 = [0, 4, 12, 24]
N_STEPS = 40
S_USES = [16, 12, 8, 4]
LAG = 2
PT = 3


def head_plan(last):
    plan, waiting = [], []

    def mul():
        g, j, k = waiting.pop(0)
        plan.append(("mul", g, j, k))
        if j == STEPS[g] - 1:
            plan.append(("out", g))

    for g in range(4):
        j = 0
        for i in range(4):
            nxt = g == 3
            if not (nxt and last):
                r = i if nxt else 4 * (g + 1) + i
                plan.append(("row", nxt, r))
                if r == 15 and not last:
                    plan.append(("fetch", 0))
                if nxt and i < 3:
                    plan.append(("fetch", i + 1))
            if g == 0:
                plan.append(("fetch_v", i))
            for _ in range(SPREAD[g][i]):
                k = STEP0[g] + j
                plan.append(("turn", g, j, k))
                waiting.append((g, j, k))
                if len(waiting) > LAG:
                    mul()
                j += 1
            if not (nxt and last):
                plan.append(("inv", nxt, r))
    while waiting:
        mul()
    return plan


def width_of(t):
    if T_QR <= t < T_V or T_Q <= t < T_MERGE:
        return KQ * P
    if T_K <= t < T_Q:
        return KKV * P
    return 1024


def score_width(r, c):
    return CH if c < r // 4 else (r % 4 + 1) * P


def score_base(r):
    return sum(q // 4 + 1 for q in range(r))


def step_cols(g, j):
    return slice(max(0, j - 4 * g) * P, CH)


T_USES = [len(range(s, N_STEPS, PT)) for s in range(PT)]
H_LO_POOL = (1, 4, 7)
TAB_STEPS = 17
U_SSQ = N_LAT
U_CONV = U_SSQ + 2
U_GATES = U_CONV + N_CONV
N_UNITS = U_GATES + N_GATES
M0 = N_LAT + N_GATES
G_QR, G_V = 0, HEADS // 2
G_K = G_V + SB // 2
G_Q = G_K + HEADS
G_UNITS = G_Q + HEADS



def build(nc, x, xt, cst, pos, b_gate, g_post, wada, w1, wqr, wv, wk, wq, wm, out):
    with ExitStack() as ctx:
        sem = lambda name: ctx.enter_context(nc.semaphore(name))
        sems = lambda name, n: [sem(f"{name}{i}") for i in range(n)]
        dram = lambda name, shape: nc.dram_tensor(name, shape, F32)
        psum = ctx.enter_context(nc.psum_tensor("psum", [P, 8, CH], F32))

        base = (nc.sbuf_base + 63) // 64 * 64

        def at(name, kib, shape, dt=F32):
            return nc.alloc_sbuf_tensor_at(name, [P] + list(shape), dt, offset=base + int(kib * 1024))

        w_raw = at("w_raw", 0, [RAW, 1024])
        w_hi = at("w_hi", 16, [2, 1024], F32R)
        w_lo = at("w_lo", 24, [2, 1024], F32R)
        ones = at("ones", 32, [P])
        ident = at("ident", 32.5, [P])
        ident_b = at("ident_b", 33, [P], BF16)
        mask_b = at("mask_b", 33.25, [P], BF16)
        consts = at("consts", 33.5, [N_CST])
        eps_c = at("eps_c", 33.75, [1])
        a_col = at("a_col", 33.8125, [KD])
        b_col = at("b_col", 33.875, [2 * KD])
        c_hi = at("c_hi", 33.9375, [KD], F32R)
        c_lo = at("c_lo", 34.4375, [KD])
        row_max = at("row_max", 34, [2, NCH])
        row_sum = at("row_sum", 34.0625, [2, NCH])
        neg_max = at("neg_max", 34.125, [2, 1])
        all_sum = at("all_sum", 34.1875, [3, 1])
        inv_sum = at("inv_sum", 34.25, [2, 1])
        o_sq = at("o_sq", 34.3125, [4, 2])
        o_st = at("o_st", 34.34375, [4, 4])
        R = 34.5
        h_hi = at("h_hi", R, [KD, SEQ], F32R)
        h_lo = at("h_lo", R + 64, [KD, SEQ], F32R)
        wa = at("wa", R, [KD, 2 * D])
        x_raw = at("x_raw", R + 64, [KD, SEQ])
        vs = at("vs", R + 128, [SEQ])
        cv = at("cv", R + 136, [SEQ])
        stage = at("stage", R + 144, [2, SEQ])
        u = at("u", R + 160, [SEQ + 2])
        t1 = at("t1", R + 168.0625, [CH])
        t2 = at("t2", R + 170.0625, [CH])
        squares = at("squares", R + 128, [2, 1024])
        r_x = at("r_x", R + 136, [SEQ])
        ang = at("ang", R + 144, [CH])
        pos_i = at("pos_i", R + 146, [CH], I32)
        turns = at("turns", R + 148, [CH])
        s_half = at("s_half", R + 150, [CH])
        tab = at("tab", R + 152, [3, CH])
        qn_hi = at("qn_hi", R, [KQ, SEQ], F32R)
        qn_lo = at("qn_lo", R + 24, [KQ, SEQ], F32R)
        kn_hi = at("kn_hi", R + 48, [KKV, SEQ], F32R)
        kn_lo = at("kn_lo", R + 64, [KKV, SEQ], F32R)
        lat = at("lat", R + 80, [KQ + KKV, SEQ])
        c_b_hi = at("c_b_hi", R + 128, [KD, P], F32R)
        c_b_lo = at("c_b_lo", R + 132, [KD, P], F32R)
        bg = at("bg", R + 136, [D])
        gp = at("gp", R + 140, [D])
        gg = at("gg", R + 120, [D])
        r_lat = at("r_lat", R + 160, [SEQ])
        rope_a = at("rope_a", R + 80, [SEQ])
        rope_b = at("rope_b", R + 88, [SEQ])
        cos_t = at("cos_t", R + 124, [SEQ])
        sin_t = at("sin_t", R + 132, [SEQ])
        k_hi = at("k_hi", R, [SEQ], F32R)
        k_lo = at("k_lo", R + 8, [SEQ], F32R)
        v_hi = at("v_hi", R + 16, [SEQ], F32R)
        v_lo = at("v_lo", R + 24, [SEQ], F32R)
        q_hi = at("q_hi", R + 32, [SEQ], F32R)
        q_lo = at("q_lo", R + 40, [SEQ], F32R)
        qr_s = at("qr_s", R + 48, [SEQ], F32R)
        kr_hi = at("kr_hi", R + 56, [SEQ], F32R)
        kr_lo = at("kr_lo", R + 64, [SEQ], F32R)
        a_raw = at("a_raw", R + 72, [3, SEQ])
        pt_hi = at("pt_hi", R + 96, [PT, CH], F32R)
        pt_lo = at("pt_lo", R + 102, [PT, CH], F32R)
        sz = at("sz", R + 108, [2, CH])
        p_even = [at(f"p_even{i}", R + 124 + 6 * i, [3 * CH]) for i in range(4)]
        p_odd = [at(f"p_odd{i}", R + (112, 148, 156, 164)[i], [4 * CH]) for i in range(4)]
        e_raw = at("e_raw", R, [KD, CH])
        y_hi = at("y_hi", R + 32, [KD, CH], F32R)
        y_lo = at("y_lo", R + 48, [KD, CH], F32R)
        o_hi = at("o_hi", R + 64, [KD, CH], F32R)
        o_lo = at("o_lo", R + 80, [KD, CH], F32R)
        m_hi = at("m_hi", R + 16, [KD, CH], F32R)
        m_lo = at("m_lo", R + 96, [KD, CH], F32R)
        gr = at("gr", R + 112, [4, CH])
        m_a = at("m_a", R + 124, [KD, CH])
        x_t = at("x_t", R + 140, [2, D])
        o_t = at("o_t", R + 148, [2, D])
        e_t = at("e_t", R + 160, [2, CH])
        sq_t = at("sq_t", R + 164, [2, CH])

        lat_d = dram("lat_d", (N_LAT, P, SEQ))
        r_d = dram("r_d", (2, P, SEQ))
        tab_d = dram("tab_d", (3, P, CH))
        y_d = dram("y_d", (KD, P, SEQ))
        gate_d = dram("gate_d", (N_GATES, P, SEQ))
        qr_d = dram("qr_d", (HEADS // 2, P, SEQ))
        v_d = dram("v_d", (SB, P, HEADS * VD))
        k_d = dram("k_d", (HEADS, P, SEQ))
        q_d = dram("q_d", (HEADS, P, SEQ))
        roped_d = dram("roped_d", (1 + HEADS // 2, P, SEQ))
        o_d = dram("o_d", (HEADS, P, SEQ))

        cst_in = sem("cst_in")
        pos_in = sem("pos_in")
        settled = sem("settled")
        settled_g = sem("settled_g")
        x_in = sems("x_in", KD)
        wa_in = sems("wa_in", KD)
        ready = sem("ready")
        ones_ready = sem("ones_ready")
        sq_ready = sem("sq_ready")
        sq_used = sem("sq_used")
        ssq_ready = sem("ssq_ready")
        ada_ready = sem("ada_ready")
        ab_step = sem("ab_step")
        rs = sem("rs")
        rs_root = sem("rs_root")
        xr_ready = sem("xr_ready")
        h32_ready = sem("h32_ready")
        hhi_ready = sem("hhi_ready")
        hlo_v = sem("hlo_v")
        hlo_g = sem("hlo_g")
        tab_step = sem("tab_step")
        tab_sin = sem("tab_sin")
        tab_ready = sem("tab_ready")
        tab_out = sem("tab_out")
        w_in = sems("w_in", RAW)
        whi = sem("whi")
        wlo = sem("wlo")
        p_full = sem("p_full")
        p_free = sems("p_free", 8)
        lat_sq = sem("lat_sq")
        lat_add = sem("lat_add")
        r_ready = sem("r_ready")
        r_out = sems("r_out", 2)
        u_zero = sem("u_zero")
        cv_step = sem("cv_step")
        sg_ready = sem("sg_ready")
        y_ready = sem("y_ready")
        y_out = sem("y_out")
        st_out = sem("st_out")
        cb_step = sem("cb_step")
        bg_in = sem("bg_in")
        g_gate = sem("g_gate")
        gg_step = sem("gg_step")
        g_full = sem("g_full")
        g_free = sems("g_free", 8)
        lat_in = sems("lat_in", KQ + KKV)
        r_in = sem("r_in")
        nrm = sem("nrm")
        nrm_hi = sem("nrm_hi")
        nrm_lo = sem("nrm_lo")
        nrm_lo_g = sem("nrm_lo_g")
        ct_in = sem("ct_in")
        ra_in = sem("ra_in")
        rp_step = sem("rp_step")
        rp_out = sem("rp_out")
        a_in = sems("a_in", 3)
        kr_hi_r = sem("kr_hi_r")
        kr_lo_r = sem("kr_lo_r")
        f_hi = sem("f_hi")
        f_lo = sem("f_lo")
        fr_lo = sem("fr_lo")
        fv_hi = sem("fv_hi")
        fv_lo = sem("fv_lo")
        s_full = sem("s_full")
        s_free = sems("s_free", NCH)
        mx_step = sem("mx_step")
        nm_ready = sem("nm_ready")
        iv_step = sem("iv_step")
        iv_ready = sem("iv_ready")
        p_ready = sem("p_ready")
        t_full = sem("t_full")
        t_free = sems("t_free", PT)
        pt_hi_r = sem("pt_hi_r")
        pv_done = sem("pv_done")
        sz_in = sems("sz_in", 2)
        o_ready = sem("o_ready")
        o_out = sems("o_out", 2)
        e_in = sem("e_in")
        e_hi = sem("e_hi")
        e_lo = sem("e_lo")
        e_full = sem("e_full")
        e_outmm = sem("e_outmm")
        e_free = sems("e_free", 8)
        gr_in = sems("gr_in", 4)
        m_step = sem("m_step")
        m_r = sem("m_r")
        m_hi_r = sem("m_hi_r")
        m_lo_r = sem("m_lo_r")
        x_t_in = sems("x_t_in", 2)
        osq = sem("osq")
        o_root = sem("o_root")
        o_step = sem("o_step")
        o_done = sem("o_done")
        out_done = sems("out_done", 2)

        def prob(r):
            return (p_even, p_odd)[r // 4 % 2][r % 4]

        blk = ctx.enter_context(nc.Block())

        def parts(whi_, wlo_, xhi_, xlo_):
            return [(whi_, xlo_), (wlo_, xhi_), (whi_, xhi_)]

        def accumulate(pe, bank, pairs, start=True, stop=True, skip=False):
            for i, (a, b) in enumerate(pairs):
                last = pe.matmul(bank, a, b, start=start and i == 0, stop=stop and i == len(pairs) - 1,
                                 skip_group_check=skip)
            return last


        @blk.sync
        def _(sp):
            def settle():
                sp.sem_inc(settled, 1)

            def load_w(t, src, width, before):
                if before is not None:
                    sp.wait_ge(wlo, before)
                sp.dma_start(w_raw[:, t % RAW, 0:width], src).then_inc(w_in[t % RAW], 16)

            def load_tile(t):
                if t < T_QR:
                    src = w1[t]
                elif t < T_V:
                    src = wqr[t - T_QR]
                elif t < T_K:
                    src = wv[t - T_V]
                elif t < T_Q:
                    src = wk[t - T_K]
                elif t < T_MERGE:
                    src = wq[t - T_Q]
                else:
                    src = wm[t - T_MERGE]
                load_w(t, src, width_of(t), t - RAW + 1 if t >= RAW else None)

            sp.dma_start(consts[:], cst).then_inc(cst_in, 16)
            for c in range(NCH):
                sp.dma_start(pos_i[c * HALF:(c + 1) * HALF, :],
                             pos[:, chunk(c)].to_broadcast([HALF, CH])).then_inc(pos_in, 16)
            for k in range(KD):
                sp.dma_start(x_raw[:, k, :], xt[k]).then_inc(x_in[k], 16)
            for t in range(2):
                load_tile(t)
            for k in range(KD):
                sp.dma_start(wa[:, k, :], wada[k]).then_inc(wa_in[k], 16)
            for t in range(2, RAW):
                load_tile(t)
            sp.wait_ge(tab_ready, 2)
            sp.dma_start(tab_d.ap().rearrange("a p n -> p a n"), tab[:]).then_inc(tab_out, 16)

            def store(dst, m, free, at_least, dst_view=None):
                if not (isinstance(m, int) and m == 0):
                    sp.wait_ge(st_out, 16 * m)
                    settle()
                for s in range(NCH):
                    sp.wait_ge(free[s], at_least)
                slot = m % 2 if isinstance(m, int) else dst_view
                sp.dma_start(dst, stage[:, slot, :]).then_inc(st_out, 16)

            def banks(sem_list, n):
                return sem_list[4 * (n % 2):4 * (n % 2) + 4]

            for t in range(N_LAT):
                load_tile(t + RAW)
                store(lat_d[t], t, banks(p_free, t), t // 2 + 2)
            sp.wait_ge(r_ready, 2 * NCH)
            sp.dma_start(r_d[0], vs[:]).then_inc(r_out[0], 16)
            sp.wait_ge(r_ready, 3 * NCH)
            sp.dma_start(r_d[1], cv[:]).then_inc(r_out[1], 16)
            with sp.Fori(0, KD) as i:
                for j in range(4):
                    t = N_LAT + j + RAW
                    load_w(t, w1[4 * i + t], 1024, 4 * i + (t - RAW + 1))
                sp.wait_ge(y_ready, 4 * i + 8)
                sp.dma_start(y_d[i], cv[:]).then_inc(y_out, 16)
            with sp.Fori(0, N_GATES // 4) as i:
                for j in range(4):
                    t = N_LAT + N_CONV + j + RAW
                    load_w(t, w1[4 * i + t], 1024, 4 * i + (t - RAW + 1))
                    store(gate_d[4 * i + j], 4 * i + (N_LAT + j), banks(p_free, j),
                          2 * i + (U_GATES // 2 + j // 2 + 2), dst_view=j % 2)
            sp.wait_ge(y_out, 16 * KD + 16)
            sp.dma_start(bg[:], b_gate.to_broadcast([P, D])).then_inc(bg_in, 16)
            sp.dma_start(gp[:], g_post.to_broadcast([P, D])).then_inc(bg_in, 16)
            for t in range(T_ADA + RAW, T_ADA + RAW + 2):
                load_tile(t)
            sp.wait_ge(p_full, 4 * N_UNITS)
            for n in range(2):
                sp.wait_ge(r_out[n], 16)
            sp.wait_ge(st_out, 16 * M0)
            sp.dma_start(r_lat[:], r_d[0]).then_inc(r_in, 16)
            for k in range(KQ + KKV):
                sp.dma_start(lat[:, k, :], lat_d[k]).then_inc(lat_in[k], 16)
            for t in range(T_ADA + RAW + 2, T_ADA + RAW + KD):
                load_tile(t)
            sp.wait_ge(nrm, KQ * NCH)
            sp.dma_start(r_lat[:], r_d[1]).then_inc(r_in, 16)
            sp.wait_ge(tab_out, 16)
            sp.wait_ge(g_gate, KD)
            sp.wait_ge(gg_step, 2)
            for j in range(4):
                rows = slice(HALF * j, HALF * (j + 1))

                def turned(a):
                    return tab_d[a].rearrange("(c f) t -> f c t", c=NCH)

                sp.dma_start(cos_t[rows, :].rearrange("p (c t) -> p c t", c=NCH), turned(0)).then_inc(ct_in, 16)
                sp.dma_start(sin_t[rows, :].rearrange("p (c t) -> p c t", c=NCH),
                             turned(2 if j % 2 == 0 else 1)).then_inc(ct_in, 16)

            def rope_load(n):
                src = lat_d[N_LAT - 1] if n == 0 else qr_d[n - 1]
                if n == 0:
                    sp.wait_ge(nrm_hi, (KQ + KKV) * NCH)
                    sp.wait_ge(nrm_lo, (KQ + KKV - 2) * NCH)
                    sp.wait_ge(nrm_lo_g, 2 * NCH)
                else:
                    sp.wait_ge(st_out, 16 * (M0 + n))
                    sp.wait_ge(rp_out, 16 * n)
                sp.dma_start(rope_a[:], src).then_inc(ra_in, 16)
                for j in range(4):
                    o = j ^ 1
                    sp.dma_start(rope_b[HALF * j:HALF * (j + 1), :],
                                 src[HALF * o:HALF * (o + 1), :]).then_inc(ra_in, 16)

            def rope_store(n):
                sp.wait_ge(rp_step, 3 * (n + 1))
                sp.dma_start(roped_d[n], rope_a[:]).then_inc(rp_out, 16)

            for g in range(G_UNITS):
                if g < G_V:
                    load_tile(T_QR + g + RAW)
                elif g == G_V:
                    load_tile(T_V + RAW)
                    load_tile(T_V + 1 + RAW)
                elif g >= G_K:
                    load_tile(T_K + g - G_K + RAW)
                if g < G_V:
                    dst = qr_d[g]
                elif g < G_K:
                    b = 2 * (g - G_V)
                    dst = v_d[b:b + 2].rearrange("b p n -> p b n")
                elif g < G_Q:
                    dst = k_d[g - G_K]
                else:
                    dst = q_d[g - G_Q]
                sp.wait_ge(st_out, 16 * (M0 + g))
                for s in range(NCH):
                    sp.wait_ge(banks(g_free, g)[s], g // 2 + 2)
                src = stage[:, (M0 + g) % 2, :]
                if G_V <= g < G_K:
                    src = src.rearrange("p (b n) -> p b n", b=2)
                sp.dma_start(dst, src).then_inc(st_out, 16)
                n, part = (g - G_V - 1) // 3, (g - G_V - 1) % 3
                if 0 <= n < 5 and part == 0:
                    rope_load(n)
                if 0 <= n < 5 and part == 2:
                    rope_store(n)

            sp.wait_ge(st_out, 16 * (M0 + G_UNITS))
            sp.wait_ge(rp_out, 16 * 5)
            sp.wait_ge(g_full, 4 * G_UNITS)

            def load_k(h):
                sp.dma_start(a_raw[:, 0, :], k_d[h]).then_inc(a_in[0], 16)

            def load_q(h):
                sp.dma_start(a_raw[:, 1, :], q_d[h]).then_inc(a_in[1], 16)

            def load_qr(pair, half):
                for d in range(2):
                    sp.dma_start(a_raw[ROPE * d:ROPE * (d + 1), 2, :],
                                 roped_d[pair + 1, ROPE * half:ROPE * (half + 1), :]).then_inc(a_in[2], 16)

            def load_v(h):
                sp.dma_start(a_raw[:, 0, :].rearrange("p (b n) -> p b n", b=SB),
                             v_d[:, :, bass.ds(h * VD, VD)].rearrange("b p n -> p b n")).then_inc(a_in[0], 16)

            def load_sz(h, g):
                sp.dma_start(sz[:, g % 2, :], gate_d[h, :, chunk(g)]).then_inc(sz_in[g % 2], 16)

            sp.dma_start(a_raw[:, 0, :], roped_d[0]).then_inc(a_in[0], 16)
            load_q(0)
            load_qr(0, 0)
            load_sz(0, 0)
            load_sz(0, 1)
            sp.wait_ge(kr_lo_r, NCH)
            load_k(0)
            sp.wait_ge(f_lo, 2 * NCH)
            sp.wait_ge(fr_lo, NCH)
            load_v(0)

            def head(h, last, pair=None, half=None):
                if not last:
                    load_q(h + 1)
                    load_qr(pair, half)
                    sp.wait_ge(fv_lo, NCH * h + NCH)
                    load_k(h + 1)
                for g in range(4):
                    if g == 3 and not last:
                        sp.wait_ge(f_lo, 2 * NCH * h + 4 * NCH)
                        settle()
                        sp.wait_ge(fr_lo, NCH * h + 2 * NCH)
                        settle()
                        load_v(h + 1)
                    sp.wait_ge(o_ready, 4 * h + (g + 2))
                    sp.dma_start(o_d[h, :, chunk(g)], sz[:, g % 2, :]).then_inc(o_out[g % 2], 16)
                    if g < 2 or not last:
                        sp.wait_ge(o_out[g % 2], 32 * h + 16 * (g // 2 + 1))
                        if g < 2:
                            load_sz(h, g + 2)
                        else:
                            load_sz(h + 1, g - 2)

            with sp.Fori(0, HEADS // 2 - 1) as j:
                head(2 * j, False, j, 1)
                head(2 * j + 1, False, j + 1, 0)
            head(HEADS - 2, False, HEADS // 2 - 1, 1)
            sp.wait_ge(s_full, N_STEPS * HEADS)
            sp.dma_start(e_raw[:], y_d[:, :, chunk(0)].rearrange("k p n -> p k n")).then_inc(e_in, 16)
            head(HEADS - 1, True)
            for s in range(2):
                sp.wait_ge(o_out[s], 32 * HEADS)

            def merge(c, last):
                cols = bass.ds(c * CH, CH)

                def load_m(j):
                    if last and j + RAW >= PER_CHUNK:
                        return
                    t = T_MERGE + RAW + j
                    load_w(t, wm[(j + RAW) % PER_CHUNK], 1024, PER_CHUNK * c + (t - RAW + 1))

                def load_gr(n):
                    if n < 4:
                        sp.wait_ge(e_free[n + 4], 3 * c + 1)
                    elif n < 12:
                        sp.wait_ge(e_free[n - 4], 3 * c + 2)
                    else:
                        sp.wait_ge(e_free[n - 12], 3 * c + 3)
                    sp.dma_start(gr[:, n % 4, :], gate_d[KD + n, :, cols]).then_inc(gr_in[n % 4], 16)

                for n in range(4):
                    load_gr(n)
                for n in range(KD):
                    load_m(n)
                    if n == 1:
                        sp.wait_ge(e_lo, 16 * c + 8)
                        settle()
                        sp.dma_start(e_raw[:], o_d[:, :, cols].rearrange("k p n -> p k n")).then_inc(e_in, 16)
                    load_gr(n + 4)
                for n in range(KD):
                    load_m(KD + n)
                    if n + 12 < 2 * KD:
                        load_gr(n + 12)
                    if n < 2:
                        sp.wait_ge(o_done, 4 * c + (n + 3))
                        sp.dma_start(x_t[:, n, :], x[4 * c + n]).then_inc(x_t_in[n], 16)
                if not last:
                    sp.wait_ge(e_lo, 16 * c + 16)
                    settle()
                    sp.dma_start(e_raw[:], y_d[:, :, bass.ds(c * CH + CH, CH)].rearrange("k p n -> p k n"))\
                      .then_inc(e_in, 16)
                for n in range(KD):
                    load_m(2 * KD + n)
                for b in range(4):
                    sp.wait_ge(o_done, 4 * c + (b + 5))
                    sp.dma_start(out[4 * c + b], o_t[:, b % 2, :]).then_inc(out_done[b % 2], 16)
                    if b < 2:
                        sp.dma_start(x_t[:, b, :], x[4 * c + (b + 2)]).then_inc(x_t_in[b], 16)

            with sp.Fori(0, NCH - 1) as c:
                merge(c, False)
            merge(NCH - 1, True)
            for s in range(2):
                sp.wait_ge(out_done[s], 16 * (2 * NCH + 1))

        @blk.gpsimd
        def _(pool):
            for b in range(8):
                pool.sem_inc(p_free[b], 1)
                pool.sem_inc(e_free[b], 1)
            for b in range(6):
                pool.sem_inc(g_free[b], 1)
            for c in range(NCH):
                pool.sem_inc(s_free[c], 1)
            for s in range(PT):
                pool.sem_inc(t_free[s], 1)
            pool.sem_inc(y_ready, 4)
            pool.sem_inc(y_out, 16)
            pool.sem_inc(t_full, N_STEPS)
            pool.sem_inc(pv_done, 1)
            pool.sem_inc(p_ready, 2)
            pool.sem_inc(o_ready, 1)
            pool.sem_inc(o_done, 4)
            pool.sem_inc(e_outmm, KD)
            for s in range(2):
                pool.sem_inc(out_done[s], 16)
            pool.memset(ones[:], 1.0).then_inc(ready, 1)
            pool.memset(eps_c[:], EPS).then_inc(ready, 1)
            pool.memset(ident[:], 0.0).then_inc(ready, 1)
            pool.memset(ident_b[:], 0.0).then_inc(ready, 1)
            pool.memset(mask_b[:], 0.0).then_inc(ready, 1)
            pool.wait_ge(ready, 5)
            for m in (ident, ident_b):
                pool.affine_select(out=m[:], in_=m[:], compare_op=ALU.not_equal, fill=1.0, base=0,
                                   pattern=[[-1, P]], channel_multiplier=1).then_inc(ready, 1)
            pool.affine_select(out=mask_b[:], in_=mask_b[:], compare_op=ALU.is_ge, fill=MASKED, base=0,
                               pattern=[[-1, P]], channel_multiplier=1).then_inc(ready, 1)

            def w_low(t, width, n):
                pool.wait_ge(whi, n)
                pool.tensor_tensor(w_lo[:, t % 2, 0:width], w_raw[:, t % RAW, 0:width],
                                   w_hi[:, t % 2, 0:width].bitcast(F32), ALU.subtract).then_inc(wlo, 1)

            for t in range(2):
                w_low(t, 1024, t + 1)
            for s in range(NCH):
                for k in H_LO_POOL:
                    pool.wait_ge(hhi_ready, KD * s + k + 1)
                    pool.tensor_tensor(h_lo[:, k, chunk(s)], x_raw[:, k, chunk(s)],
                                       h_hi[:, k, chunk(s)].bitcast(F32), ALU.subtract).then_inc(hlo_g, 1)
            for t in range(2, RAW):
                w_low(t, 1024, t + 1)
            with pool.Fori(0, (N_PROJ + 2 - RAW) // 4) as i:
                for j in range(4):
                    w_low(RAW + j, 1024, 4 * i + (RAW + j + 1))
            for t in range(N_PROJ + 2, T_QR + 2):
                w_low(t, width_of(t), t + 1)

            def lat_low(k, c, n, dst, j):
                pool.wait_ge(nrm_hi, n)
                pool.tensor_tensor(dst[0][:, j, chunk(c)], lat[:, k, chunk(c)],
                                   dst[1][:, j, chunk(c)].bitcast(F32), ALU.subtract).then_inc(nrm_lo_g, 1)

            for c in range(NCH):
                lat_low(KQ - 1, c, KQ * (c + 1), (qn_lo, qn_hi), KQ - 1)
            w_low(T_QR + 2, width_of(T_QR + 2), T_QR + 3)
            for c in range(NCH):
                lat_low(KQ + KKV - 1, c, KQ * NCH + KKV * (c + 1), (kn_lo, kn_hi), KKV - 1)
            for t in range(T_QR + 3, T_MERGE + 2):
                w_low(t, width_of(t), t + 1)

            for c in range(NCH):
                pool.wait_ge(kr_hi_r, c + 1)
                pool.tensor_tensor(kr_lo[:, chunk(c)], a_raw[:, 0, chunk(c)],
                                   kr_hi[:, chunk(c)].bitcast(F32), ALU.subtract).then_inc(kr_lo_r, 1)

            def fetch(h, c):
                n = 3 * NCH * h + 3 * c
                pool.wait_ge(f_hi, n + 1)
                pool.tensor_tensor(k_lo[:, chunk(c)], a_raw[:, 0, chunk(c)],
                                   k_hi[:, chunk(c)].bitcast(F32), ALU.subtract).then_inc(f_lo, 1)
                pool.wait_ge(f_hi, n + 2)
                pool.tensor_tensor(q_lo[:, chunk(c)], a_raw[:, 1, chunk(c)],
                                   q_hi[:, chunk(c)].bitcast(F32), ALU.subtract).then_inc(f_lo, 1)

            def normalise(h, r):
                pool.wait_ge(iv_ready, SB * h + (r + 1))
                pool.sem_inc(settled_g, 1)
                row = prob(r)[:, 0:P * (r + 1)]
                pool.tensor_scalar(row, row, inv_sum[:, r % 2, :], 1.0, ALU.mult, ALU.mult).then_inc(p_ready, 1)

            def head(h, last):
                for item in head_plan(last):
                    if item[0] == "inv":
                        normalise(h + 1 if item[1] else h, item[2])
                    elif item[0] == "fetch":
                        fetch(h + 1, item[1])
                    elif item[0] == "fetch_v":
                        c = item[1]
                        pool.wait_ge(fv_hi, NCH * h + (c + 1))
                        pool.tensor_tensor(v_lo[:, chunk(c)], a_raw[:, 0, chunk(c)],
                                           v_hi[:, chunk(c)].bitcast(F32), ALU.subtract).then_inc(fv_lo, 1)

            for c in range(NCH):
                fetch(0, c)
            for r in range(4):
                normalise(0, r)
            with pool.Fori(0, HEADS - 1) as h:
                head(h, False)
            head(HEADS - 1, True)

            def merge(c, last):
                def low(j, step=0):
                    t = T_MERGE + 2 + j
                    if not (last and j + 2 >= PER_CHUNK):
                        w_low(t, 1024, PER_CHUNK * c + (t + 1))

                def operand(first, hi, lo):
                    for k in range(KD):
                        pool.wait_ge(e_hi, 16 * c + (first + k + 1))
                        pool.tensor_tensor(lo[:, k, :], e_raw[:, k, :], hi[:, k, :].bitcast(F32),
                                           ALU.subtract).then_inc(e_lo, 1)

                operand(0, y_hi, y_lo)
                low(0)
                low(1)
                operand(KD, o_hi, o_lo)
                for j in range(2, PER_CHUNK):
                    low(j)

            with pool.Fori(0, NCH - 1) as c:
                merge(c, False)
            merge(NCH - 1, True)

        @blk.scalar
        def _(act):
            def w_high(t, width, n=None):
                act.wait_ge(w_in[t % RAW], 16 * (t // RAW + 1) if n is None else n)
                act.activation(w_hi[:, t % 2, 0:width], w_raw[:, t % RAW, 0:width], ACT.Copy).then_inc(whi, 1)

            for k in range(KD):
                act.wait_ge(x_in[k], 16)
                for f in range(2):
                    n = 2 * k + f
                    if n >= 2:
                        act.wait_ge(sq_used, n - 1)
                    act.activation(squares[:, n % 2, :], x_raw[:, k, 1024 * f:1024 * (f + 1)],
                                   ACT.Square).then_inc(sq_ready, 1)
            w_high(0, 1024)
            w_high(1, 1024)

            def root(wait_sem, value):
                act.wait_ge(wait_sem, value)
                act.activation(t2[:], t1[:], ACT.Sqrt).then_inc(rs_root, 1)

            for s in range(NCH):
                root(rs, 4 * s + 1)
            act.wait_ge(tab_step, TAB_STEPS)
            act.activation(s_half[:], ang[:], ACT.Sin, scale=0.5).then_inc(tab_sin, 1)
            act.activation(tab[:, 1, :], ang[:], ACT.Sin).then_inc(tab_sin, 1)
            act.wait_ge(ada_ready, 1)
            for s in range(NCH):
                for k in range(KD):
                    act.wait_ge(h32_ready, KD * s + k + 1)
                    act.activation(h_hi[:, k, chunk(s)], x_raw[:, k, chunk(s)], ACT.Copy).then_inc(hhi_ready, 1)

            act.wait_ge(tab_out, 16)
            for t in range(N_LAT):
                for s in range(NCH):
                    b = 4 * (t % 2) + s
                    act.wait_ge(p_full, 4 * t + s + 1)
                    if t >= 2:
                        act.wait_ge(st_out, 16 * (t - 1))
                        act.wait_ge(lat_sq, 4 * (t - 2) + s + 1)
                    act.activation(stage[:, t % 2, chunk(s)], psum[:, b, :], ACT.Copy).then_inc(p_free[b], 1)
                w_high(t + 2, 1024)
            for n in range(2):
                for s in range(NCH):
                    root(p_free[4 * n + s], U_SSQ // 2 + 2)
            act.wait_ge(r_out[0], 16)
            with act.Fori(0, KD) as i:
                for j in range(4):
                    unit = U_CONV + j
                    if j == 0:
                        for s in range(NCH):
                            act.wait_ge(p_full, 16 * i + (4 * unit + s + 1))
                            act.wait_ge(y_ready, 4 * i + (s + 1))
                            act.activation(vs[:, chunk(s)], psum[:, s, :], ACT.Copy).then_inc(p_free[s], 1)
                    if j == 3:
                        for s in range(NCH):
                            act.wait_ge(p_full, 16 * i + (4 * unit + s + 1))
                            act.wait_ge(p_free[4 + s], 2 * i + (unit // 2 + 1))
                            act.activation(vs[:, chunk(s)], psum[:, 4 + s, :], ACT.Sigmoid).then_inc(sg_ready, 1)
                    t = N_LAT + j + 2
                    act.wait_ge(p_full, 16 * i + 4 * (unit + 1))
                    w_high(t, 1024, 16 * i + 16 * (t // RAW + 1))
            def gates(i, m0, silu):
                for j in range(4):
                    unit = U_GATES + m0 + j
                    for s in range(NCH):
                        b = 4 * (j % 2) + s
                        act.wait_ge(p_full, 16 * i + (4 * unit + s + 1))
                        act.wait_ge(st_out, 64 * i + 16 * (N_LAT + m0 + j - 1))
                        act.activation(stage[:, j % 2, chunk(s)], psum[:, b, :], ACT.Sigmoid)\
                           .then_inc(sg_ready if silu else p_free[b], 1)
                    t = N_LAT + N_CONV + m0 + j + 2
                    act.wait_ge(p_full, 16 * i + 4 * (unit + 1))
                    w_high(t, 1024, 16 * i + 16 * (t // RAW + 1))

            with act.Fori(0, KD // 4) as i:
                gates(i, 0, True)
            with act.Fori(0, KD // 2) as i:
                gates(i, KD, False)

            for t in range(N_PROJ + 2, T_QR + 2):
                act.wait_ge(g_gate, t - T_ADA - 1)
                w_high(t, width_of(t))

            def lat_high(c, ks, dst, base):
                for j, k in enumerate(ks):
                    act.wait_ge(nrm, base + len(ks) * c + j + 1)
                    act.activation(dst[:, j, chunk(c)], lat[:, k, chunk(c)], ACT.Copy).then_inc(nrm_hi, 1)

            for c in range(NCH):
                lat_high(c, range(KQ), qn_hi, 0)
            for g in range(G_UNITS):
                for s in range(NCH):
                    b = 4 * (g % 2) + s
                    act.wait_ge(g_full, 4 * g + s + 1)
                    act.wait_ge(st_out, 16 * (M0 + g - 1))
                    act.activation(stage[:, (M0 + g) % 2, chunk(s)], psum[:, b, :], ACT.Copy).then_inc(g_free[b], 1)
                if g < G_V:
                    w_high(T_QR + g + 2, width_of(T_QR + g + 2))
                elif g == G_K - 1:
                    act.wait_ge(g_full, 4 * G_K)
                    w_high(T_K, width_of(T_K))
                    w_high(T_K + 1, width_of(T_K + 1))
                elif g >= G_K:
                    t = T_K + g - G_K + 2
                    w_high(t, width_of(t))
                if g == 0:
                    for c in range(NCH):
                        lat_high(c, range(KQ, KQ + KKV), kn_hi, KQ * NCH)

            act.wait_ge(a_in[0], 16)
            for c in range(NCH):
                act.activation(kr_hi[:, chunk(c)], a_raw[:, 0, chunk(c)], ACT.Copy).then_inc(kr_hi_r, 1)

            def fetch(h, c):
                act.wait_ge(a_in[0], 32 * h + 32)
                act.activation(k_hi[:, chunk(c)], a_raw[:, 0, chunk(c)], ACT.Copy).then_inc(f_hi, 1)
                act.wait_ge(a_in[1], 16 * h + 16)
                act.activation(q_hi[:, chunk(c)], a_raw[:, 1, chunk(c)], ACT.Copy).then_inc(f_hi, 1)
                act.wait_ge(a_in[2], 32 * h + 32)
                act.activation(qr_s[:, chunk(c)], a_raw[:, 2, chunk(c)], ACT.Copy).then_inc(f_hi, 1)

            def exponentials(h, r):
                g = r // 4
                act.wait_ge(nm_ready, SB * h + (r + 1))
                act.wait_ge(t_full, N_STEPS * h + (STEP0[3], N_STEPS, N_STEPS + STEP0[1], N_STEPS + STEP0[2])[g])
                for c in range(g + 1):
                    w = score_width(r, c)
                    act.activation(prob(r)[:, c * CH:c * CH + w], psum[:, c, 0:w], ACT.Exp,
                                   bias=neg_max[:, r % 2, :], scale=SCALE,
                                   accum_out=row_sum[:, r % 2, c:c + 1]).then_inc(s_free[c], 1)

            def turned(h, g, j, k):
                act.wait_ge(t_full, N_STEPS * h + (N_STEPS + k + 1))
                act.wait_ge(pv_done, N_STEPS * h + (k - PT + 2 if k >= PT else 1))
                cols = step_cols(g, j)
                act.activation(pt_hi[:, k % PT, cols], psum[:, 4 + k % PT, cols], ACT.Copy).then_inc(pt_hi_r, 1)

            def head(h, last):
                for item in head_plan(last):
                    if item[0] == "row":
                        exponentials(h + 1 if item[1] else h, item[2])
                    elif item[0] == "fetch":
                        if item[1] == 0:
                            act.wait_ge(s_full, N_STEPS * h + N_STEPS)
                        fetch(h + 1, item[1])
                    elif item[0] == "fetch_v":
                        c = item[1]
                        if c == 0:
                            act.wait_ge(pv_done, N_STEPS * h + 1)
                            act.wait_ge(a_in[0], 32 * h + 48)
                        act.activation(v_hi[:, chunk(c)], a_raw[:, 0, chunk(c)], ACT.Copy).then_inc(fv_hi, 1)
                    elif item[0] == "turn":
                        turned(h, *item[1:])

            for c in range(NCH):
                fetch(0, c)
            for r in range(4):
                exponentials(0, r)
            with act.Fori(0, HEADS - 1) as h:
                head(h, False)
            head(HEADS - 1, True)

            def merge(c, last):
                def high(j):
                    if last and j + 2 >= PER_CHUNK:
                        return
                    if j < 2 * KD:
                        act.wait_ge(e_full, 16 * c + (j + 1))
                    else:
                        act.wait_ge(e_outmm, KD * c + (KD + j - 2 * KD + 1))
                    t = T_MERGE + j + 2
                    w_high(t, 1024, 16 * (PER_CHUNK // RAW) * c + 16 * (t // RAW + 1))

                def operand(first, hi):
                    act.wait_ge(e_in, 32 * c + (16 if first == 0 else 32))
                    for k in range(KD):
                        act.activation(hi[:, k, :], e_raw[:, k, :], ACT.Copy).then_inc(e_hi, 1)

                operand(0, y_hi)
                high(0)
                high(1)
                operand(KD, o_hi)
                for j in range(2, KD):
                    high(j)
                for n in range(KD):
                    high(KD + n)
                    act.wait_ge(m_r, KD * c + (n + 1))
                    act.activation(m_hi[:, n, :], m_a[:, n, :], ACT.Copy).then_inc(m_hi_r, 1)
                for n in range(KD):
                    high(2 * KD + n)
                act.wait_ge(e_outmm, KD * c + 2 * KD)
                for b in range(4):
                    for f in range(2):
                        if 2 * b + f >= 2:
                            act.wait_ge(osq, 8 * c + (2 * b + f - 1))
                        act.activation(sq_t[:, f, :], psum[:, 2 * b + f, :], ACT.Square,
                                       accum_out=o_sq[:, b, f:f + 1]).then_inc(osq, 1)
                for b in range(4):
                    act.wait_ge(o_step, 24 * c + (6 * b + 2))
                    act.activation(o_st[:, b, 1:2], o_st[:, b, 0:1], ACT.Sqrt).then_inc(o_root, 1)

            with act.Fori(0, NCH - 1) as c:
                merge(c, False)
            merge(NCH - 1, True)

        @blk.vector
        def _(dve):
            steps = [0]

            def tab_do(ins):
                ins.then_inc(tab_step, 1)
                steps[0] += 1
                dve.wait_ge(tab_step, steps[0])

            dve.wait_ge(cst_in, 16)
            dve.wait_ge(pos_in, 16 * NCH)
            tab_do(dve.tensor_copy(ang[:], pos_i[:]))
            tab_do(dve.tensor_scalar(ang[:], ang[:], consts[:, C_INV:C_INV + 1], None, ALU.mult))
            for unit in (2048.0, 1.0):
                tab_do(dve.tensor_scalar(turns[:], ang[:], float(1.0 / (2.0 * np.pi * unit)), ROUND,
                                         ALU.mult, ALU.add))
                tab_do(dve.tensor_scalar(turns[:], turns[:], -ROUND, None, ALU.add))
                for part in TWO_PI:
                    tab_do(dve.scalar_tensor_tensor(out=ang[:], in0=turns[:], scalar=-part * unit, in1=ang[:],
                                                    op0=ALU.mult, op1=ALU.add))
            tab_do(dve.tensor_scalar(ang[:], ang[:], 3.1415925, -3.1415925, ALU.min, ALU.max))
            assert steps[0] == TAB_STEPS

            def rsqrt_rest(r_ap, root_n, chain, last_sem):
                dve.wait_ge(rs_root, root_n)
                dve.reciprocal(r_ap, t2[:]).then_inc(rs, 1)
                dve.wait_ge(rs, chain + 1)
                dve.scalar_tensor_tensor(out=t2[:], in0=r_ap, scalar=-0.5, in1=r_ap, op0=ALU.mult,
                                         op1=ALU.mult).then_inc(rs, 1)
                dve.wait_ge(rs, chain + 2)
                dve.tensor_tensor(t2[:], t2[:], t1[:], ALU.mult).then_inc(rs, 1)
                dve.wait_ge(rs, chain + 3)
                dve.scalar_tensor_tensor(out=r_ap, in0=t2[:], scalar=1.5, in1=r_ap, op0=ALU.add,
                                         op1=ALU.mult).then_inc(last_sem, 1)

            for s in range(NCH):
                dve.wait_ge(ssq_ready, s + 1)
                dve.tensor_scalar(t1[:], psum[:, s, :], 1.0 / D, EPS, ALU.mult, ALU.add).then_inc(rs, 1)
                rsqrt_rest(r_x[:, chunk(s)], s + 1, 4 * s + 1, r_ready)
            for s in range(NCH):
                dve.wait_ge(r_ready, s + 1)
                for k in range(KD):
                    dve.tensor_tensor(x_raw[:, k, chunk(s)], x_raw[:, k, chunk(s)], r_x[:, chunk(s)],
                                      ALU.mult).then_inc(xr_ready, 1)
            dve.wait_ge(tab_sin, 1)
            dve.scalar_tensor_tensor(out=tab[:, 0, :], in0=s_half[:], scalar=-2.0, in1=s_half[:],
                                     op0=ALU.mult, op1=ALU.mult).then_inc(tab_step, 1)
            dve.wait_ge(tab_step, TAB_STEPS + 1)
            dve.tensor_scalar(tab[:, 0, :], tab[:, 0, :], 1.0, None, ALU.add).then_inc(tab_ready, 1)
            dve.wait_ge(tab_sin, 2)
            dve.tensor_scalar(tab[:, 2, :], tab[:, 1, :], -1.0, None, ALU.mult).then_inc(tab_ready, 1)
            dve.wait_ge(ada_ready, 1)
            dve.tensor_tensor(b_col[:], psum[:, 4, 0:2 * KD], consts[:, C_BADA:C_BADA + 2 * KD],
                              ALU.add).then_inc(ab_step, 1)
            dve.wait_ge(ab_step, 1)
            dve.scalar_tensor_tensor(out=a_col[:], in0=b_col[:, KD:2 * KD], scalar=1.0,
                                     in1=consts[:, C_GPRE:C_GPRE + KD], op0=ALU.add,
                                     op1=ALU.mult).then_inc(ab_step, 1)
            dve.wait_ge(ab_step, 2)
            for s in range(NCH):
                for k in range(KD):
                    dve.wait_ge(xr_ready, KD * s + k + 1)
                    dve.tensor_scalar(x_raw[:, k, chunk(s)], x_raw[:, k, chunk(s)], a_col[:, k:k + 1],
                                      b_col[:, k:k + 1], ALU.mult, ALU.add).then_inc(h32_ready, 1)
                for k in range(KD):
                    if k not in H_LO_POOL:
                        dve.wait_ge(hhi_ready, KD * s + k + 1)
                        dve.tensor_tensor(h_lo[:, k, chunk(s)], x_raw[:, k, chunk(s)],
                                          h_hi[:, k, chunk(s)].bitcast(F32), ALU.subtract).then_inc(hlo_v, 1)

            for t in range(KQ + KKV):
                dst = vs if t < KQ else cv
                for s in range(NCH):
                    dve.wait_ge(p_free[4 * (t % 2) + s], t // 2 + 2)
                    st = stage[:, t % 2, chunk(s)]
                    if t in (0, KQ):
                        dve.tensor_tensor(dst[:, chunk(s)], st, st, ALU.mult).then_inc(lat_sq, 1)
                    else:
                        dve.tensor_tensor(u[:, chunk(s)], st, st, ALU.mult).then_inc(lat_sq, 1)
                        dve.wait_ge(lat_sq, 4 * t + s + 1)
                        done = 4 * (t - 1 if t < KQ else t - 2)
                        if t == 2:
                            dve.wait_ge(lat_add, s + 1)
                        dve.tensor_tensor(dst[:, chunk(s)], dst[:, chunk(s)], u[:, chunk(s)],
                                          ALU.add).then_inc(lat_add, 1)
            for n, (dst, width) in enumerate(((vs, Q_LORA), (cv, KV_LORA))):
                for s in range(NCH):
                    b = 4 * n + s
                    dve.wait_ge(p_full, 4 * (U_SSQ + n) + s + 1)
                    dve.tensor_scalar(t1[:], psum[:, b, :], 1.0 / width, EPS, ALU.mult,
                                      ALU.add).then_inc(p_free[b], 1)
                    rsqrt_rest(dst[:, chunk(s)], NCH * (n + 1) + s + 1, 4 * NCH + 3 * (NCH * n + s), r_ready)
            dve.memset(u[:, 0:2], 0.0).then_inc(u_zero, 1)
            dve.wait_ge(u_zero, 1)
            for n in range(2):
                dve.wait_ge(r_out[n], 16)
            with dve.Fori(0, KD) as i:
                n = U_CONV // 2 + 2
                for s in range(NCH):
                    dve.wait_ge(p_full, 16 * i + (4 * (U_CONV + 1) + s + 1))
                    dve.wait_ge(p_free[s], 2 * i + n)
                    dve.tensor_tensor(u[:, 2 + s * CH:2 + (s + 1) * CH], psum[:, 4 + s, :], vs[:, chunk(s)],
                                      ALU.mult).then_inc(p_free[4 + s], 1)
                for s in range(NCH):
                    dve.wait_ge(p_free[4 + s], 2 * i + n)
                dve.wait_ge(y_out, 16 * i + 16)
                for tap in range(CONV_K):
                    col = C_CONV + tap * KD
                    w_tap = consts[:, bass.ds(i + col, 1)]
                    if tap == 0:
                        dve.tensor_scalar(cv[:], u[:, 0:SEQ], w_tap, None, ALU.mult).then_inc(cv_step, 1)
                    else:
                        dve.wait_ge(cv_step, 3 * i + tap)
                        dve.scalar_tensor_tensor(out=cv[:], in0=u[:, tap:tap + SEQ], scalar=w_tap, in1=cv[:],
                                                 op0=ALU.mult, op1=ALU.add).then_inc(cv_step, 1)
                dve.wait_ge(cv_step, 3 * i + 3)
                for s in range(NCH):
                    dve.wait_ge(p_full, 16 * i + (4 * (U_CONV + 2) + s + 1))
                    dve.tensor_tensor(cv[:, chunk(s)], psum[:, s, :], cv[:, chunk(s)],
                                      ALU.mult).then_inc(p_free[s], 1)
                for s in range(NCH):
                    dve.wait_ge(sg_ready, 4 * i + (s + 1))
                    dve.tensor_tensor(vs[:, chunk(s)], psum[:, 4 + s, :], vs[:, chunk(s)],
                                      ALU.mult).then_inc(p_free[4 + s], 1)
                for s in range(NCH):
                    dve.wait_ge(p_free[4 + s], 2 * i + (n + 1))
                    dve.wait_ge(p_free[s], 2 * i + (n + 1))
                    dve.tensor_tensor(cv[:, chunk(s)], vs[:, chunk(s)], cv[:, chunk(s)],
                                      ALU.mult).then_inc(y_ready, 1)
            with dve.Fori(0, KD // 4) as i:
                for j in range(4):
                    for s in range(NCH):
                        b = 4 * (j % 2) + s
                        dve.wait_ge(sg_ready, 16 * i + (4 * KD + 4 * j + s + 1))
                        dve.tensor_tensor(stage[:, j % 2, chunk(s)], psum[:, b, :], stage[:, j % 2, chunk(s)],
                                          ALU.mult).then_inc(p_free[b], 1)

            dve.tensor_copy(c_hi[:], consts[:, C_C:C_C + KD]).then_inc(cb_step, 1)
            dve.wait_ge(cb_step, 1)
            dve.tensor_tensor(c_lo[:], consts[:, C_C:C_C + KD], c_hi[:].bitcast(F32),
                              ALU.subtract).then_inc(cb_step, 1)
            dve.wait_ge(cb_step, 2)
            for k in range(KD):
                dve.tensor_scalar(c_b_hi[:, k, :], ones[:], c_hi[:, k:k + 1].bitcast(F32), None,
                                  ALU.mult).then_inc(cb_step, 1)
                dve.tensor_scalar(c_b_lo[:, k, :], ones[:], c_lo[:, k:k + 1], None,
                                  ALU.mult).then_inc(cb_step, 1)

            def lat_norm(c, ks, r_n, g0):
                dve.wait_ge(r_in, r_n)
                for k in ks:
                    dve.wait_ge(lat_in[k], 16)
                    dve.scalar_tensor_tensor(out=lat[:, k, chunk(c)], in0=lat[:, k, chunk(c)],
                                             scalar=consts[:, g0 + k:g0 + k + 1], in1=r_lat[:, chunk(c)],
                                             op0=ALU.mult, op1=ALU.mult).then_inc(nrm, 1)

            def lat_low(c, ks, hi, lo, base):
                for j, k in enumerate(ks):
                    if j == len(ks) - 1:
                        continue
                    dve.wait_ge(nrm_hi, base + len(ks) * c + j + 1)
                    dve.tensor_tensor(lo[:, j, chunk(c)], lat[:, k, chunk(c)], hi[:, j, chunk(c)].bitcast(F32),
                                      ALU.subtract).then_inc(nrm_lo, 1)

            for c in range(NCH):
                lat_norm(c, range(KQ), 16, C_GQ)
                lat_low(c, range(KQ), qn_hi, qn_lo, 0)
            dve.wait_ge(bg_in, 32)
            dve.wait_ge(g_gate, KD)
            for f in range(2):
                half = slice(f * CH, (f + 1) * CH)
                dve.tensor_tensor(gg[:, half], psum[:, 6 + f, :], bg[:, half], ALU.add).then_inc(g_free[6 + f], 1)
                dve.wait_ge(g_free[6 + f], 1)
                dve.tensor_tensor(gg[:, half], gg[:, half], gp[:, half], ALU.mult).then_inc(gg_step, 1)
            for c in range(NCH):
                lat_norm(c, range(KQ, KQ + KKV), 32, C_GQ)
                lat_low(c, range(KQ, KQ + KKV), kn_hi, kn_lo, KQ * NCH)
            dve.wait_ge(ct_in, 16 * 8)
            for n in range(5):
                dve.wait_ge(ra_in, 80 * (n + 1))
                dve.tensor_tensor(rope_a[:], rope_a[:], cos_t[:], ALU.mult).then_inc(rp_step, 1)
                dve.tensor_tensor(rope_b[:], rope_b[:], sin_t[:], ALU.mult).then_inc(rp_step, 1)
                dve.wait_ge(rp_step, 3 * n + 2)
                dve.tensor_tensor(rope_a[:], rope_a[:], rope_b[:], ALU.add).then_inc(rp_step, 1)

            MX = N_STEPS + SB

            def rotary_low(h, c):
                dve.wait_ge(f_hi, 3 * NCH * h + 3 * (c + 1))
                dve.tensor_tensor(qr_s[ROPE:P, chunk(c)], a_raw[ROPE:P, 2, chunk(c)],
                                  qr_s[ROPE:P, chunk(c)].bitcast(F32), ALU.subtract).then_inc(fr_lo, 1)

            def row_maximum(h, r):
                nb = r // 4 + 1
                first = score_base(r)
                for c in range(nb):
                    dve.wait_ge(s_full, N_STEPS * h + (first + c + 1))
                    dve.tensor_reduce(row_max[:, r % 2, c:c + 1], psum[:, c, 0:score_width(r, c)], AX.X,
                                      ALU.max).then_inc(mx_step, 1)
                dve.wait_ge(mx_step, MX * h + (first + r + nb))
                dve.tensor_reduce(all_sum[:, 2, :], row_max[:, r % 2, 0:nb], AX.X, ALU.max).then_inc(mx_step, 1)
                dve.wait_ge(mx_step, MX * h + (first + r + nb + 1))
                dve.tensor_scalar(neg_max[:, r % 2, :], all_sum[:, 2, :], -SCALE, None,
                                  ALU.mult).then_inc(nm_ready, 1)

            def row_inverse(h, r):
                nb = r // 4 + 1
                for c in range(nb):
                    dve.wait_ge(s_free[c], S_USES[c] * h + (r - 4 * c + 2))
                dve.tensor_reduce(all_sum[:, r % 2, :], row_sum[:, r % 2, 0:nb], AX.X, ALU.add).then_inc(iv_step, 1)
                dve.wait_ge(iv_step, SB * h + (r + 1))
                dve.wait_ge(p_ready, SB * h + (r + 1))
                dve.reciprocal(inv_sum[:, r % 2, :], all_sum[:, r % 2, :]).then_inc(iv_ready, 1)

            def head(h, last):
                for item in head_plan(last):
                    if item[0] == "row":
                        row_maximum(h + 1 if item[1] else h, item[2])
                    elif item[0] == "fetch":
                        rotary_low(h + 1, item[1])
                    elif item[0] == "inv":
                        row_inverse(h + 1 if item[1] else h, item[2])
                    elif item[0] == "turn":
                        g, j, k = item[1:]
                        cols = step_cols(g, j)
                        dve.wait_ge(pt_hi_r, N_STEPS * h + (k + 1))
                        dve.tensor_tensor(pt_lo[:, k % PT, cols], psum[:, 4 + k % PT, cols],
                                          pt_hi[:, k % PT, cols].bitcast(F32),
                                          ALU.subtract).then_inc(t_free[k % PT], 1)
                    elif item[0] == "out":
                        g = item[1]
                        dve.wait_ge(pv_done, N_STEPS * h + (STEP0[g] + STEPS[g] + 1))
                        dve.wait_ge(sz_in[g % 2], 32 * h + 16 * (g // 2 + 1))
                        dve.tensor_tensor(sz[:, g % 2, :], psum[:, 7, :], sz[:, g % 2, :],
                                          ALU.mult).then_inc(o_ready, 1)

            for c in range(NCH):
                rotary_low(0, c)
            for r in range(4):
                row_maximum(0, r)
                row_inverse(0, r)
            with dve.Fori(0, HEADS - 1) as h:
                head(h, False)
            head(HEADS - 1, True)

            def merge(c, last):
                for n in range(KD):
                    dve.wait_ge(e_full, 16 * c + (n + 1))
                    dve.wait_ge(gr_in[n % 4], 64 * c + 16 * (n // 4 + 1))
                    dve.tensor_tensor(m_a[:, n, :], psum[:, n, :], gr[:, n % 4, :], ALU.mult).then_inc(e_free[n], 1)

                def low(n):
                    dve.wait_ge(m_hi_r, KD * c + (n + 1))
                    dve.tensor_tensor(m_lo[:, n, :], m_a[:, n, :], m_hi[:, n, :].bitcast(F32),
                                      ALU.subtract).then_inc(m_lo_r, 1)

                for n in range(KD):
                    dve.wait_ge(e_full, 16 * c + (KD + n + 1))
                    dve.wait_ge(gr_in[n % 4], 64 * c + 16 * (2 + n // 4 + 1))
                    if n >= 2:
                        dve.wait_ge(m_r, KD * c + (n - 1))
                    dve.tensor_tensor(e_t[:, n % 2, :], psum[:, n, :], gr[:, n % 4, :],
                                      ALU.mult).then_inc(e_free[n], 1)
                    dve.wait_ge(e_free[n], 3 * c + 3)
                    dve.tensor_tensor(m_a[:, n, :], m_a[:, n, :], e_t[:, n % 2, :], ALU.add).then_inc(m_r, 1)
                    if n >= 1:
                        low(n - 1)
                low(KD - 1)
                for b in range(4):
                    sq, st = o_sq[:, b, :], lambda k: o_st[:, b, k:k + 1]
                    base = 24 * c + 6 * b
                    dve.wait_ge(osq, 8 * c + (2 * b + 2))
                    dve.tensor_tensor(st(0), o_sq[:, b, 0:1], o_sq[:, b, 1:2], ALU.add).then_inc(o_step, 1)
                    dve.wait_ge(o_step, base + 1)
                    dve.tensor_scalar(st(0), st(0), 1.0 / D, EPS, ALU.mult, ALU.add).then_inc(o_step, 1)
                    dve.wait_ge(o_root, 4 * c + (b + 1))
                    dve.reciprocal(st(2), st(1)).then_inc(o_step, 1)
                    dve.wait_ge(o_step, base + 3)
                    dve.scalar_tensor_tensor(out=st(3), in0=st(2), scalar=-0.5, in1=st(2), op0=ALU.mult,
                                             op1=ALU.mult).then_inc(o_step, 1)
                    dve.wait_ge(o_step, base + 4)
                    dve.tensor_tensor(st(3), st(3), st(0), ALU.mult).then_inc(o_step, 1)
                    dve.wait_ge(o_step, base + 5)
                    dve.scalar_tensor_tensor(out=st(2), in0=st(3), scalar=1.5, in1=st(2), op0=ALU.add,
                                             op1=ALU.mult).then_inc(o_step, 1)
                    dve.wait_ge(o_step, base + 6)
                    dve.wait_ge(out_done[b % 2], 32 * c + 16 * (b // 2 + 1))
                    for f in range(2):
                        half = slice(f * CH, (f + 1) * CH)
                        dve.scalar_tensor_tensor(out=o_t[:, b % 2, half], in0=psum[:, 2 * b + f, :], scalar=st(2),
                                                 in1=gg[:, half], op0=ALU.mult,
                                                 op1=ALU.mult).then_inc(e_free[2 * b + f], 1)
                    for f in range(2):
                        dve.wait_ge(e_free[2 * b + f], 3 * c + 4)
                    dve.wait_ge(x_t_in[b % 2], 32 * c + 16 * (b // 2 + 1))
                    dve.tensor_tensor(o_t[:, b % 2, :], o_t[:, b % 2, :], x_t[:, b % 2, :],
                                      ALU.add).then_inc(o_done, 1)

            with dve.Fori(0, NCH - 1) as c:
                merge(c, False)
            merge(NCH - 1, True)

        @blk.tensor
        def _(pe):
            pe.wait_ge(ready, 8)
            for k in range(KD):
                for f in range(2):
                    n = 2 * k + f
                    pe.wait_ge(sq_ready, n + 1)
                    for e in range(2):
                        last = pe.matmul(psum[:, 2 * f + e, :], ones[:], squares[:, n % 2, chunk(e)],
                                         start=k == 0, stop=k == KD - 1)
                        if k == KD - 1:
                            last.then_inc(ssq_ready, 1)
                        elif e == 1:
                            last.then_inc(sq_used, 1)
            pe.wait_ge(cst_in, 16)
            for k in range(KD):
                pe.wait_ge(wa_in[k], 16)
                for n in range(2 * KD):
                    last = pe.matmul(psum[:, 4, n:n + 1], wa[:, k, block(n)], consts[:, C_C + k:C_C + k + 1],
                                     start=k == 0 and n == 0, stop=k == KD - 1, skip_group_check=True)
            last.then_inc(ada_ready, 1)

            def w_tile(p, k, n=P):
                return w_hi[:, p, k * n:(k + 1) * n], w_lo[:, p, k * n:(k + 1) * n]

            def unit(p, kk, x_hi, x_lo, full, free, tile_n, free_n, before=None):
                pe.wait_ge(wlo, tile_n)
                for s in range(NCH):
                    pe.wait_ge(free[4 * p + s], free_n)
                    if before:
                        before(s)
                    pairs = []
                    for k in range(kk):
                        pairs += parts(*w_tile(p, k), x_hi[:, k, chunk(s)], x_lo[:, k, chunk(s)])
                    accumulate(pe, psum[:, 4 * p + s, :], pairs).then_inc(full, 1)

            def h_chunk(s):
                pe.wait_ge(hlo_v, (KD - len(H_LO_POOL)) * (s + 1))
                pe.wait_ge(hlo_g, len(H_LO_POOL) * (s + 1))

            for t in range(N_LAT):
                unit(t % 2, KD, h_hi, h_lo, p_full, p_free, t + 1, t // 2 + 1, h_chunk if t == 0 else None)
            for n, src in enumerate((vs, cv)):
                for s in range(NCH):
                    pe.wait_ge(p_free[4 * n + s], U_SSQ // 2 + 1)
                    pe.wait_ge(lat_add, 4 * (KQ - 2) + s + 1 if n == 0 else 4 * (KQ - 1) + s + 1)
                    pe.matmul(psum[:, 4 * n + s, :], ones[:], src[:, chunk(s)], start=True,
                              stop=True).then_inc(p_full, 1)
            with pe.Fori(0, (N_CONV + N_GATES) // 4) as i:
                for j in range(4):
                    unit(j % 2, KD, h_hi, h_lo, p_full, p_free, 4 * i + (N_LAT + j + 1),
                         2 * i + (U_CONV // 2 + j // 2 + 1))

            for b in range(8):
                pe.wait_ge(p_free[b], N_UNITS // 2 + 1)
            pe.wait_ge(cb_step, 2 + 2 * KD)
            for k in range(KD):
                t = T_ADA + k
                pe.wait_ge(wlo, t + 1)
                for f in range(2):
                    last = accumulate(pe, psum[:, 6 + f, :],
                                      parts(c_b_hi[:, k, :], c_b_lo[:, k, :], w_hi[:, t % 2, chunk(f)],
                                            w_lo[:, t % 2, chunk(f)]), start=k == 0, stop=k == KD - 1)
                last.then_inc(g_gate, 1)

            def qn_chunk(s):
                pe.wait_ge(nrm_lo, (KQ - 1) * (s + 1))
                pe.wait_ge(nrm_lo_g, s + 1)

            for g in range(G_V):
                unit(g % 2, KQ, qn_hi, qn_lo, g_full, g_free, T_QR + g + 1, g // 2 + 1, qn_chunk if g == 0 else None)
            pe.wait_ge(wlo, T_V + KKV)
            for g in range(G_V, G_K):
                for s in range(NCH):
                    b, f = 2 * (g - G_V) + s // 2, s % 2
                    pe.wait_ge(nrm_lo, (KQ - 1) * NCH + (KKV - 1) * (b // 4 + 1))
                    pe.wait_ge(nrm_lo_g, NCH + b // 4 + 1)
                    bank = 4 * (g % 2) + s
                    pe.wait_ge(g_free[bank], g // 2 + 1)
                    pairs = []
                    for k in range(KKV):
                        pairs += parts(kn_hi[:, k, block(b)], kn_lo[:, k, block(b)],
                                       w_hi[:, k, chunk(f)], w_lo[:, k, chunk(f)])
                    accumulate(pe, psum[:, bank, :], pairs).then_inc(g_full, 1)
            for first, tile, kk, hi, lo in ((G_K, T_K, KKV, kn_hi, kn_lo), (G_Q, T_Q, KQ, qn_hi, qn_lo)):
                with pe.Fori(0, HEADS // 2) as i:
                    for j in range(2):
                        unit(j, kk, hi, lo, g_full, g_free, 2 * i + (tile + j + 1), i + (first // 2 + 1))

            for b in range(8):
                pe.wait_ge(g_free[b], G_UNITS // 2 + 1)
            pe.wait_ge(kr_lo_r, NCH)

            def scores(h, r):
                nb = r // 4 + 1
                pe.wait_ge(f_lo, 2 * NCH * h + 2 * nb)
                pe.wait_ge(fr_lo, NCH * h + nb)
                for c in range(nb):
                    w = score_width(r, c)
                    cols = slice(c * CH, c * CH + w)
                    bank = psum[:, c, 0:w]
                    pe.wait_ge(s_free[c], S_USES[c] * h + (r - 4 * c + 1))
                    rows = block(r)
                    pe.matmul(bank, q_hi[:, rows], k_lo[:, cols], start=True, stop=False)
                    pe.matmul(bank, q_lo[:, rows], k_hi[:, cols], start=False, stop=False)
                    pe.matmul(bank, qr_s[:, rows], kr_lo[:, cols], start=False, stop=False)
                    pe.matmul(bank, qr_s[:, rows], kr_hi[:, cols], start=False, stop=False)
                    if c == nb - 1:
                        pe.matmul(psum[:, c, w - P:w], ident_b[:], mask_b[:], start=False, stop=False)
                    pe.matmul(bank, q_hi[:, rows], k_hi[:, cols], start=False, stop=True).then_inc(s_full, 1)

            def head(h, last):
                for item in head_plan(last):
                    if item[0] == "row":
                        scores(h + 1 if item[1] else h, item[2])
                    elif item[0] == "turn":
                        g, j, k = item[1:]
                        slot = k % PT
                        if j == 0:
                            pe.wait_ge(p_ready, SB * h + (4 * g + 6))
                        pe.wait_ge(t_free[slot], T_USES[slot] * h + (k // PT + 1))
                        for i in range(max(0, j - 4 * g), 4):
                            ins = pe.transpose(psum[:, 4 + slot, block(i)], prob(4 * g + i)[:, block(j)], ident[:])
                        ins.then_inc(t_full, 1)
                    elif item[0] == "mul":
                        g, j, k = item[1:]
                        slot = k % PT
                        if j == 0:
                            pe.wait_ge(o_ready, 4 * h + (g + 1))
                        pe.wait_ge(fv_lo, NCH * h + (j // 4 + 1))
                        pe.wait_ge(t_free[slot], T_USES[slot] * h + (k // PT + 2))
                        cols = step_cols(g, j)
                        accumulate(pe, psum[:, 7, cols], parts(v_hi[:, block(j)], v_lo[:, block(j)],
                                                               pt_hi[:, slot, cols], pt_lo[:, slot, cols]),
                                   start=j == 0, stop=j == STEPS[g] - 1).then_inc(pv_done, 1)

            for r in range(4):
                scores(0, r)
            with pe.Fori(0, HEADS - 1) as h:
                head(h, False)
            head(HEADS - 1, True)

            for c in range(NCH):
                pe.wait_ge(s_free[c], S_USES[c] * HEADS + 1)
            for s in range(PT):
                pe.wait_ge(t_free[s], T_USES[s] * HEADS + 1)
            pe.wait_ge(o_ready, 4 * HEADS + 1)

            def merge(c):
                for n in range(2 * KD):
                    hi, lo = (y_hi, y_lo) if n < KD else (o_hi, o_lo)
                    pe.wait_ge(wlo, PER_CHUNK * c + (T_MERGE + n + 1))
                    pe.wait_ge(e_free[n % KD], 3 * c + (n // KD + 1))
                    for k in range(KD):
                        if n % KD == 0:
                            pe.wait_ge(e_lo, 16 * c + (n + k + 1))
                        last = accumulate(pe, psum[:, n % KD, :], parts(*w_tile(n % 2, k), hi[:, k, :], lo[:, k, :]),
                                          start=k == 0, stop=k == KD - 1)
                    last.then_inc(e_full, 1)
                for k in range(KD):
                    pe.wait_ge(wlo, PER_CHUNK * c + (T_MERGE + 2 * KD + k + 1))
                    pe.wait_ge(m_lo_r, KD * c + (k + 1))
                    for b in range(4):
                        for f in range(2):
                            if k == 0:
                                pe.wait_ge(e_free[2 * b + f], 3 * c + 3)
                            last = accumulate(pe, psum[:, 2 * b + f, :],
                                              parts(m_hi[:, k, block(b)], m_lo[:, k, block(b)],
                                                    w_hi[:, k % 2, chunk(f)], w_lo[:, k % 2, chunk(f)]),
                                              start=k == 0, stop=k == KD - 1)
                    last.then_inc(e_outmm, 1)

            with pe.Fori(0, NCH) as c:
                merge(c)


def kernel(x, c, positions, w_ada, b_ada, g_pre, w_in, conv_w, w_conv_out, g_q, w_uq, g_kv, w_ukv,
           w_mla_out, w_out, g_post):
    import numpy as _np
    import concourse.bacc as _bacc
    from concourse import mybir as _mybir
    from concourse.bass_utils import run_bass_kernel_spmd as _run

    def cols(v, n):
        return _np.ascontiguousarray(v.reshape(n, P).T)

    def tiles(w, perm=None):
        k, n = w.shape
        return w.reshape(k // P, P, n // P, P).transpose(2, 1, 0, 3).reshape(n // P, P, k)

    x, w_ada, b_ada, w_in, w_uq, w_ukv = (_np.asarray(a) for a in (x[0], w_ada[0], b_ada[0], w_in[0], w_uq[0], w_ukv[0]))
    inv_freq = (_np.float64(ROPE_THETA) ** (-_np.arange(0, ROPE, 2) / ROPE)).astype(_np.float32)
    cst = _np.concatenate([cols(_np.asarray(c[0]), KD), cols(b_ada[:2 * D], 2 * KD), cols(_np.asarray(g_pre[0]), KD),
                           cols(_np.asarray(g_q[0]), KQ), cols(_np.asarray(g_kv[0]), KKV),
                           cols(_np.asarray(conv_w[0]).reshape(-1), CONV_K * KD),
                           _np.tile(inv_freq, 4)[:, None]], axis=1)
    conv = tiles(w_in[:, :4 * D]).reshape(4, KD, P, D)
    lat0 = 4 * D
    rope0 = lat0 + Q_LORA + KV_LORA
    w_rope = w_in[:, rope0:rope0 + ROPE]
    w1 = _np.concatenate([
        tiles(w_in[:, lat0:rope0]),
        tiles(_np.concatenate([w_rope, w_rope], axis=1)),
        conv[[0, 2, 1, 3]].transpose(1, 0, 2, 3).reshape(N_CONV, P, D),
        tiles(w_in[:, rope0 + ROPE:]),
        w_ada[:, 2 * D:].reshape(KD, P, D),
    ])
    uq = w_uq.reshape(Q_LORA, HEADS, NOPE + ROPE)
    ukv = w_ukv.reshape(KV_LORA, HEADS, NOPE + VD)
    arrays = {
        "x": x.reshape(SB, P, D),
        "xt": x.T.reshape(KD, P, SEQ),
        "cst": cst,
        "pos": _np.asarray(positions),
        "b_gate": b_ada[None, 2 * D:],
        "g_post": _np.asarray(g_post),
        "wada": w_ada[:, :2 * D].reshape(KD, P, 2 * D),
        "w1": w1,
        "wqr": tiles(uq[:, :, NOPE:].reshape(Q_LORA, HEADS * ROPE)),
        "wv": ukv[:, :, NOPE:].reshape(KKV, P, HEADS * VD),
        "wk": tiles(ukv[:, :, :NOPE].reshape(KV_LORA, HEADS * NOPE)),
        "wq": tiles(uq[:, :, :NOPE].reshape(Q_LORA, HEADS * NOPE)),
        "wm": _np.concatenate([tiles(_np.asarray(w_conv_out[0])), tiles(_np.asarray(w_mla_out[0])),
                               _np.asarray(w_out[0]).reshape(KD, P, D)]),
    }
    nc = _bacc.Bacc("TRN2", target_bir_lowering=False, num_devices=1)
    args, named = {}, {}
    for name, a in arrays.items():
        a = _np.ascontiguousarray(a)
        named[f"in_{name}"] = a
        args[name] = nc.dram_tensor(f"in_{name}", a.shape, _mybir.dt.from_np(a.dtype), kind="ExternalInput").ap()
    out = nc.dram_tensor("out", (SB, P, D), F32, kind="ExternalOutput").ap()
    build(nc, out=out, **args)
    r = _run(nc, [named], core_ids=[0])
    return r.results[0]["out"].reshape(1, SEQ, D)
```

```python
from contextlib import ExitStack

import numpy as np

import concourse.bass as bass
from concourse import mybir

P = 128
SEQ, D = 2048, 1024
KD = D // P
CH = 512
NCH = SEQ // CH
SB = SEQ // P
HEADS, NOPE, ROPE, VD = 8, 128, 64, 128
Q_LORA, KV_LORA = 384, 256
KQ, KKV = Q_LORA // P, KV_LORA // P
CONV_K = 3
EPS = 1e-6
ROPE_THETA = 10000.0
SCALE = float((NOPE + ROPE) ** -0.5)
HALF = ROPE // 2
MASKED = -3.0e38

N_LAT = 6
N_CONV = 4 * KD
N_GATES = 3 * KD
N_PROJ = N_LAT + N_CONV + N_GATES
T_ADA = N_PROJ
T_QR = T_ADA + KD
T_V = T_QR + HEADS // 2
T_K = T_V + KKV
T_Q = T_K + HEADS
T_MERGE = T_Q + HEADS
PER_CHUNK = 3 * KD
RAW = 4

C_C = 0
C_BADA = C_C + KD
C_GPRE = C_BADA + 2 * KD
C_GQ = C_GPRE + KD
C_GKV = C_GQ + KQ
C_CONV = C_GKV + KKV
C_INV = C_CONV + CONV_K * KD
N_CST = C_INV + 1

ROUND = 12582912.0


def _parts(x, bits, n):
    out = []
    for _ in range(n - 1):
        e = np.floor(np.log2(x))
        step = 2.0 ** (e - bits + 1)
        p = np.floor(x / step) * step
        out.append(float(p))
        x = x - p
    return out + [float(np.float32(x))]


TWO_PI = _parts(2.0 * np.pi, 8, 5)

F32 = mybir.dt.float32
F32R = mybir.dt.float32r
BF16 = mybir.dt.bfloat16
I32 = mybir.dt.int32
ACT = mybir.ActivationFunctionType
ALU = mybir.AluOpType
AX = mybir.AxisListType


def chunk(s):
    return slice(s * CH, (s + 1) * CH)


def block(i):
    return slice(i * P, (i + 1) * P)


SPREAD = [[0, 1, 1, 1, 1], [0, 2, 2, 2, 2], [0, 2, 3, 3, 4], [4, 3, 3, 3, 3]]
STEPS = [4 * (g + 1) for g in range(4)]
STEP0 = [0, 4, 12, 24]
N_STEPS = 40
PT = 3


def head_plan(last):
    plan, waiting, done = [], [], [0] * 4
    after_turn = []

    def mul():
        g, j, k = waiting.pop(0)
        plan.append(("mul", g, j, k))
        if j == STEPS[g] - 1:
            plan.append(("out", g))

    def steps(g, n):
        for _ in range(n):
            if len(waiting) == PT:
                mul()
            if after_turn and after_turn[0] and after_turn[0][0][0] == "inv":
                plan.extend(after_turn.pop(0))
            j = done[g]
            plan.append(("turn", g, j, STEP0[g] + j))
            waiting.append((g, j, STEP0[g] + j))
            done[g] += 1
            if after_turn:
                plan.extend(after_turn.pop(0))

    def row(nxt, r):
        plan.append(("row", nxt, r))
        late = [[("exp", nxt, r, c)] for c in range(2, r // 4 + 1)]
        if late:
            late[-1].append(("inv", nxt, r))
        else:
            late = [[("inv", nxt, r)]]
        after_turn[:0] = late

    def flush():
        while after_turn:
            plan.extend(after_turn.pop(0))

    for g in range(4):
        nxt = g == 3
        if g == 0:
            plan.append(("fetch", "v", 0))
            after_turn += [[("fetch", "v", c)] for c in range(1, NCH)]
        if g == 3 and last:
            after_turn += [[("fetch", "y", k)] for k in range(KD)]
        if g == 3 and not last:
            after_turn += [[("fetch", what, c)] for what, c in
                           (("k", 1), ("k", 2), ("k", 3), ("q", 1), ("r", 1), ("q", 2), ("r", 2), ("q", 3), ("r", 3))]
        steps(g, SPREAD[g][0])
        for i in range(4):
            r = i if nxt else 4 * (g + 1) + i
            if not (nxt and last):
                row(nxt, r)
                if r == 15 and not last:
                    after_turn += [[("fetch", "k", 0)], [("fetch", "q", 0), ("fetch", "r", 0)]]
            steps(g, SPREAD[g][i + 1])
            while any(x[0] in ("exp", "inv") for items in after_turn for x in items):
                plan.extend(after_turn.pop(0))
        if g != 0:
            flush()
    while waiting:
        mul()
    return plan


def width_of(t):
    if T_QR <= t < T_V or T_Q <= t < T_MERGE:
        return KQ * P
    if T_K <= t < T_Q:
        return KKV * P
    return 1024


def score_width(r, c):
    return CH if c < r // 4 else (r % 4 + 1) * P


def score_base(r):
    return sum(q // 4 + 1 for q in range(r))


def score_bank(r, c):
    return (score_base(r) + c) % 4


def score_use(r, c):
    return (score_base(r) + c) // 4


BANK_USES = N_STEPS // 4


def step_cols(g, j):
    return slice(max(0, j - 4 * g) * P, CH)


T_USES = [len(range(s, N_STEPS, PT)) for s in range(PT)]
H_LO_POOL = (1, 4, 7)
H_LO_VEC = tuple(k for k in range(KD) if k not in H_LO_POOL)
TAB_STEPS = 17
WA_LOADS = ((0, 1), (1, 2), (2, 4), (4, 6), (6, 8))
U_SSQ = N_LAT
U_CONV = U_SSQ + 2
U_GATES = U_CONV + N_CONV
N_UNITS = U_GATES + N_GATES
M0 = N_LAT + N_GATES
G_QR, G_V = 0, HEADS // 2
G_K = G_V + SB // 2
G_Q = G_K + HEADS
G_UNITS = G_Q + HEADS



def build(nc, x, xt, cst, pos, b_gate, g_post, wada, w1, wqr, wv, wk, wq, wm, out):
    with ExitStack() as ctx:
        sem = lambda name: ctx.enter_context(nc.semaphore(name))
        sems = lambda name, n: [sem(f"{name}{i}") for i in range(n)]
        dram = lambda name, shape: nc.dram_tensor(name, shape, F32)
        psum = ctx.enter_context(nc.psum_tensor("psum", [P, 8, CH], F32))

        base = (nc.sbuf_base + 63) // 64 * 64

        def at(name, kib, shape, dt=F32):
            return nc.alloc_sbuf_tensor_at(name, [P] + list(shape), dt, offset=base + int(kib * 1024))

        w_raw = at("w_raw", 0, [RAW, 1024])
        w_hi = at("w_hi", 16, [2, 1024], F32R)
        w_lo = at("w_lo", 24, [2, 1024], F32R)
        ones = at("ones", 32, [P])
        ident = at("ident", 32.5, [P])
        ident_b = at("ident_b", 33, [P], BF16)
        mask_b = at("mask_b", 33.25, [P], BF16)
        consts = at("consts", 33.5, [N_CST])
        eps_c = at("eps_c", 33.75, [1])
        a_col = at("a_col", 33.8125, [KD])
        b_col = at("b_col", 33.875, [2 * KD])
        c_hi = at("c_hi", 33.9375, [KD], F32R)
        c_lo = at("c_lo", 34.4375, [KD])
        row_max = at("row_max", 34, [2, NCH])
        row_sum = at("row_sum", 34.0625, [2, NCH])
        neg_max = at("neg_max", 34.125, [2, 1])
        all_sum = at("all_sum", 34.1875, [3, 1])
        inv_sum = at("inv_sum", 34.25, [2, 1])
        o_sq = at("o_sq", 34.3125, [4, 2])
        o_st = at("o_st", 34.34375, [4, 4])
        R = 34.5
        h_hi = at("h_hi", R, [KD, SEQ], F32R)
        h_lo = at("h_lo", R + 64, [KD, SEQ], F32R)
        wa = at("wa", R, [KD, 2 * D])
        x_raw = at("x_raw", R + 64, [KD, SEQ])
        vs = at("vs", R + 128, [SEQ])
        cv = at("cv", R + 136, [SEQ])
        stage = at("stage", R + 144, [2, SEQ])
        u = at("u", R + 160, [SEQ + 2])
        t1 = at("t1", R + 168.0625, [CH])
        t2 = at("t2", R + 170.0625, [CH])
        squares = at("squares", R + 128, [2, 1024])
        diag = at("diag", R + 128, [SB, P])
        sq_sum = at("sq_sum", R + 136, [SEQ])
        r_x = at("r_x", R + 136, [SEQ])
        c_b = at("c_b", R + 160, [KD, P])
        masked = at("masked", R + 164, [2, CH])
        ang = at("ang", R + 144, [CH])
        pos_i = at("pos_i", R + 146, [CH], I32)
        turns = at("turns", R + 148, [CH])
        s_half = at("s_half", R + 150, [CH])
        tab = at("tab", R + 152, [3, CH])
        qn_hi = at("qn_hi", R, [KQ, SEQ], F32R)
        qn_lo = at("qn_lo", R + 24, [KQ, SEQ], F32R)
        kn_hi = at("kn_hi", R + 48, [KKV, SEQ], F32R)
        kn_lo = at("kn_lo", R + 64, [KKV, SEQ], F32R)
        lat = at("lat", R + 80, [KQ + KKV, SEQ])
        c_b_hi = at("c_b_hi", R + 128, [KD, P], F32R)
        c_b_lo = at("c_b_lo", R + 132, [KD, P], F32R)
        bg = at("bg", R + 136, [D])
        gp = at("gp", R + 140, [D])
        gg = at("gg", R + 120, [D])
        r_lat = at("r_lat", R + 160, [SEQ])
        rope_a = at("rope_a", R + 80, [SEQ])
        rope_b = at("rope_b", R + 88, [SEQ])
        cos_t = at("cos_t", R + 124, [SEQ])
        sin_t = at("sin_t", R + 132, [SEQ])
        q_hi = at("q_hi", R, [SEQ], F32R)
        q_lo = at("q_lo", R + 8, [SEQ], F32R)
        v_hi = at("v_hi", R + 16, [SEQ], F32R)
        v_lo = at("v_lo", R + 24, [SEQ], F32R)
        sz = at("sz", R + 44, [2, CH])
        k_hi = at("k_hi", R + 48, [SEQ], F32R)
        k_lo = at("k_lo", R + 56, [SEQ], F32R)
        qr_s = at("qr_s", R + 64, [SEQ], F32R)
        kr_hi = at("kr_hi", R + 96, [SEQ], F32R)
        kr_lo = at("kr_lo", R + 104, [SEQ], F32R)
        a_raw = [at(f"a_raw{i}", R + (80, 88, 112)[i], [SEQ]) for i in range(3)]
        pt_hi = at("pt_hi", R + 160, [PT, CH], F32R)
        pt_lo = at("pt_lo", R + 166, [PT, CH], F32R)
        p_even = [at(f"p_even{i}", R + (32, 38, 124, 130)[i], [3 * CH]) for i in range(4)]
        p_odd = [at(f"p_odd{i}", R + (72, 136, 144, 152)[i], [4 * CH]) for i in range(4)]
        e_raw = at("e_raw", R, [KD, CH])
        m_hi = at("m_hi", R + 16, [KD, CH], F32R)
        o_lo = at("o_lo", R + 32, [KD, CH], F32R)
        o_hi = at("o_hi", R + 48, [KD, CH], F32R)
        m_lo = at("m_lo", R + 64, [KD, CH], F32R)
        y_hi = at("y_hi", R + 80, [KD, CH], F32R)
        y_lo = at("y_lo", R + 96, [KD, CH], F32R)
        gr = at("gr", R + 112, [4, CH])
        m_a = at("m_a", R + 124, [KD, CH])
        x_t = at("x_t", R + 140, [2, D])
        o_t = at("o_t", R + 148, [2, D])
        e_t = at("e_t", R + 156, [2, CH])
        sq_t = at("sq_t", R + 160, [2, CH])

        lat_d = dram("lat_d", (N_LAT, P, SEQ))
        r_d = dram("r_d", (2, P, SEQ))
        tab_d = dram("tab_d", (3, P, CH))
        y_d = dram("y_d", (KD, P, SEQ))
        gate_d = dram("gate_d", (N_GATES, P, SEQ))
        qr_d = dram("qr_d", (HEADS // 2, P, SEQ))
        v_d = dram("v_d", (SB, P, HEADS * VD))
        k_d = dram("k_d", (HEADS, P, SEQ))
        q_d = dram("q_d", (HEADS, P, SEQ))
        roped_d = dram("roped_d", (1 + HEADS // 2, P, SEQ))
        o_d = dram("o_d", (HEADS, P, SEQ))

        cst_in = sem("cst_in")
        pos_in = sem("pos_in")
        settled = sem("settled")
        x_in = sems("x_in", KD)
        wa_in = sems("wa_in", len(WA_LOADS))
        ready = sem("ready")
        sq_ready = sem("sq_ready")
        sq_added = sem("sq_added")
        ssq_ready = sem("ssq_ready")
        diag_step = sem("diag_step")
        diag_ready = sem("diag_ready")
        r_bc = sem("r_bc")
        r_x_ready = sem("r_x_ready")
        ada_ready = sem("ada_ready")
        ab_step = sem("ab_step")
        rs = sem("rs")
        rs_root = sem("rs_root")
        xr_ready = sem("xr_ready")
        xr_g = sem("xr_g")
        h32_ready = sem("h32_ready")
        hhi_ready = sem("hhi_ready")
        hlo_v = sem("hlo_v")
        hlo_g = sem("hlo_g")
        tab_step = sem("tab_step")
        tab_sin = sem("tab_sin")
        tab_ready = sem("tab_ready")
        tab_out = sem("tab_out")
        w_in = sems("w_in", RAW)
        whi = sem("whi")
        wlo = sem("wlo")
        p_full = sem("p_full")
        p_free = sems("p_free", 8)
        lat_sq = sem("lat_sq")
        lat_add = sem("lat_add")
        r_ready = sem("r_ready")
        r_out = sems("r_out", 2)
        u_zero = sem("u_zero")
        cv_step = sem("cv_step")
        sg_ready = sem("sg_ready")
        y_ready = sem("y_ready")
        y_out = sem("y_out")
        st_out = sem("st_out")
        cb_step = sem("cb_step")
        bg_in = sem("bg_in")
        g_gate = sem("g_gate")
        gg_step = sem("gg_step")
        g_full = sem("g_full")
        g_free = sems("g_free", 8)
        lat_in = sems("lat_in", 2)
        r_in = sem("r_in")
        nrm = sem("nrm")
        nrm_hi = sem("nrm_hi")
        nrm_lo = sem("nrm_lo")
        nrm_lo_g = sem("nrm_lo_g")
        ct_in = sem("ct_in")
        ra_in = sem("ra_in")
        rp_step = sem("rp_step")
        rp_out = sem("rp_out")
        a_in = sems("a_in", 3)
        kr_hi_r = sem("kr_hi_r")
        kr_lo_r = sem("kr_lo_r")
        fk_hi = sem("fk_hi")
        fk_lo = sem("fk_lo")
        fq_hi = sem("fq_hi")
        fq_lo = sem("fq_lo")
        fr_hi = sem("fr_hi")
        fr_lo = sem("fr_lo")
        fv_hi = sem("fv_hi")
        fv_lo = sem("fv_lo")
        s_full = sem("s_full")
        s_free = sems("s_free", NCH)
        mx_step = sem("mx_step")
        nm_ready = sem("nm_ready")
        iv_step = sem("iv_step")
        iv_ready = sem("iv_ready")
        p_ready = sem("p_ready")
        t_full = sem("t_full")
        t_free = sems("t_free", PT)
        pt_hi_r = sem("pt_hi_r")
        pv_done = sem("pv_done")
        sz_in = sems("sz_in", 2)
        o_ready = sem("o_ready")
        o_out = sems("o_out", 2)
        e_hi = sem("e_hi")
        e_lo = sem("e_lo")
        e_full = sem("e_full")
        e_outmm = sem("e_outmm")
        o_full = sem("o_full")
        e_free = sems("e_free", 8)
        gr_in = sems("gr_in", 4)
        m_r = sem("m_r")
        m_hi_r = sem("m_hi_r")
        m_lo_r = sem("m_lo_r")
        x_t_in = sems("x_t_in", 2)
        osq = sem("osq")
        o_root = sem("o_root")
        o_step = sem("o_step")
        o_done = sem("o_done")
        out_done = sems("out_done", 2)

        def prob(r):
            return (p_even, p_odd)[r // 4 % 2][r % 4]

        blk = ctx.enter_context(nc.Block())

        def parts(whi_, wlo_, xhi_, xlo_):
            return [(whi_, xlo_), (wlo_, xhi_), (whi_, xhi_)]

        def accumulate(pe, bank, pairs, start=True, stop=True, skip=False):
            for i, (a, b) in enumerate(pairs):
                last = pe.matmul(bank, a, b, start=start and i == 0, stop=stop and i == len(pairs) - 1,
                                 skip_group_check=skip)
            return last


        @blk.sync
        def _(sp):
            def settle():
                sp.sem_inc(settled, 1)

            def load_w(t, src, width, before):
                if before is not None:
                    sp.wait_ge(wlo, before)
                sp.dma_start(w_raw[:, t % RAW, 0:width], src).then_inc(w_in[t % RAW], 16)

            def load_tile(t):
                if t < T_QR:
                    src = w1[t]
                elif t < T_V:
                    src = wqr[t - T_QR]
                elif t < T_K:
                    src = wv[t - T_V]
                elif t < T_Q:
                    src = wk[t - T_K]
                elif t < T_MERGE:
                    src = wq[t - T_Q]
                else:
                    src = wm[t - T_MERGE]
                load_w(t, src, width_of(t), t - RAW + 1 if t >= RAW else None)

            sp.dma_start(consts[:], cst).then_inc(cst_in, 16)
            for c in range(NCH):
                sp.dma_start(pos_i[c * HALF:(c + 1) * HALF, :],
                             pos[:, chunk(c)].to_broadcast([HALF, CH])).then_inc(pos_in, 16)
            def load_wa(n):
                ks = slice(*WA_LOADS[n])
                sp.dma_start(wa[:, ks, :], wada[ks].rearrange("k p n -> p k n")).then_inc(wa_in[n], 16)

            for k in range(KD):
                sp.dma_start(x_raw[:, k, :], xt[k]).then_inc(x_in[k], 16)
                if k in (3, 5):
                    load_wa(k // 2 - 1)
            for t in range(2):
                load_tile(t)
            for n in range(2, len(WA_LOADS)):
                load_wa(n)
            for t in range(2, RAW):
                load_tile(t)
            sp.wait_ge(tab_ready, 2)
            sp.dma_start(tab_d.ap().rearrange("a p n -> p a n"), tab[:]).then_inc(tab_out, 16)

            def store(dst, m, free, at_least, dst_view=None):
                if not (isinstance(m, int) and m == 0):
                    sp.wait_ge(st_out, 16 * m)
                    settle()
                for s in range(NCH):
                    sp.wait_ge(free[s], at_least)
                slot = m % 2 if isinstance(m, int) else dst_view
                sp.dma_start(dst, stage[:, slot, :]).then_inc(st_out, 16)

            def banks(sem_list, n):
                return sem_list[4 * (n % 2):4 * (n % 2) + 4]

            for t in range(N_LAT):
                load_tile(t + RAW)
                store(lat_d[t], t, banks(p_free, t), t // 2 + 2)
            sp.wait_ge(r_ready, NCH)
            sp.dma_start(r_d[0], vs[:]).then_inc(r_out[0], 16)
            sp.wait_ge(r_ready, 2 * NCH)
            sp.dma_start(r_d[1], cv[:]).then_inc(r_out[1], 16)
            with sp.Fori(0, KD) as i:
                for j in range(4):
                    t = N_LAT + j + RAW
                    load_w(t, w1[4 * i + t], 1024, 4 * i + (t - RAW + 1))
                sp.wait_ge(y_ready, 4 * i + 8)
                sp.dma_start(y_d[i], cv[:]).then_inc(y_out, 16)
            with sp.Fori(0, N_GATES // 4) as i:
                for j in range(4):
                    t = N_LAT + N_CONV + j + RAW
                    load_w(t, w1[4 * i + t], 1024, 4 * i + (t - RAW + 1))
                    store(gate_d[4 * i + j], 4 * i + (N_LAT + j), banks(p_free, j),
                          2 * i + (U_GATES // 2 + j // 2 + 2), dst_view=j % 2)
            sp.wait_ge(y_out, 16 * KD + 16)
            sp.dma_start(bg[:], b_gate.to_broadcast([P, D])).then_inc(bg_in, 16)
            sp.dma_start(gp[:], g_post.to_broadcast([P, D])).then_inc(bg_in, 16)
            for t in range(T_ADA + RAW, T_ADA + RAW + 2):
                load_tile(t)
            sp.wait_ge(p_full, 4 * N_UNITS)
            for n in range(2):
                sp.wait_ge(r_out[n], 16)
            sp.wait_ge(st_out, 16 * M0)
            sp.dma_start(r_lat[:], r_d[0]).then_inc(r_in, 16)
            for n, ks in enumerate((slice(0, KQ), slice(KQ, KQ + KKV))):
                sp.dma_start(lat[:, ks, :], lat_d[ks].rearrange("k p n -> p k n")).then_inc(lat_in[n], 16)
            for t in range(T_ADA + RAW + 2, T_ADA + RAW + KD):
                load_tile(t)
            sp.wait_ge(nrm, KQ * NCH)
            sp.dma_start(r_lat[:], r_d[1]).then_inc(r_in, 16)
            sp.wait_ge(tab_out, 16)
            sp.wait_ge(g_gate, KD)
            sp.wait_ge(gg_step, 2)
            for j in range(4):
                rows = slice(HALF * j, HALF * (j + 1))

                def turned(a):
                    return tab_d[a].rearrange("(c f) t -> f c t", c=NCH)

                sp.dma_start(cos_t[rows, :].rearrange("p (c t) -> p c t", c=NCH), turned(0)).then_inc(ct_in, 16)
                sp.dma_start(sin_t[rows, :].rearrange("p (c t) -> p c t", c=NCH),
                             turned(2 if j % 2 == 0 else 1)).then_inc(ct_in, 16)

            def rope_load(n):
                src = lat_d[N_LAT - 1] if n == 0 else qr_d[n - 1]
                if n == 0:
                    sp.wait_ge(nrm_hi, (KQ + KKV) * NCH)
                    sp.wait_ge(nrm_lo, (KQ + KKV - 2) * NCH)
                    sp.wait_ge(nrm_lo_g, 2 * NCH)
                else:
                    sp.wait_ge(st_out, 16 * (M0 + n))
                    sp.wait_ge(rp_out, 16 * n)
                sp.dma_start(rope_a[:], src).then_inc(ra_in, 16)
                for j in range(4):
                    o = j ^ 1
                    sp.dma_start(rope_b[HALF * j:HALF * (j + 1), :],
                                 src[HALF * o:HALF * (o + 1), :]).then_inc(ra_in, 16)

            def rope_store(n):
                sp.wait_ge(rp_step, 3 * (n + 1))
                sp.dma_start(roped_d[n], rope_a[:]).then_inc(rp_out, 16)

            for g in range(G_UNITS):
                if g < G_V:
                    load_tile(T_QR + g + RAW)
                elif g == G_V:
                    load_tile(T_V + RAW)
                    load_tile(T_V + 1 + RAW)
                elif g >= G_K:
                    load_tile(T_K + g - G_K + RAW)
                if g < G_V:
                    dst = qr_d[g]
                elif g < G_K:
                    b = 2 * (g - G_V)
                    dst = v_d[b:b + 2].rearrange("b p n -> p b n")
                elif g < G_Q:
                    dst = k_d[g - G_K]
                else:
                    dst = q_d[g - G_Q]
                sp.wait_ge(st_out, 16 * (M0 + g))
                for s in range(NCH):
                    sp.wait_ge(banks(g_free, g)[s], g // 2 + 2)
                src = stage[:, (M0 + g) % 2, :]
                if G_V <= g < G_K:
                    src = src.rearrange("p (b n) -> p b n", b=2)
                sp.dma_start(dst, src).then_inc(st_out, 16)
                n, part = (g - G_V - 1) // 3, (g - G_V - 1) % 3
                if 0 <= n < 5 and part == 0:
                    rope_load(n)
                if 0 <= n < 5 and part == 2:
                    rope_store(n)

            sp.wait_ge(st_out, 16 * (M0 + G_UNITS))
            sp.wait_ge(rp_out, 16 * 5)
            sp.wait_ge(g_full, 4 * G_UNITS)

            def load_k(h):
                sp.dma_start(a_raw[0][:, :], k_d[h]).then_inc(a_in[0], 16)

            def load_q(h):
                sp.dma_start(a_raw[1][:, :], q_d[h]).then_inc(a_in[1], 16)

            def load_qr(pair, half):
                for d in range(2):
                    sp.dma_start(a_raw[2][ROPE * d:ROPE * (d + 1), :],
                                 roped_d[pair + 1, ROPE * half:ROPE * (half + 1), :]).then_inc(a_in[2], 16)

            def load_v(h):
                sp.dma_start(a_raw[0][:, :].rearrange("p (b n) -> p b n", b=SB),
                             v_d[:, :, bass.ds(h * VD, VD)].rearrange("b p n -> p b n")).then_inc(a_in[0], 16)

            def load_sz(h, g):
                sp.dma_start(sz[:, g % 2, :], gate_d[h, :, chunk(g)]).then_inc(sz_in[g % 2], 16)

            sp.dma_start(a_raw[0][:, :], roped_d[0]).then_inc(a_in[0], 16)
            load_q(0)
            load_qr(0, 0)
            load_sz(0, 0)
            load_sz(0, 1)
            sp.wait_ge(kr_lo_r, NCH)
            load_k(0)
            sp.wait_ge(fk_lo, NCH)
            load_v(0)

            def load_e(src, k, cols):
                sp.dma_start(e_raw[:, k, :], src[k, :, cols]).then_inc(x_in[k], 16)

            def head(h, last, pair=None, half=None):
                if not last:
                    sp.wait_ge(fq_lo, NCH * h + NCH)
                    settle()
                    load_q(h + 1)
                    sp.wait_ge(fr_lo, NCH * h + NCH)
                    settle()
                    load_qr(pair, half)
                    sp.wait_ge(fv_lo, NCH * h + NCH)
                    load_k(h + 1)
                for g in range(4):
                    if g == 3 and not last:
                        sp.wait_ge(fk_lo, NCH * h + 2 * NCH)
                        settle()
                        load_v(h + 1)
                    if g == 2 and last:
                        sp.wait_ge(s_full, N_STEPS * HEADS)
                        for k in range(KD):
                            load_e(y_d, k, chunk(0))
                        sp.wait_ge(fr_lo, NCH * HEADS)
                        for n in range(4):
                            sp.dma_start(gr[:, n, :], gate_d[KD + n, :, chunk(0)]).then_inc(gr_in[n], 16)
                    sp.wait_ge(o_ready, 4 * h + (g + 2))
                    sp.dma_start(o_d[h, :, chunk(g)], sz[:, g % 2, :]).then_inc(o_out[g % 2], 16)
                    if g < 2 or not last:
                        sp.wait_ge(o_out[g % 2], 32 * h + 16 * (g // 2 + 1))
                        if g < 2:
                            load_sz(h, g + 2)
                        else:
                            load_sz(h + 1, g - 2)

            with sp.Fori(0, HEADS // 2 - 1) as j:
                head(2 * j, False, j, 1)
                head(2 * j + 1, False, j + 1, 0)
            head(HEADS - 2, False, HEADS // 2 - 1, 1)
            head(HEADS - 1, True)
            for s in range(2):
                sp.wait_ge(o_out[s], 32 * HEADS)
            for k in range(KD):
                sp.wait_ge(e_lo, k + 1)
                load_e(o_d, k, chunk(0))
            sp.wait_ge(t_full, N_STEPS * (HEADS + 1))

            for t in range(T_MERGE + RAW, T_MERGE + RAW + 2):
                load_tile(t)

            def merge(c, last):
                cols = bass.ds(c * CH, CH)
                cols_next = bass.ds(c * CH + CH, CH)

                def load_m(j):
                    if last and j + RAW >= PER_CHUNK:
                        return
                    t = T_MERGE + RAW + j
                    load_w(t, wm[(j + RAW) % PER_CHUNK], 1024, PER_CHUNK * c + (t - RAW + 1))

                def load_gr(n):
                    m, u = (n - 4) % KD, (n - 4) // KD
                    sp.wait_ge(e_free[m], 3 * c + (u + 2))
                    sp.dma_start(gr[:, n % 4, :], gate_d[KD + n % (2 * KD), :, cols if n < 2 * KD else cols_next])\
                      .then_inc(gr_in[n % 4], 16)

                for n in range(KD):
                    if n >= 2:
                        load_m(n)
                    load_gr(n + 4)
                    if not last:
                        sp.wait_ge(e_lo, 16 * c + (KD + n + 1))
                        settle()
                        load_e(y_d, n, cols_next)
                for n in range(KD):
                    load_m(KD + n)
                    if n < 4:
                        load_gr(n + 12)
                    if n < 2:
                        sp.wait_ge(o_done, 4 * c + (n + 3))
                        sp.dma_start(x_t[:, n, :], x[4 * c + n]).then_inc(x_t_in[n], 16)
                for n in range(KD):
                    load_m(2 * KD + n)
                    if not last:
                        if n < 4:
                            load_gr(n + 2 * KD)
                        sp.wait_ge(e_lo, 16 * c + (2 * KD + n + 1))
                        settle()
                        load_e(o_d, n, cols_next)
                for b in range(4):
                    if b % 2 == 0 and not last:
                        load_m(PER_CHUNK + b // 2)
                    sp.wait_ge(o_done, 4 * c + (b + 5))
                    sp.dma_start(out[4 * c + b], o_t[:, b % 2, :]).then_inc(out_done[b % 2], 16)
                    if b < 2:
                        sp.dma_start(x_t[:, b, :], x[4 * c + (b + 2)]).then_inc(x_t_in[b], 16)

            with sp.Fori(0, NCH - 1) as c:
                merge(c, False)
            merge(NCH - 1, True)
            for s in range(2):
                sp.wait_ge(out_done[s], 16 * (2 * NCH + 1))

        @blk.gpsimd
        def _(pool):
            for b in range(8):
                pool.sem_inc(p_free[b], 1)
                pool.sem_inc(e_free[b], 1)
            for b in range(6):
                pool.sem_inc(g_free[b], 1)
            for c in range(NCH):
                pool.sem_inc(s_free[c], 1)
            for s in range(PT):
                pool.sem_inc(t_free[s], 1)
            pool.sem_inc(y_ready, 4)
            pool.sem_inc(y_out, 16)
            pool.sem_inc(t_full, N_STEPS)
            pool.sem_inc(pv_done, 1)
            pool.sem_inc(p_ready, 2)
            pool.sem_inc(o_ready, 1)
            pool.sem_inc(o_done, 4)
            for s in range(2):
                pool.sem_inc(out_done[s], 16)
            pool.memset(ones[:], 1.0).then_inc(ready, 1)
            pool.memset(eps_c[:], EPS).then_inc(ready, 1)
            pool.memset(ident[:], 0.0).then_inc(ready, 1)
            pool.memset(ident_b[:], 0.0).then_inc(ready, 1)
            pool.memset(mask_b[:], 0.0).then_inc(ready, 1)
            pool.wait_ge(ready, 5)
            for m in (ident, ident_b):
                pool.affine_select(out=m[:], in_=m[:], compare_op=ALU.not_equal, fill=1.0, base=0,
                                   pattern=[[-1, P]], channel_multiplier=1).then_inc(ready, 1)
            pool.affine_select(out=mask_b[:], in_=mask_b[:], compare_op=ALU.is_ge, fill=MASKED, base=0,
                               pattern=[[-1, P]], channel_multiplier=1).then_inc(ready, 1)

            pool.wait_ge(ready, 8)
            pool.wait_ge(cst_in, 16)
            for k in range(KD):
                ins = pool.tensor_scalar(c_b[:, k, :], ones[:], consts[:, C_C + k:C_C + k + 1], 1.0, ALU.mult,
                                         ALU.mult)
            ins.then_inc(cb_step, 1)

            def w_low(t, width, n):
                pool.wait_ge(whi, n)
                pool.tensor_tensor(w_lo[:, t % 2, 0:width], w_raw[:, t % RAW, 0:width],
                                   w_hi[:, t % 2, 0:width].bitcast(F32), ALU.subtract).then_inc(wlo, 1)

            for t in range(2):
                w_low(t, 1024, t + 1)
            for s in range(NCH):
                pool.wait_ge(r_x_ready, s + 1)
                for k in H_LO_POOL:
                    pool.tensor_tensor(x_raw[:, k, chunk(s)], x_raw[:, k, chunk(s)], r_x[:, chunk(s)],
                                       ALU.mult).then_inc(xr_g, 1)
            for s in range(NCH):
                for k in H_LO_POOL:
                    pool.wait_ge(hhi_ready, KD * s + k + 1)
                    pool.tensor_tensor(h_lo[:, k, chunk(s)], x_raw[:, k, chunk(s)],
                                       h_hi[:, k, chunk(s)].bitcast(F32), ALU.subtract).then_inc(hlo_g, 1)
            for t in range(2, RAW):
                w_low(t, 1024, t + 1)
            with pool.Fori(0, (N_PROJ + 2 - RAW) // 4) as i:
                for j in range(4):
                    w_low(RAW + j, 1024, 4 * i + (RAW + j + 1))
            for t in range(N_PROJ + 2, T_QR + 2):
                w_low(t, width_of(t), t + 1)

            def lat_low(k, c, n, dst, j):
                pool.wait_ge(nrm_hi, n)
                pool.tensor_tensor(dst[0][:, j, chunk(c)], lat[:, k, chunk(c)],
                                   dst[1][:, j, chunk(c)].bitcast(F32), ALU.subtract).then_inc(nrm_lo_g, 1)

            for c in range(NCH):
                lat_low(KQ - 1, c, KQ * (c + 1), (qn_lo, qn_hi), KQ - 1)
            w_low(T_QR + 2, width_of(T_QR + 2), T_QR + 3)
            for c in range(NCH):
                lat_low(KQ + KKV - 1, c, KQ * NCH + KKV * (c + 1), (kn_lo, kn_hi), KKV - 1)
            for t in range(T_QR + 3, T_MERGE + 2):
                w_low(t, width_of(t), t + 1)

            for c in range(NCH):
                pool.wait_ge(kr_hi_r, c + 1)
                pool.tensor_tensor(kr_lo[:, chunk(c)], a_raw[0][:, chunk(c)],
                                   kr_hi[:, chunk(c)].bitcast(F32), ALU.subtract).then_inc(kr_lo_r, 1)

            def fetch(h, what, c):
                hi, lo, slot, hi_r, lo_r = {"k": (k_hi, k_lo, 0, fk_hi, fk_lo), "q": (q_hi, q_lo, 1, fq_hi, fq_lo),
                                            "v": (v_hi, v_lo, 0, fv_hi, fv_lo)}[what]
                pool.wait_ge(hi_r, NCH * h + (c + 1))
                pool.tensor_tensor(lo[:, chunk(c)], a_raw[slot][:, chunk(c)],
                                   hi[:, chunk(c)].bitcast(F32), ALU.subtract).then_inc(lo_r, 1)

            def normalise(h, r):
                pool.wait_ge(iv_ready, SB * h + (r + 1))
                pool.sem_inc(settled, 1)
                row = prob(r)[:, 0:P * (r + 1)]
                pool.tensor_scalar(row, row, inv_sum[:, r % 2, :], 1.0, ALU.mult, ALU.mult).then_inc(p_ready, 1)

            def block_low(first, k, hi, lo):
                pool.wait_ge(e_hi, first + k + 1)
                pool.tensor_tensor(lo[:, k, :], e_raw[:, k, :], hi[:, k, :].bitcast(F32),
                                   ALU.subtract).then_inc(e_lo, 1)

            def head(h, last):
                for item in head_plan(last):
                    if item[0] == "inv":
                        normalise(h + 1 if item[1] else h, item[2])
                    elif item[0] == "fetch" and item[1] == "y":
                        block_low(0, item[2], y_hi, y_lo)
                    elif item[0] == "fetch" and item[1] != "r":
                        fetch(h if item[1] == "v" else h + 1, item[1], item[2])

            for c in range(NCH):
                fetch(0, "k", c)
                fetch(0, "q", c)
            for r in range(4):
                normalise(0, r)
            with pool.Fori(0, HEADS - 1) as h:
                head(h, False)
            head(HEADS - 1, True)

            def merge(c, last):
                def low(j):
                    t = T_MERGE + 2 + j
                    if not (last and j + 2 >= PER_CHUNK):
                        w_low(t, 1024, PER_CHUNK * c + (t + 1))

                for k in range(KD):
                    low(k)
                    block_low(16 * c + KD, k, o_hi, o_lo)
                for j in range(KD, 2 * KD):
                    low(j)
                for k in range(KD):
                    if not last:
                        block_low(16 * c + 2 * KD, k, y_hi, y_lo)
                    low(2 * KD + k)

            for s in range(2):
                pool.wait_ge(o_out[s], 32 * HEADS)
            with pool.Fori(0, NCH - 1) as c:
                merge(c, False)
            merge(NCH - 1, True)

        @blk.scalar
        def _(act):
            def w_high(t, width, n=None):
                act.wait_ge(w_in[t % RAW], 16 * (t // RAW + 1) if n is None else n)
                act.activation(w_hi[:, t % 2, 0:width], w_raw[:, t % RAW, 0:width], ACT.Copy).then_inc(whi, 1)

            for k in range(KD):
                act.wait_ge(x_in[k], 16)
                for f in range(2):
                    n = 2 * k + f
                    half = slice(1024 * f, 1024 * (f + 1))
                    if n >= 4:
                        act.wait_ge(sq_added, n - 3)
                    act.activation(sq_sum[:, half] if k == 0 else squares[:, f, :], x_raw[:, k, half],
                                   ACT.Square).then_inc(sq_ready, 1)
            w_high(0, 1024)
            w_high(1, 1024)

            def root(wait_sem, value):
                act.wait_ge(wait_sem, value)
                act.activation(t2[:], t1[:], ACT.Sqrt).then_inc(rs_root, 1)

            act.wait_ge(rs, 1)
            act.activation(t2[:, 0:SB], t1[:, 0:SB], ACT.Sqrt).then_inc(rs_root, 1)
            for s in range(NCH):
                act.wait_ge(r_bc, s + 1)
                act.activation(r_x[:, chunk(s)], psum[:, s, :], ACT.Copy).then_inc(r_x_ready, 1)
            act.wait_ge(tab_step, TAB_STEPS)
            act.activation(s_half[:], ang[:], ACT.Sin, scale=0.5).then_inc(tab_sin, 1)
            act.activation(tab[:, 1, :], ang[:], ACT.Sin).then_inc(tab_sin, 1)
            act.wait_ge(ada_ready, 4)
            for s in range(NCH):
                for k in range(KD):
                    act.wait_ge(h32_ready, KD * s + k + 1)
                    act.activation(h_hi[:, k, chunk(s)], x_raw[:, k, chunk(s)], ACT.Copy).then_inc(hhi_ready, 1)

            act.wait_ge(tab_out, 16)
            for t in range(N_LAT):
                for s in range(NCH):
                    b = 4 * (t % 2) + s
                    act.wait_ge(p_full, 4 * t + s + 1)
                    if t >= 2:
                        act.wait_ge(st_out, 16 * (t - 1))
                        act.wait_ge(lat_sq, 4 * (t - 2) + s + 1)
                    act.activation(stage[:, t % 2, chunk(s)], psum[:, b, :], ACT.Copy).then_inc(p_free[b], 1)
                w_high(t + 2, 1024)
            for n in range(2):
                for s in range(NCH):
                    root(p_free[4 * n + s], U_SSQ // 2 + 2)
            act.wait_ge(r_out[0], 16)
            with act.Fori(0, KD) as i:
                for j in range(4):
                    unit = U_CONV + j
                    if j == 0:
                        for s in range(NCH):
                            act.wait_ge(p_full, 16 * i + (4 * unit + s + 1))
                            act.wait_ge(y_ready, 4 * i + (s + 1))
                            act.activation(vs[:, chunk(s)], psum[:, s, :], ACT.Copy).then_inc(p_free[s], 1)
                    if j == 3:
                        for s in range(NCH):
                            act.wait_ge(p_full, 16 * i + (4 * unit + s + 1))
                            act.wait_ge(p_free[4 + s], 2 * i + (unit // 2 + 1))
                            act.activation(vs[:, chunk(s)], psum[:, 4 + s, :], ACT.Sigmoid).then_inc(sg_ready, 1)
                    t = N_LAT + j + 2
                    act.wait_ge(p_full, 16 * i + 4 * (unit + 1))
                    w_high(t, 1024, 16 * i + 16 * (t // RAW + 1))
            def gates(i, m0, silu):
                for j in range(4):
                    unit = U_GATES + m0 + j
                    for s in range(NCH):
                        b = 4 * (j % 2) + s
                        act.wait_ge(p_full, 16 * i + (4 * unit + s + 1))
                        act.wait_ge(st_out, 64 * i + 16 * (N_LAT + m0 + j - 1))
                        act.activation(stage[:, j % 2, chunk(s)], psum[:, b, :], ACT.Sigmoid)\
                           .then_inc(sg_ready if silu else p_free[b], 1)
                    t = N_LAT + N_CONV + m0 + j + 2
                    act.wait_ge(p_full, 16 * i + 4 * (unit + 1))
                    w_high(t, 1024, 16 * i + 16 * (t // RAW + 1))

            with act.Fori(0, KD // 4) as i:
                gates(i, 0, True)
            with act.Fori(0, KD // 2) as i:
                gates(i, KD, False)

            for t in range(N_PROJ + 2, T_QR + 2):
                act.wait_ge(g_gate, t - T_ADA - 1)
                w_high(t, width_of(t))

            def lat_high(c, ks, dst, base):
                for j, k in enumerate(ks):
                    act.wait_ge(nrm, base + len(ks) * c + j + 1)
                    act.activation(dst[:, j, chunk(c)], lat[:, k, chunk(c)], ACT.Copy).then_inc(nrm_hi, 1)

            for c in range(NCH):
                lat_high(c, range(KQ), qn_hi, 0)
            for g in range(G_UNITS):
                for s in range(NCH):
                    b = 4 * (g % 2) + s
                    act.wait_ge(g_full, 4 * g + s + 1)
                    act.wait_ge(st_out, 16 * (M0 + g - 1))
                    act.activation(stage[:, (M0 + g) % 2, chunk(s)], psum[:, b, :], ACT.Copy).then_inc(g_free[b], 1)
                if g < G_V:
                    w_high(T_QR + g + 2, width_of(T_QR + g + 2))
                elif g == G_K - 1:
                    act.wait_ge(g_full, 4 * G_K)
                    w_high(T_K, width_of(T_K))
                    w_high(T_K + 1, width_of(T_K + 1))
                elif g >= G_K:
                    t = T_K + g - G_K + 2
                    w_high(t, width_of(t))
                if g == 0:
                    for c in range(NCH):
                        lat_high(c, range(KQ, KQ + KKV), kn_hi, KQ * NCH)

            act.wait_ge(a_in[0], 16)
            for c in range(NCH):
                act.activation(kr_hi[:, chunk(c)], a_raw[0][:, chunk(c)], ACT.Copy).then_inc(kr_hi_r, 1)

            def fetch(h, what, c):
                dst, slot, loaded, hi_r = {"k": (k_hi, 0, 32 * h + 32, fk_hi), "q": (q_hi, 1, 16 * h + 16, fq_hi),
                                           "r": (qr_s, 2, 32 * h + 32, fr_hi), "v": (v_hi, 0, 32 * h + 48, fv_hi)}[what]
                act.wait_ge(a_in[slot], loaded)
                act.activation(dst[:, chunk(c)], a_raw[slot][:, chunk(c)], ACT.Copy).then_inc(hi_r, 1)

            def exponentials(h, r, chunks):
                g = r // 4
                if 0 in chunks:
                    act.wait_ge(nm_ready, SB * h + (r + 1))
                    act.wait_ge(t_full,
                                N_STEPS * h + (STEP0[3], N_STEPS, N_STEPS + STEP0[1], N_STEPS + STEP0[2])[g])
                for c in chunks:
                    w = score_width(r, c)
                    bank = score_bank(r, c)
                    act.activation(prob(r)[:, c * CH:c * CH + w], psum[:, bank, 0:w], ACT.Exp,
                                   bias=neg_max[:, r % 2, :], scale=SCALE,
                                   accum_out=row_sum[:, r % 2, c:c + 1]).then_inc(s_free[bank], 1)

            def turned(h, g, j, k):
                act.wait_ge(t_full, N_STEPS * h + (N_STEPS + k + 1))
                act.wait_ge(pv_done, N_STEPS * h + (k - PT + 2 if k >= PT else 1))
                cols = step_cols(g, j)
                act.activation(pt_hi[:, k % PT, cols], psum[:, 4 + k % PT, cols], ACT.Copy).then_inc(pt_hi_r, 1)

            def block_high(first, k, hi, loaded):
                act.wait_ge(x_in[k], loaded)
                act.activation(hi[:, k, :], e_raw[:, k, :], ACT.Copy).then_inc(e_hi, 1)

            def head(h, last):
                for item in head_plan(last):
                    if item[0] == "row":
                        exponentials(h + 1 if item[1] else h, item[2], range(min(2, item[2] // 4 + 1)))
                    elif item[0] == "exp":
                        exponentials(h + 1 if item[1] else h, item[2], [item[3]])
                    elif item[0] == "fetch":
                        if item[1:] == ("k", 0):
                            act.wait_ge(s_full, N_STEPS * h + N_STEPS)
                        if item[1:] == ("v", 0):
                            act.wait_ge(pv_done, N_STEPS * h + 1)
                        if item[1] == "y":
                            if item[2] == 0:
                                act.wait_ge(s_full, N_STEPS * HEADS)
                            block_high(0, item[2], y_hi, 32)
                        else:
                            fetch(h if item[1] == "v" else h + 1, item[1], item[2])
                    elif item[0] == "turn":
                        turned(h, *item[1:])

            for c in range(NCH):
                for what in "kqr":
                    fetch(0, what, c)
            for r in range(4):
                exponentials(0, r, [0])
            with act.Fori(0, HEADS - 1) as h:
                head(h, False)
            head(HEADS - 1, True)

            def merge(c, last):
                def high(j):
                    if last and j + 2 >= PER_CHUNK:
                        return
                    if j < 2 * KD:
                        act.wait_ge(e_full, 16 * c + (j + 1))
                    elif j < PER_CHUNK - 1:
                        act.wait_ge(e_outmm, (KD - 1) * c + (j - 2 * KD + 1))
                    else:
                        act.wait_ge(o_full, KD * c + KD)
                    t = T_MERGE + j + 2
                    w_high(t, 1024, 16 * (PER_CHUNK // RAW) * c + 16 * (t // RAW + 1))

                def square(b):
                    for f in range(2):
                        act.wait_ge(o_full, KD * c + (2 * b + f + 1))
                        if 2 * b + f >= 2:
                            act.wait_ge(osq, 8 * c + (2 * b + f - 1))
                        act.activation(sq_t[:, f, :], psum[:, 2 * b + f, :], ACT.Square,
                                       accum_out=o_sq[:, b, f:f + 1]).then_inc(osq, 1)

                def block_root(b):
                    act.wait_ge(o_step, 24 * c + (6 * b + 2))
                    act.activation(o_st[:, b, 1:2], o_st[:, b, 0:1], ACT.Sqrt).then_inc(o_root, 1)

                for k in range(KD):
                    high(k)
                    block_high(16 * c + KD, k, o_hi, 32 * c + 48)
                for n in range(KD):
                    high(KD + n)
                    act.wait_ge(m_r, KD * c + (n + 1))
                    act.activation(m_hi[:, n, :], m_a[:, n, :], ACT.Copy).then_inc(m_hi_r, 1)
                for n in range(KD):
                    if not last:
                        block_high(16 * c + 2 * KD, n, y_hi, 32 * c + 64)
                    if n < KD - 1:
                        high(2 * KD + n)
                for b in range(4):
                    square(b)
                    if b == 2:
                        high(PER_CHUNK - 1)
                    block_root(b)

            with act.Fori(0, NCH - 1) as c:
                merge(c, False)
            merge(NCH - 1, True)

        @blk.vector
        def _(dve):
            for k in range(1, KD):
                for f in range(2):
                    half = slice(1024 * f, 1024 * (f + 1))
                    dve.wait_ge(sq_ready, 2 * k + f + 1)
                    if k > 1:
                        dve.wait_ge(sq_added, 2 * k + f - 3)
                    dve.tensor_tensor(sq_sum[:, half], sq_sum[:, half], squares[:, f, :],
                                      ALU.add).then_inc(sq_added, 1)

            def diagonals(bank, dst, n):
                m = masked[:, n % 2, :].rearrange("p (b n) -> p b n", b=4)
                if n >= 2:
                    dve.wait_ge(diag_step, 2 * n - 2)
                dve.tensor_tensor(m, psum[:, bank, :].rearrange("p (b n) -> p b n", b=4),
                                  ident[:].unsqueeze(1).to_broadcast([P, 4, P]), ALU.mult).then_inc(diag_step, 1)
                dve.wait_ge(diag_step, 2 * n + 1)
                dve.tensor_reduce(dst, m, AX.X, ALU.add).then_inc(diag_step, 1)

            def rsqrt_rest(r_ap, root_n, chain, last_sem, root=t2[:], ms=t1[:]):
                dve.wait_ge(rs_root, root_n)
                dve.reciprocal(r_ap, root).then_inc(rs, 1)
                dve.wait_ge(rs, chain + 1)
                dve.scalar_tensor_tensor(out=root, in0=r_ap, scalar=-0.5, in1=r_ap, op0=ALU.mult,
                                         op1=ALU.mult).then_inc(rs, 1)
                dve.wait_ge(rs, chain + 2)
                dve.tensor_tensor(root, root, ms, ALU.mult).then_inc(rs, 1)
                dve.wait_ge(rs, chain + 3)
                dve.scalar_tensor_tensor(out=r_ap, in0=root, scalar=1.5, in1=r_ap, op0=ALU.add,
                                         op1=ALU.mult).then_inc(last_sem, 1)

            ms, root, r_col = t1[:, 0:SB], t2[:, 0:SB], t1[:, SB:2 * SB]
            for s in range(NCH):
                dve.wait_ge(ssq_ready, s + 1)
                diagonals(s, ms[:, 4 * s:4 * s + 4], s)
            dve.wait_ge(diag_step, 2 * NCH)
            dve.tensor_scalar(ms, ms, 1.0 / D, EPS, ALU.mult, ALU.add).then_inc(rs, 1)
            rsqrt_rest(r_col, 1, 1, rs, root, ms)
            dve.wait_ge(rs, 5)
            for b in range(SB):
                dve.tensor_scalar(diag[:, b, :], ident[:], r_col[:, b:b + 1], None, ALU.mult).then_inc(diag_ready, 1)
            steps = [0]

            def tab_do(ins):
                ins.then_inc(tab_step, 1)
                steps[0] += 1
                dve.wait_ge(tab_step, steps[0])

            dve.wait_ge(cst_in, 16)
            dve.wait_ge(pos_in, 16 * NCH)
            tab_do(dve.tensor_copy(ang[:], pos_i[:]))
            tab_do(dve.tensor_scalar(ang[:], ang[:], consts[:, C_INV:C_INV + 1], None, ALU.mult))
            for unit in (2048.0, 1.0):
                tab_do(dve.tensor_scalar(turns[:], ang[:], float(1.0 / (2.0 * np.pi * unit)), ROUND,
                                         ALU.mult, ALU.add))
                tab_do(dve.tensor_scalar(turns[:], turns[:], -ROUND, None, ALU.add))
                for part in TWO_PI:
                    tab_do(dve.scalar_tensor_tensor(out=ang[:], in0=turns[:], scalar=-part * unit, in1=ang[:],
                                                    op0=ALU.mult, op1=ALU.add))
            tab_do(dve.tensor_scalar(ang[:], ang[:], 3.1415925, -3.1415925, ALU.min, ALU.max))
            assert steps[0] == TAB_STEPS

            for s in range(NCH):
                dve.wait_ge(r_x_ready, s + 1)
                for k in range(KD):
                    if k not in H_LO_POOL:
                        dve.tensor_tensor(x_raw[:, k, chunk(s)], x_raw[:, k, chunk(s)], r_x[:, chunk(s)],
                                          ALU.mult).then_inc(xr_ready, 1)
            for j in range(4):
                dve.wait_ge(ada_ready, j + 1)
                diagonals(4 + j, b_col[:, 4 * j:4 * j + 4], 4 + j)
            dve.wait_ge(diag_step, 4 * NCH)
            dve.tensor_tensor(b_col[:], b_col[:], consts[:, C_BADA:C_BADA + 2 * KD], ALU.add).then_inc(ab_step, 1)
            dve.wait_ge(ab_step, 1)
            dve.scalar_tensor_tensor(out=a_col[:], in0=b_col[:, KD:2 * KD], scalar=1.0,
                                     in1=consts[:, C_GPRE:C_GPRE + KD], op0=ALU.add,
                                     op1=ALU.mult).then_inc(ab_step, 1)
            dve.wait_ge(ab_step, 2)
            for s in range(NCH):
                for k in range(KD):
                    if k in H_LO_POOL:
                        dve.wait_ge(xr_g, len(H_LO_POOL) * s + H_LO_POOL.index(k) + 1)
                    else:
                        dve.wait_ge(xr_ready, len(H_LO_VEC) * s + H_LO_VEC.index(k) + 1)
                    dve.tensor_scalar(x_raw[:, k, chunk(s)], x_raw[:, k, chunk(s)], a_col[:, k:k + 1],
                                      b_col[:, k:k + 1], ALU.mult, ALU.add).then_inc(h32_ready, 1)
                for k in range(KD):
                    if k not in H_LO_POOL:
                        dve.wait_ge(hhi_ready, KD * s + k + 1)
                        dve.tensor_tensor(h_lo[:, k, chunk(s)], x_raw[:, k, chunk(s)],
                                          h_hi[:, k, chunk(s)].bitcast(F32), ALU.subtract).then_inc(hlo_v, 1)

            dve.wait_ge(tab_sin, 1)
            dve.scalar_tensor_tensor(out=tab[:, 0, :], in0=s_half[:], scalar=-2.0, in1=s_half[:],
                                     op0=ALU.mult, op1=ALU.mult).then_inc(tab_step, 1)
            dve.wait_ge(tab_step, TAB_STEPS + 1)
            dve.tensor_scalar(tab[:, 0, :], tab[:, 0, :], 1.0, None, ALU.add).then_inc(tab_ready, 1)
            dve.wait_ge(tab_sin, 2)
            dve.tensor_scalar(tab[:, 2, :], tab[:, 1, :], -1.0, None, ALU.mult).then_inc(tab_ready, 1)
            for t in range(KQ + KKV):
                dst = vs if t < KQ else cv
                for s in range(NCH):
                    dve.wait_ge(p_free[4 * (t % 2) + s], t // 2 + 2)
                    st = stage[:, t % 2, chunk(s)]
                    if t in (0, KQ):
                        dve.tensor_tensor(dst[:, chunk(s)], st, st, ALU.mult).then_inc(lat_sq, 1)
                    else:
                        dve.tensor_tensor(u[:, chunk(s)], st, st, ALU.mult).then_inc(lat_sq, 1)
                        dve.wait_ge(lat_sq, 4 * t + s + 1)
                        done = 4 * (t - 1 if t < KQ else t - 2)
                        if t == 2:
                            dve.wait_ge(lat_add, s + 1)
                        dve.tensor_tensor(dst[:, chunk(s)], dst[:, chunk(s)], u[:, chunk(s)],
                                          ALU.add).then_inc(lat_add, 1)
            for n, (dst, width) in enumerate(((vs, Q_LORA), (cv, KV_LORA))):
                for s in range(NCH):
                    b = 4 * n + s
                    dve.wait_ge(p_full, 4 * (U_SSQ + n) + s + 1)
                    dve.tensor_scalar(t1[:], psum[:, b, :], 1.0 / width, EPS, ALU.mult,
                                      ALU.add).then_inc(p_free[b], 1)
                    rsqrt_rest(dst[:, chunk(s)], NCH * n + s + 2, 5 + 3 * (NCH * n + s), r_ready)
            dve.memset(u[:, 0:2], 0.0).then_inc(u_zero, 1)
            dve.wait_ge(u_zero, 1)
            for n in range(2):
                dve.wait_ge(r_out[n], 16)
            with dve.Fori(0, KD) as i:
                n = U_CONV // 2 + 2
                for s in range(NCH):
                    dve.wait_ge(p_full, 16 * i + (4 * (U_CONV + 1) + s + 1))
                    dve.wait_ge(p_free[s], 2 * i + n)
                    dve.tensor_tensor(u[:, 2 + s * CH:2 + (s + 1) * CH], psum[:, 4 + s, :], vs[:, chunk(s)],
                                      ALU.mult).then_inc(p_free[4 + s], 1)
                for s in range(NCH):
                    dve.wait_ge(p_free[4 + s], 2 * i + n)
                dve.wait_ge(y_out, 16 * i + 16)
                for tap in range(CONV_K):
                    col = C_CONV + tap * KD
                    w_tap = consts[:, bass.ds(i + col, 1)]
                    if tap == 0:
                        dve.tensor_scalar(cv[:], u[:, 0:SEQ], w_tap, None, ALU.mult).then_inc(cv_step, 1)
                    else:
                        dve.wait_ge(cv_step, 3 * i + tap)
                        dve.scalar_tensor_tensor(out=cv[:], in0=u[:, tap:tap + SEQ], scalar=w_tap, in1=cv[:],
                                                 op0=ALU.mult, op1=ALU.add).then_inc(cv_step, 1)
                dve.wait_ge(cv_step, 3 * i + 3)
                for s in range(NCH):
                    dve.wait_ge(p_full, 16 * i + (4 * (U_CONV + 2) + s + 1))
                    dve.tensor_tensor(cv[:, chunk(s)], psum[:, s, :], cv[:, chunk(s)],
                                      ALU.mult).then_inc(p_free[s], 1)
                for s in range(NCH):
                    dve.wait_ge(sg_ready, 4 * i + (s + 1))
                    dve.tensor_tensor(vs[:, chunk(s)], psum[:, 4 + s, :], vs[:, chunk(s)],
                                      ALU.mult).then_inc(p_free[4 + s], 1)
                for s in range(NCH):
                    dve.wait_ge(p_free[4 + s], 2 * i + (n + 1))
                    dve.wait_ge(p_free[s], 2 * i + (n + 1))
                    dve.tensor_tensor(cv[:, chunk(s)], vs[:, chunk(s)], cv[:, chunk(s)],
                                      ALU.mult).then_inc(y_ready, 1)
            with dve.Fori(0, KD // 4) as i:
                for j in range(4):
                    for s in range(NCH):
                        b = 4 * (j % 2) + s
                        dve.wait_ge(sg_ready, 16 * i + (4 * KD + 4 * j + s + 1))
                        dve.tensor_tensor(stage[:, j % 2, chunk(s)], psum[:, b, :], stage[:, j % 2, chunk(s)],
                                          ALU.mult).then_inc(p_free[b], 1)

            dve.tensor_copy(c_hi[:], consts[:, C_C:C_C + KD]).then_inc(cb_step, 1)
            dve.wait_ge(cb_step, 2)
            dve.tensor_tensor(c_lo[:], consts[:, C_C:C_C + KD], c_hi[:].bitcast(F32),
                              ALU.subtract).then_inc(cb_step, 1)
            dve.wait_ge(cb_step, 3)
            for k in range(KD):
                dve.tensor_scalar(c_b_hi[:, k, :], ones[:], c_hi[:, k:k + 1].bitcast(F32), None,
                                  ALU.mult).then_inc(cb_step, 1)
                dve.tensor_scalar(c_b_lo[:, k, :], ones[:], c_lo[:, k:k + 1], None,
                                  ALU.mult).then_inc(cb_step, 1)

            def lat_norm(c, ks, r_n, g0):
                dve.wait_ge(r_in, r_n)
                for k in ks:
                    dve.wait_ge(lat_in[k // KQ], 16)
                    dve.scalar_tensor_tensor(out=lat[:, k, chunk(c)], in0=lat[:, k, chunk(c)],
                                             scalar=consts[:, g0 + k:g0 + k + 1], in1=r_lat[:, chunk(c)],
                                             op0=ALU.mult, op1=ALU.mult).then_inc(nrm, 1)

            def lat_low(c, ks, hi, lo, base):
                for j, k in enumerate(ks):
                    if j == len(ks) - 1:
                        continue
                    dve.wait_ge(nrm_hi, base + len(ks) * c + j + 1)
                    dve.tensor_tensor(lo[:, j, chunk(c)], lat[:, k, chunk(c)], hi[:, j, chunk(c)].bitcast(F32),
                                      ALU.subtract).then_inc(nrm_lo, 1)

            for c in range(NCH):
                lat_norm(c, range(KQ), 16, C_GQ)
                lat_low(c, range(KQ), qn_hi, qn_lo, 0)
            dve.wait_ge(bg_in, 32)
            dve.wait_ge(g_gate, KD)
            for f in range(2):
                half = slice(f * CH, (f + 1) * CH)
                dve.tensor_tensor(gg[:, half], psum[:, 6 + f, :], bg[:, half], ALU.add).then_inc(g_free[6 + f], 1)
                dve.wait_ge(g_free[6 + f], 1)
                dve.tensor_tensor(gg[:, half], gg[:, half], gp[:, half], ALU.mult).then_inc(gg_step, 1)
            for c in range(NCH):
                lat_norm(c, range(KQ, KQ + KKV), 32, C_GQ)
                lat_low(c, range(KQ, KQ + KKV), kn_hi, kn_lo, KQ * NCH)
            dve.wait_ge(ct_in, 16 * 8)
            for n in range(5):
                dve.wait_ge(ra_in, 80 * (n + 1))
                dve.tensor_tensor(rope_a[:], rope_a[:], cos_t[:], ALU.mult).then_inc(rp_step, 1)
                dve.tensor_tensor(rope_b[:], rope_b[:], sin_t[:], ALU.mult).then_inc(rp_step, 1)
                dve.wait_ge(rp_step, 3 * n + 2)
                dve.tensor_tensor(rope_a[:], rope_a[:], rope_b[:], ALU.add).then_inc(rp_step, 1)

            MX = N_STEPS + SB

            def rotary_low(h, c):
                dve.wait_ge(fr_hi, NCH * h + (c + 1))
                dve.tensor_tensor(qr_s[ROPE:P, chunk(c)], a_raw[2][ROPE:P, chunk(c)],
                                  qr_s[ROPE:P, chunk(c)].bitcast(F32), ALU.subtract).then_inc(fr_lo, 1)

            def row_maximum(h, r):
                nb = r // 4 + 1
                first = score_base(r)
                for c in range(nb):
                    dve.wait_ge(s_full, N_STEPS * h + (first + c + 1))
                    dve.tensor_reduce(row_max[:, r % 2, c:c + 1],
                                      psum[:, score_bank(r, c), 0:score_width(r, c)], AX.X,
                                      ALU.max).then_inc(mx_step, 1)
                dve.wait_ge(mx_step, MX * h + (first + r + nb))
                dve.tensor_reduce(all_sum[:, 2, :], row_max[:, r % 2, 0:nb], AX.X, ALU.max).then_inc(mx_step, 1)
                dve.wait_ge(mx_step, MX * h + (first + r + nb + 1))
                dve.tensor_scalar(neg_max[:, r % 2, :], all_sum[:, 2, :], -SCALE, None,
                                  ALU.mult).then_inc(nm_ready, 1)

            def row_inverse(h, r):
                nb = r // 4 + 1
                for c in range(nb):
                    dve.wait_ge(s_free[score_bank(r, c)], BANK_USES * h + (score_use(r, c) + 2))
                dve.tensor_reduce(all_sum[:, r % 2, :], row_sum[:, r % 2, 0:nb], AX.X, ALU.add).then_inc(iv_step, 1)
                dve.wait_ge(iv_step, SB * h + (r + 1))
                dve.wait_ge(p_ready, SB * h + (r + 1))
                dve.reciprocal(inv_sum[:, r % 2, :], all_sum[:, r % 2, :]).then_inc(iv_ready, 1)

            def head(h, last):
                for item in head_plan(last):
                    if item[0] == "row":
                        row_maximum(h + 1 if item[1] else h, item[2])
                    elif item[0] == "inv":
                        row_inverse(h + 1 if item[1] else h, item[2])
                    elif item[0] == "fetch" and item[1] == "r":
                        rotary_low(h + 1, item[2])
                    elif item[0] == "turn":
                        g, j, k = item[1:]
                        cols = step_cols(g, j)
                        dve.wait_ge(pt_hi_r, N_STEPS * h + (k + 1))
                        dve.tensor_tensor(pt_lo[:, k % PT, cols], psum[:, 4 + k % PT, cols],
                                          pt_hi[:, k % PT, cols].bitcast(F32),
                                          ALU.subtract).then_inc(t_free[k % PT], 1)
                    elif item[0] == "out":
                        g = item[1]
                        dve.wait_ge(pv_done, N_STEPS * h + (STEP0[g] + STEPS[g] + 1))
                        dve.wait_ge(sz_in[g % 2], 32 * h + 16 * (g // 2 + 1))
                        dve.tensor_tensor(sz[:, g % 2, :], psum[:, 7, :], sz[:, g % 2, :],
                                          ALU.mult).then_inc(o_ready, 1)

            for c in range(NCH):
                rotary_low(0, c)
            for r in range(4):
                row_maximum(0, r)
                row_inverse(0, r)
            with dve.Fori(0, HEADS - 1) as h:
                head(h, False)
            head(HEADS - 1, True)

            def merge(c, last):
                for n in range(KD):
                    dve.wait_ge(e_full, 16 * c + (n + 1))
                    dve.wait_ge(gr_in[n % 4], 64 * c + 16 * (n // 4 + 1))
                    dve.tensor_tensor(m_a[:, n, :], psum[:, n, :], gr[:, n % 4, :], ALU.mult).then_inc(e_free[n], 1)

                def low(n):
                    dve.wait_ge(m_hi_r, KD * c + (n + 1))
                    dve.tensor_tensor(m_lo[:, n, :], m_a[:, n, :], m_hi[:, n, :].bitcast(F32),
                                      ALU.subtract).then_inc(m_lo_r, 1)

                for n in range(KD):
                    dve.wait_ge(e_full, 16 * c + (KD + n + 1))
                    dve.wait_ge(gr_in[n % 4], 64 * c + 16 * (2 + n // 4 + 1))
                    if n >= 2:
                        dve.wait_ge(m_r, KD * c + (n - 1))
                    dve.tensor_tensor(e_t[:, n % 2, :], psum[:, n, :], gr[:, n % 4, :],
                                      ALU.mult).then_inc(e_free[n], 1)
                    dve.wait_ge(e_free[n], 3 * c + 3)
                    dve.tensor_tensor(m_a[:, n, :], m_a[:, n, :], e_t[:, n % 2, :], ALU.add).then_inc(m_r, 1)
                    if n >= 1:
                        low(n - 1)
                low(KD - 1)
                for b in range(4):
                    sq, st = o_sq[:, b, :], lambda k: o_st[:, b, k:k + 1]
                    base = 24 * c + 6 * b
                    dve.wait_ge(osq, 8 * c + (2 * b + 2))
                    dve.tensor_tensor(st(0), o_sq[:, b, 0:1], o_sq[:, b, 1:2], ALU.add).then_inc(o_step, 1)
                    dve.wait_ge(o_step, base + 1)
                    dve.tensor_scalar(st(0), st(0), 1.0 / D, EPS, ALU.mult, ALU.add).then_inc(o_step, 1)
                    dve.wait_ge(o_root, 4 * c + (b + 1))
                    dve.reciprocal(st(2), st(1)).then_inc(o_step, 1)
                    dve.wait_ge(o_step, base + 3)
                    dve.scalar_tensor_tensor(out=st(3), in0=st(2), scalar=-0.5, in1=st(2), op0=ALU.mult,
                                             op1=ALU.mult).then_inc(o_step, 1)
                    dve.wait_ge(o_step, base + 4)
                    dve.tensor_tensor(st(3), st(3), st(0), ALU.mult).then_inc(o_step, 1)
                    dve.wait_ge(o_step, base + 5)
                    dve.scalar_tensor_tensor(out=st(2), in0=st(3), scalar=1.5, in1=st(2), op0=ALU.add,
                                             op1=ALU.mult).then_inc(o_step, 1)
                    dve.wait_ge(o_step, base + 6)
                    dve.wait_ge(out_done[b % 2], 32 * c + 16 * (b // 2 + 1))
                    for f in range(2):
                        half = slice(f * CH, (f + 1) * CH)
                        dve.scalar_tensor_tensor(out=o_t[:, b % 2, half], in0=psum[:, 2 * b + f, :], scalar=st(2),
                                                 in1=gg[:, half], op0=ALU.mult,
                                                 op1=ALU.mult).then_inc(e_free[2 * b + f], 1)
                    for f in range(2):
                        dve.wait_ge(e_free[2 * b + f], 3 * c + 4)
                    dve.wait_ge(x_t_in[b % 2], 32 * c + 16 * (b // 2 + 1))
                    dve.tensor_tensor(o_t[:, b % 2, :], o_t[:, b % 2, :], x_t[:, b % 2, :],
                                      ALU.add).then_inc(o_done, 1)

            with dve.Fori(0, NCH - 1) as c:
                merge(c, False)
            merge(NCH - 1, True)

        @blk.tensor
        def _(pe):
            pe.wait_ge(ready, 8)
            def ada(k):
                for n, ks in enumerate(WA_LOADS):
                    if k == ks[0]:
                        pe.wait_ge(wa_in[n], 16)
                for j in range(4):
                    last = pe.matmul(psum[:, 4 + j, :], c_b[:, k, :], wa[:, k, chunk(j)], start=k == 0,
                                     stop=k == KD - 1)
                    if k == KD - 1:
                        last.then_inc(ada_ready, 1)

            pe.wait_ge(cb_step, 1)
            ada(0)
            ada(1)
            for s in range(NCH):
                pe.wait_ge(sq_added, 2 * KD - 2 if s >= 2 else 2 * KD - 3)
                pe.matmul(psum[:, s, :], ones[:], sq_sum[:, chunk(s)], start=True, stop=True).then_inc(ssq_ready, 1)
            ada(2)
            ada(3)
            for b in range(SB):
                pe.wait_ge(diag_ready, b + 1)
                last = pe.matmul(psum[:, b // 4, block(b % 4)], ones[:], diag[:, b, :], start=True, stop=True,
                                 skip_group_check=True)
                if b % 4 == 3:
                    last.then_inc(r_bc, 1)
            for k in range(4, KD):
                ada(k)

            def w_tile(p, k, n=P):
                return w_hi[:, p, k * n:(k + 1) * n], w_lo[:, p, k * n:(k + 1) * n]

            def unit(p, kk, x_hi, x_lo, full, free, tile_n, free_n, before=None):
                pe.wait_ge(wlo, tile_n)
                for s in range(NCH):
                    pe.wait_ge(free[4 * p + s], free_n)
                    for k in range(kk):
                        if before:
                            before(s, k)
                        last = accumulate(pe, psum[:, 4 * p + s, :],
                                          parts(*w_tile(p, k), x_hi[:, k, chunk(s)], x_lo[:, k, chunk(s)]),
                                          start=k == 0, stop=k == kk - 1)
                    last.then_inc(full, 1)

            def h_chunk(s, k):
                if k in H_LO_POOL:
                    pe.wait_ge(hlo_g, len(H_LO_POOL) * s + H_LO_POOL.index(k) + 1)
                else:
                    pe.wait_ge(hlo_v, len(H_LO_VEC) * s + H_LO_VEC.index(k) + 1)

            for t in range(N_LAT):
                unit(t % 2, KD, h_hi, h_lo, p_full, p_free, t + 1, t // 2 + 1, h_chunk if t == 0 else None)
            for n, src in enumerate((vs, cv)):
                for s in range(NCH):
                    pe.wait_ge(p_free[4 * n + s], U_SSQ // 2 + 1)
                    pe.wait_ge(lat_add, 4 * (KQ - 2) + s + 1 if n == 0 else 4 * (KQ - 1) + s + 1)
                    pe.matmul(psum[:, 4 * n + s, :], ones[:], src[:, chunk(s)], start=True,
                              stop=True).then_inc(p_full, 1)
            with pe.Fori(0, (N_CONV + N_GATES) // 4) as i:
                for j in range(4):
                    unit(j % 2, KD, h_hi, h_lo, p_full, p_free, 4 * i + (N_LAT + j + 1),
                         2 * i + (U_CONV // 2 + j // 2 + 1))

            for b in range(8):
                pe.wait_ge(p_free[b], N_UNITS // 2 + 1)
            pe.wait_ge(cb_step, 3 + 2 * KD)
            for k in range(KD):
                t = T_ADA + k
                pe.wait_ge(wlo, t + 1)
                for f in range(2):
                    last = accumulate(pe, psum[:, 6 + f, :],
                                      parts(c_b_hi[:, k, :], c_b_lo[:, k, :], w_hi[:, t % 2, chunk(f)],
                                            w_lo[:, t % 2, chunk(f)]), start=k == 0, stop=k == KD - 1)
                last.then_inc(g_gate, 1)

            def qn_chunk(s, k):
                if k == KQ - 1:
                    pe.wait_ge(nrm_lo_g, s + 1)
                else:
                    pe.wait_ge(nrm_lo, (KQ - 1) * s + k + 1)

            for g in range(G_V):
                unit(g % 2, KQ, qn_hi, qn_lo, g_full, g_free, T_QR + g + 1, g // 2 + 1, qn_chunk if g == 0 else None)
            pe.wait_ge(wlo, T_V + KKV)
            for g in range(G_V, G_K):
                for s in range(NCH):
                    b, f = 2 * (g - G_V) + s // 2, s % 2
                    pe.wait_ge(nrm_lo, (KQ - 1) * NCH + (KKV - 1) * (b // 4 + 1))
                    pe.wait_ge(nrm_lo_g, NCH + b // 4 + 1)
                    bank = 4 * (g % 2) + s
                    pe.wait_ge(g_free[bank], g // 2 + 1)
                    pairs = []
                    for k in range(KKV):
                        pairs += parts(kn_hi[:, k, block(b)], kn_lo[:, k, block(b)],
                                       w_hi[:, k, chunk(f)], w_lo[:, k, chunk(f)])
                    accumulate(pe, psum[:, bank, :], pairs).then_inc(g_full, 1)
            for first, tile, kk, hi, lo in ((G_K, T_K, KKV, kn_hi, kn_lo), (G_Q, T_Q, KQ, qn_hi, qn_lo)):
                with pe.Fori(0, HEADS // 2) as i:
                    for j in range(2):
                        unit(j, kk, hi, lo, g_full, g_free, 2 * i + (tile + j + 1), i + (first // 2 + 1))

            for b in range(8):
                pe.wait_ge(g_free[b], G_UNITS // 2 + 1)
            pe.wait_ge(kr_lo_r, NCH)

            def scores(h, r):
                nb = r // 4 + 1
                pe.wait_ge(fk_lo, NCH * h + nb)
                pe.wait_ge(fq_lo, NCH * h + nb)
                pe.wait_ge(fr_lo, NCH * h + nb)
                for c in range(nb):
                    w = score_width(r, c)
                    cols = slice(c * CH, c * CH + w)
                    bank = psum[:, score_bank(r, c), 0:w]
                    pe.wait_ge(s_free[score_bank(r, c)], BANK_USES * h + (score_use(r, c) + 1))
                    rows = block(r)
                    pe.matmul(bank, q_hi[:, rows], k_lo[:, cols], start=True, stop=False)
                    pe.matmul(bank, q_lo[:, rows], k_hi[:, cols], start=False, stop=False)
                    pe.matmul(bank, qr_s[:, rows], kr_lo[:, cols], start=False, stop=False)
                    pe.matmul(bank, qr_s[:, rows], kr_hi[:, cols], start=False, stop=False)
                    if c == nb - 1:
                        pe.matmul(bank[:, w - P:w], ident_b[:], mask_b[:], start=False, stop=False)
                    pe.matmul(bank, q_hi[:, rows], k_hi[:, cols], start=False, stop=True).then_inc(s_full, 1)

            def head(h, last):
                for item in head_plan(last):
                    if item[0] == "row":
                        scores(h + 1 if item[1] else h, item[2])
                    elif item[0] == "turn":
                        g, j, k = item[1:]
                        slot = k % PT
                        pe.wait_ge(t_free[slot], T_USES[slot] * h + (k // PT + 1))
                        for i in range(max(0, j - 4 * g), 4):
                            if j == 0:
                                pe.wait_ge(p_ready, SB * h + (4 * g + i + 3))
                            ins = pe.transpose(psum[:, 4 + slot, block(i)], prob(4 * g + i)[:, block(j)], ident[:])
                        ins.then_inc(t_full, 1)
                    elif item[0] == "mul":
                        g, j, k = item[1:]
                        slot = k % PT
                        if j == 0:
                            pe.wait_ge(o_ready, 4 * h + (g + 1))
                        pe.wait_ge(fv_lo, NCH * h + (j // 4 + 1))
                        pe.wait_ge(t_free[slot], T_USES[slot] * h + (k // PT + 2))
                        cols = step_cols(g, j)
                        accumulate(pe, psum[:, 7, cols], parts(v_hi[:, block(j)], v_lo[:, block(j)],
                                                               pt_hi[:, slot, cols], pt_lo[:, slot, cols]),
                                   start=j == 0, stop=j == STEPS[g] - 1).then_inc(pv_done, 1)

            for r in range(4):
                scores(0, r)
            with pe.Fori(0, HEADS - 1) as h:
                head(h, False)
            head(HEADS - 1, True)

            for c in range(NCH):
                pe.wait_ge(s_free[c], BANK_USES * HEADS + 1)
            for s in range(PT):
                pe.wait_ge(t_free[s], T_USES[s] * HEADS + 1)
            pe.wait_ge(o_ready, 4 * HEADS + 1)

            def merge(c):
                for n in range(2 * KD):
                    hi, lo = (y_hi, y_lo) if n < KD else (o_hi, o_lo)
                    pe.wait_ge(wlo, PER_CHUNK * c + (T_MERGE + n + 1))
                    pe.wait_ge(e_free[n % KD], 3 * c + (n // KD + 1))
                    for k in range(KD):
                        if n % KD == 0:
                            pe.wait_ge(e_lo, 16 * c + (n + k + 1))
                        last = accumulate(pe, psum[:, n % KD, :], parts(*w_tile(n % 2, k), hi[:, k, :], lo[:, k, :]),
                                          start=k == 0, stop=k == KD - 1)
                    last.then_inc(e_full, 1)
                for k in range(KD):
                    pe.wait_ge(wlo, PER_CHUNK * c + (T_MERGE + 2 * KD + k + 1))
                    pe.wait_ge(m_lo_r, KD * c + (k + 1))
                    for b in range(4):
                        for f in range(2):
                            if k == 0:
                                pe.wait_ge(e_free[2 * b + f], 3 * c + 3)
                            last = accumulate(pe, psum[:, 2 * b + f, :],
                                              parts(m_hi[:, k, block(b)], m_lo[:, k, block(b)],
                                                    w_hi[:, k % 2, chunk(f)], w_lo[:, k % 2, chunk(f)]),
                                              start=k == 0, stop=k == KD - 1)
                            if k == KD - 1:
                                last.then_inc(o_full, 1)
                    if k < KD - 1:
                        last.then_inc(e_outmm, 1)

            with pe.Fori(0, NCH) as c:
                merge(c)


def kernel(x, c, positions, w_ada, b_ada, g_pre, w_in, conv_w, w_conv_out, g_q, w_uq, g_kv, w_ukv,
           w_mla_out, w_out, g_post):
    import numpy as _np
    import concourse.bacc as _bacc
    from concourse import mybir as _mybir
    from concourse.bass_utils import run_bass_kernel_spmd as _run

    def cols(v, n):
        return _np.ascontiguousarray(v.reshape(n, P).T)

    def tiles(w, perm=None):
        k, n = w.shape
        return w.reshape(k // P, P, n // P, P).transpose(2, 1, 0, 3).reshape(n // P, P, k)

    x, w_ada, b_ada, w_in, w_uq, w_ukv = (_np.asarray(a) for a in (x[0], w_ada[0], b_ada[0], w_in[0], w_uq[0], w_ukv[0]))
    inv_freq = (_np.float64(ROPE_THETA) ** (-_np.arange(0, ROPE, 2) / ROPE)).astype(_np.float32)
    cst = _np.concatenate([cols(_np.asarray(c[0]), KD), cols(b_ada[:2 * D], 2 * KD), cols(_np.asarray(g_pre[0]), KD),
                           cols(_np.asarray(g_q[0]), KQ), cols(_np.asarray(g_kv[0]), KKV),
                           cols(_np.asarray(conv_w[0]).reshape(-1), CONV_K * KD),
                           _np.tile(inv_freq, 4)[:, None]], axis=1)
    conv = tiles(w_in[:, :4 * D]).reshape(4, KD, P, D)
    lat0 = 4 * D
    rope0 = lat0 + Q_LORA + KV_LORA
    w_rope = w_in[:, rope0:rope0 + ROPE]
    w1 = _np.concatenate([
        tiles(w_in[:, lat0:rope0]),
        tiles(_np.concatenate([w_rope, w_rope], axis=1)),
        conv[[0, 2, 1, 3]].transpose(1, 0, 2, 3).reshape(N_CONV, P, D),
        tiles(w_in[:, rope0 + ROPE:]),
        w_ada[:, 2 * D:].reshape(KD, P, D),
    ])
    uq = w_uq.reshape(Q_LORA, HEADS, NOPE + ROPE)
    ukv = w_ukv.reshape(KV_LORA, HEADS, NOPE + VD)
    arrays = {
        "x": x.reshape(SB, P, D),
        "xt": x.T.reshape(KD, P, SEQ),
        "cst": cst,
        "pos": _np.asarray(positions),
        "b_gate": b_ada[None, 2 * D:],
        "g_post": _np.asarray(g_post),
        "wada": w_ada[:, :2 * D].reshape(KD, P, 2 * D),
        "w1": w1,
        "wqr": tiles(uq[:, :, NOPE:].reshape(Q_LORA, HEADS * ROPE)),
        "wv": ukv[:, :, NOPE:].reshape(KKV, P, HEADS * VD),
        "wk": tiles(ukv[:, :, :NOPE].reshape(KV_LORA, HEADS * NOPE)),
        "wq": tiles(uq[:, :, :NOPE].reshape(Q_LORA, HEADS * NOPE)),
        "wm": _np.concatenate([tiles(_np.asarray(w_conv_out[0])), tiles(_np.asarray(w_mla_out[0])),
                               _np.asarray(w_out[0]).reshape(KD, P, D)]),
    }
    nc = _bacc.Bacc("TRN2", target_bir_lowering=False, num_devices=1)
    args, named = {}, {}
    for name, a in arrays.items():
        a = _np.ascontiguousarray(a)
        named[f"in_{name}"] = a
        args[name] = nc.dram_tensor(f"in_{name}", a.shape, _mybir.dt.from_np(a.dtype), kind="ExternalInput").ap()
    out = nc.dram_tensor("out", (SB, P, D), F32, kind="ExternalOutput").ap()
    build(nc, out=out, **args)
    r = _run(nc, [named], core_ids=[0])
    return r.results[0]["out"].reshape(1, SEQ, D)
```

```python
from contextlib import ExitStack

import numpy as np

import concourse.bass as bass
from concourse import mybir

P = 128
SEQ, D = 2048, 1024
KD = D // P
CH = 512
NCH = SEQ // CH
SB = SEQ // P
HEADS, NOPE, ROPE, VD = 8, 128, 64, 128
Q_LORA, KV_LORA = 384, 256
KQ, KKV = Q_LORA // P, KV_LORA // P
CONV_K = 3
EPS = 1e-6
ROPE_THETA = 10000.0
SCALE = float((NOPE + ROPE) ** -0.5)
HALF = ROPE // 2
MASKED = -3.0e38

N_LAT = 6
N_CONV = 4 * KD
N_GATES = 3 * KD
N_PROJ = N_LAT + N_CONV + N_GATES
T_ADA = N_PROJ
T_SHARED = T_ADA + 2
T_QR = T_ADA + KD
T_V = T_QR + HEADS // 2
T_K = T_V + KKV
T_Q = T_K + HEADS
T_MERGE = T_Q + HEADS
PER_CHUNK = 3 * KD
RAW = 4

C_C = 0
C_BADA = C_C + KD
C_GPRE = C_BADA + 2 * KD
C_GQ = C_GPRE + KD
C_GKV = C_GQ + KQ
C_CONV = C_GKV + KKV
C_INV = C_CONV + CONV_K * KD
N_CST = C_INV + 1

ROUND = 12582912.0


def _parts(x, bits, n):
    out = []
    for _ in range(n - 1):
        e = np.floor(np.log2(x))
        step = 2.0 ** (e - bits + 1)
        p = np.floor(x / step) * step
        out.append(float(p))
        x = x - p
    return out + [float(np.float32(x))]


TWO_PI = _parts(2.0 * np.pi, 8, 5)

F32 = mybir.dt.float32
F32R = mybir.dt.float32r
BF16 = mybir.dt.bfloat16
I32 = mybir.dt.int32
ACT = mybir.ActivationFunctionType
ALU = mybir.AluOpType
AX = mybir.AxisListType


def chunk(s):
    return slice(s * CH, (s + 1) * CH)


def block(i):
    return slice(i * P, (i + 1) * P)


SPREAD = [[0, 1, 1, 1, 1], [0, 1, 2, 2, 3], [0, 2, 2, 3, 5], [4, 4, 4, 4, 0]]
STEPS = [4 * (g + 1) for g in range(4)]
STEP0 = [0, 4, 12, 24]
N_STEPS = 40
PT = 3


def head_plan(last):
    plan, waiting, done = [], [], [0] * 4
    after_turn = []

    def mul():
        g, j, k = waiting.pop(0)
        plan.append(("mul", g, j, k))
        if j == STEPS[g] - 1:
            plan.append(("out", g))

    def steps(g, n):
        for _ in range(n):
            if len(waiting) == PT:
                mul()
            if after_turn and after_turn[0] and after_turn[0][0][0] == "inv":
                plan.extend(after_turn.pop(0))
            j = done[g]
            plan.append(("turn", g, j, STEP0[g] + j))
            waiting.append((g, j, STEP0[g] + j))
            done[g] += 1
            if after_turn:
                plan.extend(after_turn.pop(0))

    def row(nxt, r):
        plan.append(("row", nxt, r))
        late = [[("exp", nxt, r, c)] for c in range(2, r // 4 + 1)]
        if late:
            late[-1].append(("inv", nxt, r))
        else:
            late = [[("inv", nxt, r)]]
        after_turn[:0] = late

    def flush():
        while after_turn:
            plan.extend(after_turn.pop(0))

    for g in range(4):
        nxt = g == 3
        if g == 0:
            plan.append(("fetch", "v", 0))
            after_turn += [[("fetch", "v", c)] for c in range(1, NCH)]
        if g == 3 and last:
            after_turn += [[("fetch", "y", k)] for k in range(KD)] + [[("fetch", "w", n)] for n in range(2)]
        if g == 3 and not last:
            after_turn += [[("fetch", what, c)] for what, c in
                           (("k", 1), ("k", 2), ("k", 3), ("q", 1), ("r", 1), ("q", 2), ("r", 2), ("q", 3), ("r", 3))]
        steps(g, SPREAD[g][0])
        for i in range(4):
            r = i if nxt else 4 * (g + 1) + i
            if not (nxt and last):
                row(nxt, r)
                if r == 15 and not last:
                    after_turn += [[("fetch", "k", 0)], [("fetch", "q", 0), ("fetch", "r", 0)]]
            steps(g, SPREAD[g][i + 1])
            while any(x[0] in ("exp", "inv") for items in after_turn for x in items):
                plan.extend(after_turn.pop(0))
        if g != 0:
            flush()
    while waiting:
        mul()
    return plan


def vector_plan(last):
    plan, held, pending, hold = [], [], [], False
    for item in head_plan(last):
        if item[0] == "row":
            plan += pending
            nxt, r = item[1:]
            maxima = [("max", nxt, r, c) for c in range(r // 4 + 1)]
            if r >= 12:
                turns = [x for x in held if x[0] == "turn"]
                pending = [x for x in held if x[0] != "turn"]
                while turns or maxima:
                    plan += turns[:1] + maxima[:1]
                    turns, maxima = turns[1:], maxima[1:]
            else:
                plan += maxima
                pending = held
            plan.append(("shift", nxt, r))
            held = []
            hold = not nxt and r % 4 != 3
        elif item[0] in ("turn", "inv"):
            plan += pending
            pending = []
            (held if hold else plan).append(item)
        elif item[0] == "out":
            before = plan[-1][0] == "turn" and plan[-1][1] != item[1]
            plan.insert(len(plan) - before, item)
        elif item[0] == "fetch" and item[1] == "r":
            plan.append(item)
    assert not held and not pending
    return plan


def width_of(t):
    if T_QR <= t < T_V or T_Q <= t < T_MERGE:
        return KQ * P
    if T_K <= t < T_Q:
        return KKV * P
    return 1024


def score_width(r, c):
    return CH if c < r // 4 else (r % 4 + 1) * P


def score_base(r):
    return sum(q // 4 + 1 for q in range(r))


def score_bank(r, c):
    return (score_base(r) + c) % 4


def score_use(r, c):
    return (score_base(r) + c) // 4


BANK_USES = N_STEPS // 4


def step_cols(g, j):
    return slice(max(0, j - 4 * g) * P, CH)


T_USES = [len(range(s, N_STEPS, PT)) for s in range(PT)]
H_LO_POOL = (1, 4, 7)
H_LO_VEC = tuple(
    k for k in range(KD) if k not in H_LO_POOL)
TAB_STEPS = 17
WA_LOADS = ((0, 1), (1, 2), (2, 4), (4, 6), (6, 8))
U_SSQ = N_LAT
U_CONV = U_SSQ + 2
U_GATES = U_CONV + N_CONV
N_UNITS = U_GATES + N_GATES
M0 = N_LAT + N_GATES
G_QR, G_V = 0, HEADS // 2
G_K = G_V + SB // 2
G_Q = G_K + HEADS
G_UNITS = G_Q + HEADS
ROPE_AT = (G_V + 1, G_V + 5, G_V + 9, G_V + 13, G_Q)


def build(nc, x, xt, cst, pos, b_gate, g_post, wada, w1, wqr, wv, wk, wq, wm, out):
    with ExitStack() as ctx:
        sem = lambda name: ctx.enter_context(nc.semaphore(name))
        sems = lambda name, n: [sem(f"{name}{i}") for i in range(n)]
        dram = lambda name, shape: nc.dram_tensor(name, shape, F32)
        psum = ctx.enter_context(nc.psum_tensor("psum", [P, 8, CH], F32))

        base = (nc.sbuf_base + 63) // 64 * 64

        def at(name, kib, shape, dt=F32):
            return nc.alloc_sbuf_tensor_at(name, [P] + list(shape), dt, offset=base + int(kib * 1024))

        w_raw = at("w_raw", 0, [RAW, 1024])
        w_hi = at("w_hi", 16, [2, 1024], F32R)
        w_lo = at("w_lo", 24, [2, 1024], F32R)
        ones = at("ones", 32, [P])
        ident = at("ident", 32.5, [P])
        ident_b = at("ident_b", 33, [P], BF16)
        mask_b = at("mask_b", 33.25, [P], BF16)
        consts = at("consts", 33.5, [N_CST])
        a_col = at("a_col", 33.8125, [KD])
        b_col = at("b_col", 33.875, [2 * KD])
        c_hi = at("c_hi", 33.9375, [KD], F32R)
        c_lo = at("c_lo", 34.4375, [KD])
        row_max = at("row_max", 34, [2, NCH])
        row_sum = at("row_sum", 34.0625, [2, NCH])
        neg_max = at("neg_max", 34.125, [2, 1])
        all_sum = at("all_sum", 34.1875, [3, 1])
        inv_sum = at("inv_sum", 34.25, [2, 1])
        o_sq = at("o_sq", 34.3125, [4, 2])
        o_st = at("o_st", 34.34375, [4, 4])
        R = 34.5
        h_hi = at("h_hi", R, [KD, SEQ], F32R)
        h_lo = at("h_lo", R + 64, [KD, SEQ], F32R)
        wa = at("wa", R, [KD, 2 * D])
        x_raw = at("x_raw", R + 64, [KD, SEQ])
        vs = at("vs", R + 128, [SEQ])
        cv = at("cv", R + 136, [SEQ])
        stage = at("stage", R + 144, [2, SEQ])
        u = at("u", R + 160, [SEQ + 2])
        t1 = at("t1", R + 168.0625, [CH])
        t2 = at("t2", R + 170.0625, [CH])
        lat_ms, lat_root, r_lat_col = (t1[:, 2 * SB * i:2 * SB * (i + 1)] for i in range(1, 4))
        squares = at("squares", R + 128, [2, 1024])
        diag = at("diag", R + 128, [SB, P])
        sq_sum = at("sq_sum", R + 136, [SEQ])
        r_x = at("r_x", R + 136, [SEQ])
        c_b = at("c_b", R + 160, [KD, P])
        masked = at("masked", R + 164, [2, CH])
        ang = at("ang", R + 144, [CH])
        pos_i = at("pos_i", R + 146, [CH], I32)
        turns = at("turns", R + 148, [CH])
        s_half = at("s_half", R + 150, [CH])
        tab = at("tab", R + 152, [3, CH])
        qn_hi = at("qn_hi", R, [KQ, SEQ], F32R)
        qn_lo = at("qn_lo", R + 24, [KQ, SEQ], F32R)
        kn_hi = at("kn_hi", R + 48, [KKV, SEQ], F32R)
        kn_lo = at("kn_lo", R + 64, [KKV, SEQ], F32R)
        lat = [at(f"lat{k}", R + (136, 80, 88, 96, 104)[k], [SEQ]) for k in range(KQ + KKV)]
        c_b_hi = at("c_b_hi", R + 128, [KD, P], F32R)
        c_b_lo = at("c_b_lo", R + 132, [KD, P], F32R)
        bg = at("bg", R + 112, [D])
        gp = at("gp", R + 116, [D])
        gg = at("gg", R + 120, [D])
        r_lat = at("r_lat", R + 160, [SEQ])
        rope_a = at("rope_a", R + 80, [SEQ])
        rope_b = at("rope_b", R + 88, [SEQ])
        cos_t = at("cos_t", R + 124, [SEQ])
        sin_t = at("sin_t", R + 132, [SEQ])
        q_hi = at("q_hi", R, [SEQ], F32R)
        q_lo = at("q_lo", R + 8, [SEQ], F32R)
        v_hi = at("v_hi", R + 16, [SEQ], F32R)
        v_lo = at("v_lo", R + 24, [SEQ], F32R)
        sz = at("sz", R + 44, [2, CH])
        k_hi = at("k_hi", R + 48, [SEQ], F32R)
        k_lo = at("k_lo", R + 56, [SEQ], F32R)
        qr_s = at("qr_s", R + 64, [SEQ], F32R)
        kr_hi = at("kr_hi", R + 96, [SEQ], F32R)
        kr_lo = at("kr_lo", R + 104, [SEQ], F32R)
        a_raw = [at(f"a_raw{i}", R + (80, 88, 112)[i], [SEQ]) for i in range(3)]
        pt_hi = at("pt_hi", R + 160, [PT, CH], F32R)
        pt_lo = at("pt_lo", R + 166, [PT, CH], F32R)
        p_even = [at(f"p_even{i}", R + (32, 38, 124, 130)[i], [3 * CH]) for i in range(4)]
        p_odd = [at(f"p_odd{i}", R + (72, 136, 144, 152)[i], [4 * CH]) for i in range(4)]
        e_raw = at("e_raw", R, [KD, CH])
        m_hi = at("m_hi", R + 16, [KD, CH], F32R)
        o_lo = at("o_lo", R + 32, [KD, CH], F32R)
        o_hi = at("o_hi", R + 48, [KD, CH], F32R)
        m_lo = at("m_lo", R + 64, [KD, CH], F32R)
        y_hi = at("y_hi", R + 80, [KD, CH], F32R)
        y_lo = at("y_lo", R + 96, [KD, CH], F32R)
        gr = at("gr", R + 112, [4, CH])
        m_a = at("m_a", R + 124, [KD, CH])
        x_t = at("x_t", R + 140, [2, D])
        o_t = at("o_t", R + 148, [2, D])
        e_t = at("e_t", R + 156, [2, CH])
        sq_t = at("sq_t", R + 160, [2, CH])

        lat_d = dram("lat_d", (N_LAT, P, SEQ))
        r_d = dram("r_d", (2, SEQ))
        tab_d = dram("tab_d", (3, P, CH))
        y_d = dram("y_d", (KD, P, SEQ))
        gate_d = dram("gate_d", (N_GATES, P, SEQ))
        qr_d = dram("qr_d", (HEADS // 2, P, SEQ))
        v_d = dram("v_d", (SB, P, HEADS * VD))
        k_d = dram("k_d", (HEADS, P, SEQ))
        q_d = dram("q_d", (HEADS, P, SEQ))
        roped_d = dram("roped_d", (HEADS // 2, P, SEQ))
        o_d = dram("o_d", (HEADS, P, SEQ))

        cst_in = sem("cst_in")
        pos_in = sem("pos_in")
        settled = sem("settled")
        x_in = sems("x_in", KD)
        wa_in = sems("wa_in", len(WA_LOADS))
        ready = sem("ready")
        sq_ready = sem("sq_ready")
        sq_added = sem("sq_added")
        ssq_ready = sem("ssq_ready")
        diag_step = sem("diag_step")
        diag_ready = sem("diag_ready")
        r_bc = sem("r_bc")
        r_x_ready = sem("r_x_ready")
        ada_ready = sem("ada_ready")
        ab_step = sem("ab_step")
        rs = sem("rs")
        rs_root = sem("rs_root")
        xr_ready = sem("xr_ready")
        xr_g = sem("xr_g")
        h32_ready = sem("h32_ready")
        hhi_ready = sem("hhi_ready")
        hlo_v = sem("hlo_v")
        hlo_g = sem("hlo_g")
        tab_step = sem("tab_step")
        tab_sin = sem("tab_sin")
        tab_ready = sem("tab_ready")
        tab_out = sem("tab_out")
        w_in = sems("w_in", RAW)
        whi = sem("whi")
        wlo = sem("wlo")
        p_full = sem("p_full")
        p_free = sems("p_free", 8)
        lat_sq = sem("lat_sq")
        lat_add = sem("lat_add")
        r_ready = sem("r_ready")
        r_out = sem("r_out")
        u_zero = sem("u_zero")
        cv_step = sem("cv_step")
        sg_ready = sem("sg_ready")
        y_ready = sem("y_ready")
        y_out = sem("y_out")
        st_out = sems("st_out", 2)
        cb_step = sem("cb_step")
        bg_in = sem("bg_in")
        wlo_v = sem("wlo_v")
        g_gate = sem("g_gate")
        gg_step = sem("gg_step")
        g_full = sem("g_full")
        g_free = sems("g_free", 8)
        lat_in = sems("lat_in", 3)
        r_in = sem("r_in")
        nrm = sem("nrm")
        nrm_hi = sem("nrm_hi")
        nrm_lo = sem("nrm_lo")
        nrm_lo_g = sem("nrm_lo_g")
        ct_in = sem("ct_in")
        ra_in = sem("ra_in")
        rp_step = sem("rp_step")
        rp_out = sem("rp_out")
        a_in = sems("a_in", 3)
        kr_hi_r = sem("kr_hi_r")
        kr_lo_r = sem("kr_lo_r")
        fk_hi = sem("fk_hi")
        fk_lo = sem("fk_lo")
        fq_hi = sem("fq_hi")
        fq_lo = sem("fq_lo")
        fr_hi = sem("fr_hi")
        fr_lo = sem("fr_lo")
        fv_hi = sem("fv_hi")
        fv_lo = sem("fv_lo")
        s_full = sem("s_full")
        s_free = sems("s_free", NCH)
        mx_step = sem("mx_step")
        nm_ready = sem("nm_ready")
        iv_step = sem("iv_step")
        iv_ready = sem("iv_ready")
        p_ready = sem("p_ready")
        t_full = sem("t_full")
        t_free = sems("t_free", PT)
        pt_hi_r = sem("pt_hi_r")
        pv_done = sem("pv_done")
        sz_in = sems("sz_in", 2)
        o_ready = sem("o_ready")
        o_out = sems("o_out", 2)
        e_hi = sem("e_hi")
        e_lo = sem("e_lo")
        e_full = sem("e_full")
        e_outmm = sem("e_outmm")
        o_full = sem("o_full")
        e_free = sems("e_free", 8)
        gr_in = sems("gr_in", 4)
        m_r = sem("m_r")
        m_hi_r = sem("m_hi_r")
        m_lo_r = sem("m_lo_r")
        x_t_in = sems("x_t_in", 2)
        osq = sem("osq")
        o_root = sem("o_root")
        o_step = sem("o_step")
        o_done = sem("o_done")
        out_done = sems("out_done", 2)

        def prob(r):
            return (p_even, p_odd)[r // 4 % 2][r % 4]

        blk = ctx.enter_context(nc.Block())

        def parts(whi_, wlo_, xhi_, xlo_):
            return [(whi_, xlo_), (wlo_, xhi_), (whi_, xhi_)]

        def accumulate(pe, bank, pairs, start=True, stop=True, skip=False):
            for i, (a, b) in enumerate(pairs):
                last = pe.matmul(bank, a, b, start=start and i == 0, stop=stop and i == len(pairs) - 1,
                                 skip_group_check=skip)
            return last

        def residual(eng, c, b):
            for f in range(2):
                eng.wait_ge(e_free[2 * b + f], 3 * c + 4)
            eng.wait_ge(x_t_in[b % 2], 32 * c + 16 * (b // 2 + 1))
            eng.tensor_tensor(o_t[:, b % 2, :], o_t[:, b % 2, :], x_t[:, b % 2, :], ALU.add).then_inc(o_done, 1)


        @blk.sync
        def _(sp):
            def settle():
                sp.sem_inc(settled, 1)

            def load_w(t, src, width, before):
                if before is not None:
                    sp.wait_ge(wlo, before)
                sp.dma_start(w_raw[:, t % RAW, 0:width], src).then_inc(w_in[t % RAW], 16)

            def load_tile(t):
                if t < T_QR:
                    src = w1[t]
                elif t < T_V:
                    src = wqr[t - T_QR]
                elif t < T_K:
                    src = wv[t - T_V]
                elif t < T_Q:
                    src = wk[t - T_K]
                elif t < T_MERGE:
                    src = wq[t - T_Q]
                else:
                    src = wm[t - T_MERGE]
                if T_QR > t - RAW >= T_SHARED:
                    sp.wait_ge(wlo_v, t - RAW - T_SHARED + 1)
                load_w(t, src, width_of(t), t - RAW + 1 if t >= RAW else None)

            sp.dma_start(consts[:], cst).then_inc(cst_in, 16)
            for c in range(NCH):
                sp.dma_start(pos_i[c * HALF:(c + 1) * HALF, :],
                             pos[:, chunk(c)].to_broadcast([HALF, CH])).then_inc(pos_in, 16)
            def load_wa(n):
                ks = slice(*WA_LOADS[n])
                sp.dma_start(wa[:, ks, :], wada[ks].rearrange("k p n -> p k n")).then_inc(wa_in[n], 16)

            for k in range(KD):
                sp.dma_start(x_raw[:, k, :], xt[k]).then_inc(x_in[k], 16)
                if k in (3, 5):
                    load_wa(k // 2 - 1)
            for n in range(2, len(WA_LOADS)):
                load_wa(n)
            for t in range(RAW):
                load_tile(t)
            sp.wait_ge(tab_ready, 2)
            sp.dma_start(tab_d.ap().rearrange("a p n -> p a n"), tab[:]).then_inc(tab_out, 16)

            def store(dst, slot, free, at_least):
                for s in range(NCH):
                    sp.wait_ge(free[s], at_least)
                    settle()
                sp.dma_start(dst, stage[:, slot, :]).then_inc(st_out[slot], 16)

            def banks(sem_list, n):
                return sem_list[4 * (n % 2):4 * (n % 2) + 4]

            for t in range(N_LAT):
                load_tile(t + RAW)
                store(lat_d[t], t % 2, banks(p_free, t), t // 2 + 2)
            sp.wait_ge(r_ready, 1)
            with nc.allow_non_contiguous_dma(reason="columns to rows, 16 KiB in all"):
                sp.dma_start(r_d.ap().rearrange("n (b p) -> p (n b)", p=P), r_lat_col).then_inc(r_out, 16)
            with sp.Fori(0, KD) as i:
                for j in range(4):
                    t = N_LAT + j + RAW
                    load_w(t, w1[4 * i + t], 1024, 4 * i + (t - RAW + 1))
                sp.wait_ge(y_ready, 4 * i + 8)
                sp.dma_start(y_d[i], cv[:]).then_inc(y_out, 16)
            def gates(i, last):
                for j in range(4):
                    t = N_LAT + N_CONV + j + RAW
                    load_w(t, w1[4 * i + t], 1024, 4 * i + (t - RAW + 1))
                    if last and j == 3:
                        load_tile(T_ADA + RAW)
                    store(gate_d[4 * i + j], j % 2, banks(p_free, j), 2 * i + (U_GATES // 2 + j // 2 + 2))

            for n in range(2):
                sp.wait_ge(st_out[n], 16 * (N_LAT // 2))
            sp.wait_ge(r_out, 16)
            sp.wait_ge(y_out, 16 * KD + 16)
            sp.dma_start(r_lat[:], r_d[0:1].to_broadcast([P, SEQ])).then_inc(r_in, 16)
            sp.dma_start(lat[0][:], lat_d[0]).then_inc(lat_in[0], 16)
            with sp.Fori(0, N_GATES // 4 - 1) as i:
                gates(i, False)
            gates(N_GATES // 4 - 1, True)
            load_tile(T_ADA + RAW + 1)
            sp.wait_ge(p_full, 4 * N_UNITS)
            for k in (1, 2):
                sp.dma_start(lat[k][:], lat_d[k]).then_inc(lat_in[k], 16)
            for t in range(T_ADA + RAW + 2, T_ADA + RAW + 6):
                load_tile(t)
            for k in range(KQ, KQ + KKV):
                sp.wait_ge(nrm, 1)
                sp.dma_start(lat[k][:], lat_d[k]).then_inc(lat_in[k - KQ], 16)
            sp.dma_start(bg[:], b_gate.to_broadcast([P, D])).then_inc(bg_in, 16)
            sp.dma_start(gp[:], g_post.to_broadcast([P, D])).then_inc(bg_in, 16)
            for t in range(T_ADA + RAW + 6, T_ADA + RAW + KD):
                load_tile(t)
            sp.wait_ge(nrm, KQ * NCH)
            sp.dma_start(r_lat[:], r_d[1:2].to_broadcast([P, SEQ])).then_inc(r_in, 16)
            sp.wait_ge(tab_out, 16)
            sp.wait_ge(g_gate, KD)
            sp.wait_ge(gg_step, 2)
            sp.wait_ge(nrm_lo, (KQ - 1) * NCH)
            for j in range(4):
                rows = slice(HALF * j, HALF * (j + 1))

                def turned(a):
                    return tab_d[a].rearrange("(c f) t -> f c t", c=NCH)

                sp.dma_start(cos_t[rows, :].rearrange("p (c t) -> p c t", c=NCH), turned(0)).then_inc(ct_in, 16)
                sp.dma_start(sin_t[rows, :].rearrange("p (c t) -> p c t", c=NCH),
                             turned(2 if j % 2 == 0 else 1)).then_inc(ct_in, 16)

            def rope_load(n):
                src = lat_d[N_LAT - 1] if n == 0 else qr_d[n - 1]
                if n == 0:
                    sp.wait_ge(nrm_hi, (KQ + KKV) * NCH)
                    sp.wait_ge(nrm_lo, (KQ + KKV - 2) * NCH)
                    sp.wait_ge(nrm_lo_g, 2 * NCH)
                else:
                    sp.wait_ge(st_out[(n - 1) % 2], 16 * ((M0 + n - 1) // 2 + 1))
                    if n == 1:
                        sp.wait_ge(kr_lo_r, NCH)
                    else:
                        sp.wait_ge(rp_out, 16 * (n - 1))
                sp.dma_start(rope_a[:], src).then_inc(ra_in, 16)
                for j in range(4):
                    o = j ^ 1
                    sp.dma_start(rope_b[HALF * j:HALF * (j + 1), :],
                                 src[HALF * o:HALF * (o + 1), :]).then_inc(ra_in, 16)

            def rope_store(n):
                sp.wait_ge(rp_step, 3 * (n + 1))
                sp.dma_start(roped_d[n - 1], rope_a[:]).then_inc(rp_out, 16)

            def load_k(h):
                sp.dma_start(a_raw[0][:], k_d[h]).then_inc(a_in[0], 16)

            def load_q(h):
                sp.dma_start(a_raw[1][:], q_d[h]).then_inc(a_in[1], 16)

            def load_qr(pair, half):
                for d in range(2):
                    sp.dma_start(a_raw[2][ROPE * d:ROPE * (d + 1), :],
                                 roped_d[pair, ROPE * half:ROPE * (half + 1), :]).then_inc(a_in[2], 16)

            def load_v(h):
                sp.dma_start(a_raw[0][:].rearrange("p (b n) -> p b n", b=SB),
                             v_d[:, :, bass.ds(h * VD, VD)].rearrange("b p n -> p b n")).then_inc(a_in[0], 16)

            def load_sz(h, g):
                sp.dma_start(sz[:, g % 2, :], gate_d[h, :, chunk(g)]).then_inc(sz_in[g % 2], 16)

            for g in range(G_UNITS):
                if g < G_V:
                    load_tile(T_QR + g + RAW)
                elif g == G_V:
                    load_tile(T_V + RAW)
                    load_tile(T_V + 1 + RAW)
                elif g >= G_K:
                    load_tile(T_K + g - G_K + RAW)
                if g < G_V:
                    dst = qr_d[g]
                elif g < G_K:
                    b = 2 * (g - G_V)
                    dst = v_d[b:b + 2].rearrange("b p n -> p b n")
                elif g < G_Q:
                    dst = k_d[g - G_K]
                else:
                    dst = q_d[g - G_Q]
                for s in range(NCH):
                    sp.wait_ge(banks(g_free, g)[s], g // 2 + 2)
                src = stage[:, g % 2, :]
                if G_V <= g < G_K:
                    src = src.rearrange("p (b n) -> p b n", b=2)
                sp.dma_start(dst, src).then_inc(st_out[g % 2], 16)
                if g in ROPE_AT:
                    rope_load(ROPE_AT.index(g))
                if g - 2 in ROPE_AT[1:]:
                    rope_store(ROPE_AT.index(g - 2))
                if g == G_Q + 3:
                    sp.wait_ge(rp_out, 16 * (HEADS // 2))
                    sp.wait_ge(st_out[G_K % 2], 16 * ((M0 + G_K) // 2 + 1))
                    load_k(0)
                    load_qr(0, 0)
                if g == G_Q + 3:
                    sp.wait_ge(st_out[G_Q % 2], 16 * ((M0 + G_Q) // 2 + 1))
                    load_q(0)

            for n in range(2):
                sp.wait_ge(st_out[n], 16 * ((M0 + G_UNITS) // 2))
            sp.wait_ge(fk_lo, NCH)
            load_v(0)
            sp.wait_ge(g_full, 4 * G_UNITS)
            load_sz(0, 0)
            load_sz(0, 1)

            def load_e(src, k, cols):
                sp.dma_start(e_raw[:, k, :], src[k, :, cols]).then_inc(x_in[k], 16)

            def head(h, last, pair=None, half=None):
                if not last:
                    sp.wait_ge(fq_lo, NCH * h + NCH)
                    settle()
                    load_q(h + 1)
                    sp.wait_ge(fr_lo, NCH * h + NCH)
                    settle()
                    load_qr(pair, half)
                    sp.wait_ge(fv_lo, NCH * h + NCH)
                    load_k(h + 1)
                for g in range(4):
                    if g == 3 and not last:
                        sp.wait_ge(fk_lo, NCH * h + 2 * NCH)
                        settle()
                        load_v(h + 1)
                    if g == 2 and last:
                        sp.wait_ge(s_full, N_STEPS * HEADS)
                        for k in range(KD):
                            load_e(y_d, k, chunk(0))
                        sp.wait_ge(fr_lo, NCH * HEADS)
                        for n in range(4):
                            sp.dma_start(gr[:, n, :], gate_d[KD + n, :, chunk(0)]).then_inc(gr_in[n], 16)
                    sp.wait_ge(o_ready, 4 * h + (g + 2))
                    sp.dma_start(o_d[h, :, chunk(g)], sz[:, g % 2, :]).then_inc(o_out[g % 2], 16)
                    if g < 2 or not last:
                        sp.wait_ge(o_out[g % 2], 32 * h + 16 * (g // 2 + 1))
                        if g < 2:
                            load_sz(h, g + 2)
                        else:
                            load_sz(h + 1, g - 2)

            with sp.Fori(0, HEADS // 2 - 1) as j:
                head(2 * j, False, j, 1)
                head(2 * j + 1, False, j + 1, 0)
            head(HEADS - 2, False, HEADS // 2 - 1, 1)
            head(HEADS - 1, True)
            for s in range(2):
                sp.wait_ge(o_out[s], 32 * HEADS)
            for k in range(KD):
                sp.wait_ge(e_lo, k + 1)
                load_e(o_d, k, chunk(0))
            sp.wait_ge(t_full, N_STEPS * (HEADS + 1))

            for t in range(T_MERGE + RAW, T_MERGE + RAW + 2):
                load_tile(t)

            def merge(c, last):
                cols = bass.ds(c * CH, CH)
                cols_next = bass.ds(c * CH + CH, CH)

                def load_m(j):
                    if last and j + RAW >= PER_CHUNK:
                        return
                    t = T_MERGE + RAW + j
                    load_w(t, wm[(j + RAW) % PER_CHUNK], 1024, PER_CHUNK * c + (t - RAW + 1))

                def load_gr(n):
                    m, u = (n - 4) % KD, (n - 4) // KD
                    sp.wait_ge(e_free[m], 3 * c + (u + 2))
                    sp.dma_start(gr[:, n % 4, :], gate_d[KD + n % (2 * KD), :, cols if n < 2 * KD else cols_next])\
                      .then_inc(gr_in[n % 4], 16)

                for n in range(KD):
                    if n >= 2:
                        load_m(n)
                    load_gr(n + 4)
                    if not last:
                        sp.wait_ge(e_lo, 16 * c + (KD + n + 1))
                        settle()
                        load_e(y_d, n, cols_next)
                for n in range(KD):
                    load_m(KD + n)
                    if n < 4:
                        load_gr(n + 12)
                    if n < 2:
                        sp.wait_ge(o_done, 4 * c + (n + 3))
                        sp.dma_start(x_t[:, n, :], x[4 * c + n]).then_inc(x_t_in[n], 16)
                for n in range(KD):
                    load_m(2 * KD + n)
                    if not last:
                        if n < 4:
                            load_gr(n + 2 * KD)
                        sp.wait_ge(e_lo, 16 * c + (2 * KD + n + 1))
                        settle()
                        load_e(o_d, n, cols_next)
                for b in range(4):
                    if b % 2 == 0 and not last:
                        load_m(PER_CHUNK + b // 2)
                    sp.wait_ge(o_done, 4 * c + (b + 5))
                    sp.dma_start(out[4 * c + b], o_t[:, b % 2, :]).then_inc(out_done[b % 2], 16)
                    if b < 2:
                        sp.dma_start(x_t[:, b, :], x[4 * c + (b + 2)]).then_inc(x_t_in[b], 16)

            with sp.Fori(0, NCH - 1) as c:
                merge(c, False)
            merge(NCH - 1, True)
            for s in range(2):
                sp.wait_ge(out_done[s], 16 * (2 * NCH + 1))

        @blk.gpsimd
        def _(pool):
            for b in range(8):
                pool.sem_inc(p_free[b], 1)
                pool.sem_inc(e_free[b], 1)
            for b in range(6):
                pool.sem_inc(g_free[b], 1)
            for c in range(NCH):
                pool.sem_inc(s_free[c], 1)
            for s in range(PT):
                pool.sem_inc(t_free[s], 1)
            pool.sem_inc(y_ready, 4)
            pool.sem_inc(y_out, 16)
            pool.sem_inc(t_full, N_STEPS)
            pool.sem_inc(pv_done, 1)
            pool.sem_inc(p_ready, 2)
            pool.sem_inc(o_ready, 1)
            pool.sem_inc(o_done, 4)
            for s in range(2):
                pool.sem_inc(out_done[s], 16)
            pool.memset(ones[:], 1.0).then_inc(ready, 1)
            pool.memset(ident[:], 0.0).then_inc(ready, 1)
            pool.memset(ident_b[:], 0.0).then_inc(ready, 1)
            pool.memset(mask_b[:], 0.0).then_inc(ready, 1)
            pool.wait_ge(ready, 4)
            for m in (ident, ident_b):
                pool.affine_select(out=m[:], in_=m[:], compare_op=ALU.not_equal, fill=1.0, base=0,
                                   pattern=[[-1, P]], channel_multiplier=1).then_inc(ready, 1)
            pool.affine_select(out=mask_b[:], in_=mask_b[:], compare_op=ALU.is_ge, fill=MASKED, base=0,
                               pattern=[[-1, P]], channel_multiplier=1).then_inc(ready, 1)

            pool.wait_ge(ready, 7)
            pool.wait_ge(cst_in, 16)
            for k in range(KD):
                ins = pool.tensor_scalar(c_b[:, k, :], ones[:], consts[:, C_C + k:C_C + k + 1], 1.0, ALU.mult,
                                         ALU.mult)
            ins.then_inc(cb_step, 1)

            def w_low(t, width, n):
                pool.wait_ge(whi, n)
                if T_SHARED <= t < T_QR:
                    width = CH
                pool.tensor_tensor(w_lo[:, t % 2, 0:width], w_raw[:, t % RAW, 0:width],
                                   w_hi[:, t % 2, 0:width].bitcast(F32), ALU.subtract).then_inc(wlo, 1)

            for s in range(NCH):
                pool.wait_ge(r_x_ready, s + 1)
                for k in H_LO_POOL:
                    pool.tensor_tensor(x_raw[:, k, chunk(s)], x_raw[:, k, chunk(s)], r_x[:, chunk(s)],
                                       ALU.mult).then_inc(xr_g, 1)
            for t in range(2):
                w_low(t, 1024, t + 1)
            for s in range(NCH):
                for k in H_LO_POOL:
                    pool.wait_ge(hhi_ready, KD * s + k + 1)
                    pool.tensor_tensor(h_lo[:, k, chunk(s)], x_raw[:, k, chunk(s)],
                                       h_hi[:, k, chunk(s)].bitcast(F32), ALU.subtract).then_inc(hlo_g, 1)
            for t in range(2, RAW):
                w_low(t, 1024, t + 1)
            with pool.Fori(0, (N_PROJ + 2 - RAW) // 4) as i:
                for j in range(4):
                    w_low(RAW + j, 1024, 4 * i + (RAW + j + 1))
            for t in range(N_PROJ + 2, T_QR + 2):
                w_low(t, width_of(t), t + 1)

            def lat_low(k, c, n, dst, j):
                pool.wait_ge(nrm_hi, n)
                pool.tensor_tensor(dst[0][:, j, chunk(c)], lat[k][:, chunk(c)],
                                   dst[1][:, j, chunk(c)].bitcast(F32), ALU.subtract).then_inc(nrm_lo_g, 1)

            for c in range(NCH):
                lat_low(KQ - 1, c, KQ * (c + 1), (qn_lo, qn_hi), KQ - 1)
            w_low(T_QR + 2, width_of(T_QR + 2), T_QR + 3)
            for c in range(NCH):
                lat_low(KQ + KKV - 1, c, KQ * NCH + KKV * (c + 1), (kn_lo, kn_hi), KKV - 1)
            for t in range(T_QR + 3, T_K):
                w_low(t, width_of(t), t + 1)
            for c in range(NCH):
                pool.wait_ge(kr_hi_r, c + 1)
                pool.tensor_tensor(kr_lo[:, chunk(c)], rope_a[:, chunk(c)],
                                   kr_hi[:, chunk(c)].bitcast(F32), ALU.subtract).then_inc(kr_lo_r, 1)
            for t in range(T_K, T_MERGE):
                w_low(t, width_of(t), t + 1)

            def fetch(h, what, c):
                hi, lo, slot, hi_r, lo_r = {"k": (k_hi, k_lo, 0, fk_hi, fk_lo), "q": (q_hi, q_lo, 1, fq_hi, fq_lo),
                                            "v": (v_hi, v_lo, 0, fv_hi, fv_lo)}[what]
                pool.wait_ge(hi_r, NCH * h + (c + 1))
                pool.tensor_tensor(lo[:, chunk(c)], a_raw[slot][:, chunk(c)],
                                   hi[:, chunk(c)].bitcast(F32), ALU.subtract).then_inc(lo_r, 1)

            def normalise(h, r):
                pool.wait_ge(iv_ready, SB * h + (r + 1))
                pool.sem_inc(settled, 1)
                row = prob(r)[:, 0:P * (r + 1)]
                pool.tensor_scalar(row, row, inv_sum[:, r % 2, :], 1.0, ALU.mult, ALU.mult).then_inc(p_ready, 1)

            def block_low(first, k, hi, lo):
                pool.wait_ge(e_hi, first + k + 1)
                pool.tensor_tensor(lo[:, k, :], e_raw[:, k, :], hi[:, k, :].bitcast(F32),
                                   ALU.subtract).then_inc(e_lo, 1)

            def head(h, last):
                for item in head_plan(last):
                    if item[0] == "inv":
                        normalise(h + 1 if item[1] else h, item[2])
                    elif item[0] == "fetch" and item[1] == "y":
                        block_low(0, item[2], y_hi, y_lo)
                    elif item[0] == "fetch" and item[1] == "w":
                        w_low(T_MERGE + item[2], 1024, T_MERGE + item[2] + 1)
                    elif item[0] == "fetch" and item[1] != "r":
                        fetch(h if item[1] == "v" else h + 1, item[1], item[2])

            for c in range(NCH):
                fetch(0, "k", c)
            for r in range(4):
                fetch(0, "q", r)
                normalise(0, r)
            with pool.Fori(0, HEADS - 1) as h:
                head(h, False)
            head(HEADS - 1, True)

            def merge(c, last):
                def low(j):
                    t = T_MERGE + 2 + j
                    if not (last and j + 2 >= PER_CHUNK):
                        w_low(t, 1024, PER_CHUNK * c + (t + 1))

                for k in range(KD):
                    low(k)
                    block_low(16 * c + KD, k, o_hi, o_lo)
                for j in range(KD, 2 * KD):
                    low(j)
                for k in range(KD):
                    if not last:
                        block_low(16 * c + 2 * KD, k, y_hi, y_lo)
                    low(2 * KD + k)
                if last:
                    for b in range(4):
                        residual(pool, c, b)

            for s in range(2):
                pool.wait_ge(o_out[s], 32 * HEADS)
            with pool.Fori(0, NCH - 1) as c:
                merge(c, False)
            merge(NCH - 1, True)

        @blk.scalar
        def _(act):
            def w_high(t, width, n=None):
                act.wait_ge(w_in[t % RAW], 16 * (t // RAW + 1) if n is None else n)
                act.activation(w_hi[:, t % 2, 0:width], w_raw[:, t % RAW, 0:width], ACT.Copy).then_inc(whi, 1)

            for k in range(KD):
                act.wait_ge(x_in[k], 16)
                for f in range(2):
                    n = 2 * k + f
                    half = slice(1024 * f, 1024 * (f + 1))
                    if n >= 4:
                        act.wait_ge(sq_added, n - 3)
                    act.activation(sq_sum[:, half] if k == 0 else squares[:, f, :], x_raw[:, k, half],
                                   ACT.Square).then_inc(sq_ready, 1)

            act.wait_ge(rs, 1)
            act.activation(t2[:, 0:SB], t1[:, 0:SB], ACT.Sqrt).then_inc(rs_root, 1)
            for s in range(NCH):
                act.wait_ge(r_bc, s + 1)
                act.activation(r_x[:, chunk(s)], psum[:, s, :], ACT.Copy).then_inc(r_x_ready, 1)
            w_high(0, 1024)
            w_high(1, 1024)
            act.wait_ge(tab_step, TAB_STEPS)
            act.activation(s_half[:], ang[:], ACT.Sin, scale=0.5).then_inc(tab_sin, 1)
            act.activation(tab[:, 1, :], ang[:], ACT.Sin).then_inc(tab_sin, 1)
            act.wait_ge(ada_ready, 4)
            for s in range(NCH):
                for k in range(KD):
                    act.wait_ge(h32_ready, KD * s + k + 1)
                    act.activation(h_hi[:, k, chunk(s)], x_raw[:, k, chunk(s)], ACT.Copy).then_inc(hhi_ready, 1)

            act.wait_ge(tab_out, 16)
            for t in range(N_LAT):
                for s in range(NCH):
                    b = 4 * (t % 2) + s
                    act.wait_ge(p_full, 4 * t + s + 1)
                    if t >= 2:
                        act.wait_ge(st_out[t % 2], 16 * (t // 2))
                        act.wait_ge(lat_sq, 4 * (t - 2) + s + 1)
                    act.activation(stage[:, t % 2, chunk(s)], psum[:, b, :], ACT.Copy).then_inc(p_free[b], 1)
                w_high(t + 2, 1024)
            act.wait_ge(rs, 6)
            act.activation(lat_root, lat_ms, ACT.Sqrt).then_inc(rs_root, 1)
            with act.Fori(0, KD) as i:
                for j in range(4):
                    unit = U_CONV + j
                    if j == 0:
                        for s in range(NCH):
                            act.wait_ge(p_full, 16 * i + (4 * unit + s + 1))
                            act.wait_ge(y_ready, 4 * i + (s + 1))
                            act.activation(vs[:, chunk(s)], psum[:, s, :], ACT.Copy).then_inc(p_free[s], 1)
                    if j == 3:
                        for s in range(NCH):
                            act.wait_ge(p_full, 16 * i + (4 * unit + s + 1))
                            act.wait_ge(p_free[4 + s], 2 * i + (unit // 2 + 1))
                            act.activation(vs[:, chunk(s)], psum[:, 4 + s, :], ACT.Sigmoid).then_inc(sg_ready, 1)
                    t = N_LAT + j + 2
                    act.wait_ge(p_full, 16 * i + 4 * (unit + 1))
                    w_high(t, 1024, 16 * i + 16 * (t // RAW + 1))
            def gates(i, m0, silu):
                for j in range(4):
                    unit = U_GATES + m0 + j
                    for s in range(NCH):
                        b = 4 * (j % 2) + s
                        act.wait_ge(p_full, 16 * i + (4 * unit + s + 1))
                        act.wait_ge(st_out[j % 2], 32 * i + 16 * ((N_LAT + m0 + j) // 2))
                        act.activation(stage[:, j % 2, chunk(s)], psum[:, b, :], ACT.Sigmoid)\
                           .then_inc(sg_ready if silu else p_free[b], 1)
                    t = N_LAT + N_CONV + m0 + j + 2
                    act.wait_ge(p_full, 16 * i + 4 * (unit + 1))
                    w_high(t, 1024, 16 * i + 16 * (t // RAW + 1))

            with act.Fori(0, KD // 4) as i:
                gates(i, 0, True)
            with act.Fori(0, KD // 2) as i:
                gates(i, KD, False)

            for t in range(N_PROJ + 2, T_QR + 2):
                act.wait_ge(g_gate, t - T_ADA - 1)
                w_high(t, width_of(t))

            def lat_high(c, ks, dst, base):
                for j, k in enumerate(ks):
                    act.wait_ge(nrm, base + len(ks) * c + j + 1)
                    act.activation(dst[:, j, chunk(c)], lat[k][:, chunk(c)], ACT.Copy).then_inc(nrm_hi, 1)

            for c in range(NCH):
                lat_high(c, range(KQ), qn_hi, 0)
            def fetch(h, what, c):
                dst, slot, loaded, hi_r = {"k": (k_hi, 0, 32 * h + 16, fk_hi), "q": (q_hi, 1, 16 * h + 16, fq_hi),
                                           "r": (qr_s, 2, 32 * h + 32, fr_hi), "v": (v_hi, 0, 32 * h + 32, fv_hi)}[what]
                act.wait_ge(a_in[slot], loaded)
                act.activation(dst[:, chunk(c)], a_raw[slot][:, chunk(c)], ACT.Copy).then_inc(hi_r, 1)

            for g in range(G_UNITS):
                for s in range(NCH):
                    b = 4 * (g % 2) + s
                    act.wait_ge(g_full, 4 * g + s + 1)
                    if g == G_K - 1 and s == NCH - 1:
                        w_high(T_K, width_of(T_K))
                        w_high(T_K + 1, width_of(T_K + 1))
                    act.wait_ge(st_out[g % 2], 16 * ((M0 + g) // 2))
                    act.activation(stage[:, g % 2, chunk(s)], psum[:, b, :], ACT.Copy).then_inc(g_free[b], 1)
                if g < G_V:
                    w_high(T_QR + g + 2, width_of(T_QR + g + 2))
                elif G_K <= g < G_UNITS - 2:
                    t = T_K + g - G_K + 2
                    w_high(t, width_of(t))
                if g == 0:
                    for c in range(NCH):
                        lat_high(c, range(KQ, KQ + KKV), kn_hi, KQ * NCH)
                if g == G_V + 3:
                    act.wait_ge(rp_step, 3)
                    for c in range(NCH):
                        act.activation(kr_hi[:, chunk(c)], rope_a[:, chunk(c)], ACT.Copy).then_inc(kr_hi_r, 1)
                if g == G_Q + 5:
                    for c in range(NCH):
                        fetch(0, "k", c)
                if g == G_Q + 6:
                    for c in range(NCH):
                        fetch(0, "r", c)

            def exponentials(h, r, chunks):
                g = r // 4
                if 0 in chunks:
                    act.wait_ge(nm_ready, SB * h + (r + 1))
                    act.wait_ge(t_full,
                                N_STEPS * h + (STEP0[3], N_STEPS, N_STEPS + STEP0[1], N_STEPS + STEP0[2])[g])
                for c in chunks:
                    w = score_width(r, c)
                    bank = score_bank(r, c)
                    act.activation(prob(r)[:, c * CH:c * CH + w], psum[:, bank, 0:w], ACT.Exp,
                                   bias=neg_max[:, r % 2, :], scale=SCALE,
                                   accum_out=row_sum[:, r % 2, c:c + 1]).then_inc(s_free[bank], 1)

            def turned(h, g, j, k):
                act.wait_ge(t_full, N_STEPS * h + (N_STEPS + k + 1))
                act.wait_ge(pv_done, N_STEPS * h + (k - PT + 2 if k >= PT else 1))
                cols = step_cols(g, j)
                act.activation(pt_hi[:, k % PT, cols], psum[:, 4 + k % PT, cols], ACT.Copy).then_inc(pt_hi_r, 1)

            def block_high(first, k, hi, loaded):
                act.wait_ge(x_in[k], loaded)
                act.activation(hi[:, k, :], e_raw[:, k, :], ACT.Copy).then_inc(e_hi, 1)

            def head(h, last):
                for item in head_plan(last):
                    if item[0] == "row":
                        exponentials(h + 1 if item[1] else h, item[2], range(min(2, item[2] // 4 + 1)))
                    elif item[0] == "exp":
                        exponentials(h + 1 if item[1] else h, item[2], [item[3]])
                    elif item[0] == "fetch":
                        if item[1:] == ("k", 0):
                            act.wait_ge(s_full, N_STEPS * h + N_STEPS)
                        if item[1:] == ("v", 0):
                            act.wait_ge(pv_done, N_STEPS * h + 1)
                        if item[1] == "w":
                            w_high(T_MERGE + item[2], 1024)
                        elif item[1] == "y":
                            if item[2] == 0:
                                act.wait_ge(s_full, N_STEPS * HEADS)
                            block_high(0, item[2], y_hi, 32)
                        else:
                            fetch(h if item[1] == "v" else h + 1, item[1], item[2])
                    elif item[0] == "turn":
                        turned(h, *item[1:])

            act.wait_ge(rp_step, 15)
            for r in range(4):
                fetch(0, "q", r)
                exponentials(0, r, [0])
            for n in range(2):
                act.wait_ge(st_out[n], 16 * ((M0 + G_UNITS) // 2))
            with act.Fori(0, HEADS - 1) as h:
                head(h, False)
            head(HEADS - 1, True)

            def merge(c, last):
                def high(j):
                    if last and j + 2 >= PER_CHUNK:
                        return
                    if j < 2 * KD:
                        act.wait_ge(e_full, 16 * c + (j + 1))
                    elif j < PER_CHUNK - 1:
                        act.wait_ge(e_outmm, (KD - 1) * c + (j - 2 * KD + 1))
                    else:
                        act.wait_ge(o_full, KD * c + KD)
                    t = T_MERGE + j + 2
                    w_high(t, 1024, 16 * (PER_CHUNK // RAW) * c + 16 * (t // RAW + 1))

                def square(b):
                    for f in range(2):
                        act.wait_ge(o_full, KD * c + (2 * b + f + 1))
                        if 2 * b + f >= 2:
                            act.wait_ge(osq, 8 * c + (2 * b + f - 1))
                        act.activation(sq_t[:, f, :], psum[:, 2 * b + f, :], ACT.Square,
                                       accum_out=o_sq[:, b, f:f + 1]).then_inc(osq, 1)

                def block_root(b):
                    act.wait_ge(o_step, 24 * c + (6 * b + 2))
                    act.activation(o_st[:, b, 1:2], o_st[:, b, 0:1], ACT.Sqrt).then_inc(o_root, 1)

                for k in range(KD):
                    high(k)
                    block_high(16 * c + KD, k, o_hi, 32 * c + 48)
                for n in range(KD):
                    high(KD + n)
                    act.wait_ge(m_r, KD * c + (n + 1))
                    act.activation(m_hi[:, n, :], m_a[:, n, :], ACT.Copy).then_inc(m_hi_r, 1)
                for n in range(KD):
                    if not last:
                        block_high(16 * c + 2 * KD, n, y_hi, 32 * c + 64)
                    if n < KD - 1:
                        high(2 * KD + n)
                for b in range(4):
                    square(b)
                    if b == 2:
                        high(PER_CHUNK - 1)
                    block_root(b)

            with act.Fori(0, NCH - 1) as c:
                merge(c, False)
            merge(NCH - 1, True)

        @blk.vector
        def _(dve):
            steps = [0]

            def tab_do(ins):
                ins.then_inc(tab_step, 1)
                steps[0] += 1
                dve.wait_ge(tab_step, steps[0])

            dve.wait_ge(cst_in, 16)
            dve.wait_ge(pos_in, 16 * NCH)
            tab_do(dve.tensor_copy(ang[:], pos_i[:]))
            tab_do(dve.tensor_scalar(ang[:], ang[:], consts[:, C_INV:C_INV + 1], None, ALU.mult))
            for unit in (2048.0, 1.0):
                tab_do(dve.tensor_scalar(turns[:], ang[:], float(1.0 / (2.0 * np.pi * unit)), ROUND,
                                         ALU.mult, ALU.add))
                tab_do(dve.tensor_scalar(turns[:], turns[:], -ROUND, None, ALU.add))
                for part in TWO_PI:
                    tab_do(dve.scalar_tensor_tensor(out=ang[:], in0=turns[:], scalar=-part * unit, in1=ang[:],
                                                    op0=ALU.mult, op1=ALU.add))
            tab_do(dve.tensor_scalar(ang[:], ang[:], 3.1415925, -3.1415925, ALU.min, ALU.max))
            assert steps[0] == TAB_STEPS

            for k in range(1, KD):
                for f in range(2):
                    half = slice(1024 * f, 1024 * (f + 1))
                    dve.wait_ge(sq_ready, 2 * k + f + 1)
                    if k > 1:
                        dve.wait_ge(sq_added, 2 * k + f - 3)
                    dve.tensor_tensor(sq_sum[:, half], sq_sum[:, half], squares[:, f, :],
                                      ALU.add).then_inc(sq_added, 1)

            def diagonals(bank, dst, n):
                m = masked[:, n % 2, :].rearrange("p (b n) -> p b n", b=4)
                if n >= 2:
                    dve.wait_ge(diag_step, 2 * n - 2)
                dve.tensor_tensor(m, psum[:, bank, :].rearrange("p (b n) -> p b n", b=4),
                                  ident[:].unsqueeze(1).to_broadcast([P, 4, P]), ALU.mult).then_inc(diag_step, 1)
                dve.wait_ge(diag_step, 2 * n + 1)
                dve.tensor_reduce(dst, m, AX.X, ALU.add).then_inc(diag_step, 1)

            def rsqrt_rest(out, r, root, ms, root_n, chain, last_sem):
                dve.wait_ge(rs_root, root_n)
                dve.reciprocal(r, root).then_inc(rs, 1)
                dve.wait_ge(rs, chain + 1)
                dve.scalar_tensor_tensor(out=root, in0=r, scalar=-0.5, in1=r, op0=ALU.mult,
                                         op1=ALU.mult).then_inc(rs, 1)
                dve.wait_ge(rs, chain + 2)
                dve.tensor_tensor(root, root, ms, ALU.mult).then_inc(rs, 1)
                dve.wait_ge(rs, chain + 3)
                dve.scalar_tensor_tensor(out=out, in0=root, scalar=1.5, in1=r, op0=ALU.add,
                                         op1=ALU.mult).then_inc(last_sem, 1)

            ms, root, r_col = t1[:, 0:SB], t2[:, 0:SB], t1[:, SB:2 * SB]
            for s in range(NCH):
                dve.wait_ge(ssq_ready, s + 1)
                diagonals(s, ms[:, 4 * s:4 * s + 4], s)
            dve.wait_ge(diag_step, 2 * NCH)
            dve.tensor_scalar(ms, ms, 1.0 / D, EPS, ALU.mult, ALU.add).then_inc(rs, 1)
            rsqrt_rest(r_col, r_col, root, ms, 1, 1, rs)
            dve.wait_ge(rs, 5)
            for b in range(SB):
                dve.tensor_scalar(diag[:, b, :], ident[:], r_col[:, b:b + 1], None, ALU.mult).then_inc(diag_ready, 1)
            for s in range(NCH):
                dve.wait_ge(r_x_ready, s + 1)
                for k in range(KD):
                    if k not in H_LO_POOL:
                        dve.tensor_tensor(x_raw[:, k, chunk(s)], x_raw[:, k, chunk(s)], r_x[:, chunk(s)],
                                          ALU.mult).then_inc(xr_ready, 1)
            for j in range(4):
                dve.wait_ge(ada_ready, j + 1)
                diagonals(4 + j, b_col[:, 4 * j:4 * j + 4], 4 + j)
            dve.wait_ge(diag_step, 4 * NCH)
            dve.tensor_tensor(b_col[:], b_col[:], consts[:, C_BADA:C_BADA + 2 * KD], ALU.add).then_inc(ab_step, 1)
            dve.wait_ge(ab_step, 1)
            dve.scalar_tensor_tensor(out=a_col[:], in0=b_col[:, KD:2 * KD], scalar=1.0,
                                     in1=consts[:, C_GPRE:C_GPRE + KD], op0=ALU.add,
                                     op1=ALU.mult).then_inc(ab_step, 1)
            dve.wait_ge(ab_step, 2)
            for s in range(NCH):
                for k in range(KD):
                    if k in H_LO_POOL:
                        dve.wait_ge(xr_g, len(H_LO_POOL) * s + H_LO_POOL.index(k) + 1)
                    else:
                        dve.wait_ge(xr_ready, len(H_LO_VEC) * s + H_LO_VEC.index(k) + 1)
                    dve.tensor_scalar(x_raw[:, k, chunk(s)], x_raw[:, k, chunk(s)], a_col[:, k:k + 1],
                                      b_col[:, k:k + 1], ALU.mult, ALU.add).then_inc(h32_ready, 1)
                for k in range(KD):
                    if k not in H_LO_POOL:
                        dve.wait_ge(hhi_ready, KD * s + k + 1)
                        dve.tensor_tensor(h_lo[:, k, chunk(s)], x_raw[:, k, chunk(s)],
                                          h_hi[:, k, chunk(s)].bitcast(F32), ALU.subtract).then_inc(hlo_v, 1)

            dve.wait_ge(tab_sin, 1)
            dve.scalar_tensor_tensor(out=tab[:, 0, :], in0=s_half[:], scalar=-2.0, in1=s_half[:],
                                     op0=ALU.mult, op1=ALU.mult).then_inc(tab_step, 1)
            dve.wait_ge(tab_step, TAB_STEPS + 1)
            dve.tensor_scalar(tab[:, 0, :], tab[:, 0, :], 1.0, None, ALU.add).then_inc(tab_ready, 1)
            dve.wait_ge(tab_sin, 2)
            dve.tensor_scalar(tab[:, 2, :], tab[:, 1, :], -1.0, None, ALU.mult).then_inc(tab_ready, 1)
            for t in range(KQ + KKV):
                dst = vs if t < KQ else cv
                for s in range(NCH):
                    dve.wait_ge(p_free[4 * (t % 2) + s], t // 2 + 2)
                    st = stage[:, t % 2, chunk(s)]
                    if t in (0, KQ):
                        dve.tensor_tensor(dst[:, chunk(s)], st, st, ALU.mult).then_inc(lat_sq, 1)
                    else:
                        dve.tensor_tensor(u[:, chunk(s)], st, st, ALU.mult).then_inc(lat_sq, 1)
                        dve.wait_ge(lat_sq, 4 * t + s + 1)
                        if t == 2:
                            dve.wait_ge(lat_add, s + 1)
                        dve.tensor_tensor(dst[:, chunk(s)], dst[:, chunk(s)], u[:, chunk(s)],
                                          ALU.add).then_inc(lat_add, 1)
            for n in range(2):
                for s in range(NCH):
                    b = 4 * n + s
                    m = masked[:, b % 2, :].rearrange("p (b n) -> p b n", b=4)
                    dve.wait_ge(p_full, 4 * (U_SSQ + n) + s + 1)
                    if b >= 2:
                        dve.wait_ge(diag_step, 4 * NCH + b - 1)
                    dve.tensor_tensor(m, psum[:, b, :].rearrange("p (b n) -> p b n", b=4),
                                      ident[:].unsqueeze(1).to_broadcast([P, 4, P]), ALU.mult).then_inc(p_free[b], 1)
                    dve.wait_ge(p_free[b], U_SSQ // 2 + 2)
                    dve.tensor_reduce(lat_ms[:, 4 * b:4 * b + 4], m, AX.X, ALU.add).then_inc(diag_step, 1)
            for n, width in enumerate((Q_LORA, KV_LORA)):
                dve.wait_ge(diag_step, 4 * NCH + 4 * (n + 1))
                cols = lat_ms[:, SB * n:SB * (n + 1)]
                ins = dve.tensor_scalar(cols, cols, 1.0 / width, EPS, ALU.mult, ALU.add)
            ins.then_inc(rs, 1)
            rsqrt_rest(r_lat_col, r_lat_col, lat_root, lat_ms, 2, 6, r_ready)
            dve.memset(u[:, 0:2], 0.0).then_inc(u_zero, 1)
            dve.wait_ge(u_zero, 1)
            with dve.Fori(0, KD) as i:
                n = U_CONV // 2 + 2
                for s in range(NCH):
                    dve.wait_ge(p_full, 16 * i + (4 * (U_CONV + 1) + s + 1))
                    dve.wait_ge(p_free[s], 2 * i + n)
                    dve.tensor_tensor(u[:, 2 + s * CH:2 + (s + 1) * CH], psum[:, 4 + s, :], vs[:, chunk(s)],
                                      ALU.mult).then_inc(p_free[4 + s], 1)
                for s in range(NCH):
                    dve.wait_ge(p_free[4 + s], 2 * i + n)
                dve.wait_ge(y_out, 16 * i + 16)
                for tap in range(CONV_K):
                    col = C_CONV + tap * KD
                    w_tap = consts[:, bass.ds(i + col, 1)]
                    if tap == 0:
                        dve.tensor_scalar(cv[:], u[:, 0:SEQ], w_tap, None, ALU.mult).then_inc(cv_step, 1)
                    else:
                        dve.wait_ge(cv_step, 3 * i + tap)
                        dve.scalar_tensor_tensor(out=cv[:], in0=u[:, tap:tap + SEQ], scalar=w_tap, in1=cv[:],
                                                 op0=ALU.mult, op1=ALU.add).then_inc(cv_step, 1)
                dve.wait_ge(cv_step, 3 * i + 3)
                for s in range(NCH):
                    dve.wait_ge(p_full, 16 * i + (4 * (U_CONV + 2) + s + 1))
                    dve.tensor_tensor(cv[:, chunk(s)], psum[:, s, :], cv[:, chunk(s)],
                                      ALU.mult).then_inc(p_free[s], 1)
                for s in range(NCH):
                    dve.wait_ge(sg_ready, 4 * i + (s + 1))
                    dve.tensor_tensor(vs[:, chunk(s)], psum[:, 4 + s, :], vs[:, chunk(s)],
                                      ALU.mult).then_inc(p_free[4 + s], 1)
                for s in range(NCH):
                    dve.wait_ge(p_free[4 + s], 2 * i + (n + 1))
                    dve.wait_ge(p_free[s], 2 * i + (n + 1))
                    dve.tensor_tensor(cv[:, chunk(s)], vs[:, chunk(s)], cv[:, chunk(s)],
                                      ALU.mult).then_inc(y_ready, 1)
            with dve.Fori(0, KD // 4) as i:
                for j in range(4):
                    for s in range(NCH):
                        b = 4 * (j % 2) + s
                        dve.wait_ge(sg_ready, 16 * i + (4 * KD + 4 * j + s + 1))
                        dve.tensor_tensor(stage[:, j % 2, chunk(s)], psum[:, b, :], stage[:, j % 2, chunk(s)],
                                          ALU.mult).then_inc(p_free[b], 1)

            dve.tensor_copy(c_hi[:], consts[:, C_C:C_C + KD]).then_inc(cb_step, 1)
            dve.wait_ge(cb_step, 2)
            dve.tensor_tensor(c_lo[:], consts[:, C_C:C_C + KD], c_hi[:].bitcast(F32),
                              ALU.subtract).then_inc(cb_step, 1)
            dve.wait_ge(cb_step, 3)
            for k in range(KD):
                dve.tensor_scalar(c_b_hi[:, k, :], ones[:], c_hi[:, k:k + 1].bitcast(F32), None,
                                  ALU.mult).then_inc(cb_step, 1)
                dve.tensor_scalar(c_b_lo[:, k, :], ones[:], c_lo[:, k:k + 1], None,
                                  ALU.mult).then_inc(cb_step, 1)

            for t in range(T_SHARED, T_QR):
                dve.wait_ge(whi, t + 1)
                dve.tensor_tensor(w_lo[:, t % 2, chunk(1)], w_raw[:, t % RAW, chunk(1)],
                                  w_hi[:, t % 2, chunk(1)].bitcast(F32), ALU.subtract).then_inc(wlo_v, 1)

            def lat_norm(c, ks, r_n, g0):
                dve.wait_ge(r_in, r_n)
                for k in ks:
                    dve.wait_ge(lat_in[k % KQ], 16 * (k // KQ + 1))
                    dve.scalar_tensor_tensor(out=lat[k][:, chunk(c)], in0=lat[k][:, chunk(c)],
                                             scalar=consts[:, g0 + k:g0 + k + 1], in1=r_lat[:, chunk(c)],
                                             op0=ALU.mult, op1=ALU.mult).then_inc(nrm, 1)

            def lat_low(c, ks, hi, lo, base):
                for j, k in enumerate(ks):
                    if j == len(ks) - 1:
                        continue
                    dve.wait_ge(nrm_hi, base + len(ks) * c + j + 1)
                    dve.tensor_tensor(lo[:, j, chunk(c)], lat[k][:, chunk(c)], hi[:, j, chunk(c)].bitcast(F32),
                                      ALU.subtract).then_inc(nrm_lo, 1)

            for c in range(NCH):
                lat_norm(c, range(KQ), 16, C_GQ)
                lat_low(c, range(KQ), qn_hi, qn_lo, 0)
            dve.wait_ge(bg_in, 32)
            dve.wait_ge(g_gate, KD)
            for f in range(2):
                half = slice(f * CH, (f + 1) * CH)
                dve.tensor_tensor(gg[:, half], psum[:, 6 + f, :], bg[:, half], ALU.add).then_inc(g_free[6 + f], 1)
                dve.wait_ge(g_free[6 + f], 1)
                dve.tensor_tensor(gg[:, half], gg[:, half], gp[:, half], ALU.mult).then_inc(gg_step, 1)
            for c in range(NCH):
                lat_norm(c, range(KQ, KQ + KKV), 32, C_GQ)
                lat_low(c, range(KQ, KQ + KKV), kn_hi, kn_lo, KQ * NCH)
            dve.wait_ge(ct_in, 16 * 8)
            for n in range(5):
                dve.wait_ge(ra_in, 80 * (n + 1))
                dve.tensor_tensor(rope_a[:], rope_a[:], cos_t[:], ALU.mult).then_inc(rp_step, 1)
                dve.tensor_tensor(rope_b[:], rope_b[:], sin_t[:], ALU.mult).then_inc(rp_step, 1)
                dve.wait_ge(rp_step, 3 * n + 2)
                dve.tensor_tensor(rope_a[:], rope_a[:], rope_b[:], ALU.add).then_inc(rp_step, 1)

            MX = N_STEPS + SB

            def rotary_low(h, c):
                dve.wait_ge(fr_hi, NCH * h + (c + 1))
                dve.tensor_tensor(qr_s[ROPE:P, chunk(c)], a_raw[2][ROPE:P, chunk(c)],
                                  qr_s[ROPE:P, chunk(c)].bitcast(F32), ALU.subtract).then_inc(fr_lo, 1)

            def row_maximum(h, r, c):
                dve.wait_ge(s_full, N_STEPS * h + (score_base(r) + c + 1))
                dve.tensor_reduce(row_max[:, r % 2, c:c + 1], psum[:, score_bank(r, c), 0:score_width(r, c)],
                                  AX.X, ALU.max).then_inc(mx_step, 1)

            def row_shift(h, r):
                nb = r // 4 + 1
                done = MX * h + (score_base(r) + r + nb)
                dve.wait_ge(mx_step, done)
                dve.tensor_reduce(all_sum[:, 2, :], row_max[:, r % 2, 0:nb], AX.X, ALU.max).then_inc(mx_step, 1)
                dve.wait_ge(mx_step, done + 1)
                dve.tensor_scalar(neg_max[:, r % 2, :], all_sum[:, 2, :], -SCALE, None,
                                  ALU.mult).then_inc(nm_ready, 1)

            def row_inverse(h, r):
                nb = r // 4 + 1
                for c in range(nb):
                    dve.wait_ge(s_free[score_bank(r, c)], BANK_USES * h + (score_use(r, c) + 2))
                dve.tensor_reduce(all_sum[:, r % 2, :], row_sum[:, r % 2, 0:nb], AX.X, ALU.add).then_inc(iv_step, 1)
                dve.wait_ge(iv_step, SB * h + (r + 1))
                dve.wait_ge(p_ready, SB * h + (r + 1))
                dve.reciprocal(inv_sum[:, r % 2, :], all_sum[:, r % 2, :]).then_inc(iv_ready, 1)

            def head(h, last):
                for item in vector_plan(last):
                    if item[0] == "max":
                        row_maximum(h + 1 if item[1] else h, *item[2:])
                    elif item[0] == "shift":
                        row_shift(h + 1 if item[1] else h, item[2])
                    elif item[0] == "inv":
                        row_inverse(h + 1 if item[1] else h, item[2])
                    elif item[0] == "fetch":
                        rotary_low(h + 1, item[2])
                    elif item[0] == "turn":
                        g, j, k = item[1:]
                        cols = step_cols(g, j)
                        dve.wait_ge(pt_hi_r, N_STEPS * h + (k + 1))
                        dve.tensor_tensor(pt_lo[:, k % PT, cols], psum[:, 4 + k % PT, cols],
                                          pt_hi[:, k % PT, cols].bitcast(F32),
                                          ALU.subtract).then_inc(t_free[k % PT], 1)
                    elif item[0] == "out":
                        g = item[1]
                        dve.wait_ge(pv_done, N_STEPS * h + (STEP0[g] + STEPS[g] + 1))
                        dve.wait_ge(sz_in[g % 2], 32 * h + 16 * (g // 2 + 1))
                        dve.tensor_tensor(sz[:, g % 2, :], psum[:, 7, :], sz[:, g % 2, :],
                                          ALU.mult).then_inc(o_ready, 1)

            for c in range(NCH):
                rotary_low(0, c)
            for r in range(4):
                row_maximum(0, r, 0)
                row_shift(0, r)
                row_inverse(0, r)
            with dve.Fori(0, HEADS - 1) as h:
                head(h, False)
            head(HEADS - 1, True)

            def merge(c, last):
                for n in range(KD):
                    dve.wait_ge(e_full, 16 * c + (n + 1))
                    dve.wait_ge(gr_in[n % 4], 64 * c + 16 * (n // 4 + 1))
                    dve.tensor_tensor(m_a[:, n, :], psum[:, n, :], gr[:, n % 4, :], ALU.mult).then_inc(e_free[n], 1)

                def low(n):
                    dve.wait_ge(m_hi_r, KD * c + (n + 1))
                    dve.tensor_tensor(m_lo[:, n, :], m_a[:, n, :], m_hi[:, n, :].bitcast(F32),
                                      ALU.subtract).then_inc(m_lo_r, 1)

                for n in range(KD):
                    dve.wait_ge(e_full, 16 * c + (KD + n + 1))
                    dve.wait_ge(gr_in[n % 4], 64 * c + 16 * (2 + n // 4 + 1))
                    if n >= 2:
                        dve.wait_ge(m_r, KD * c + (n - 1))
                    dve.tensor_tensor(e_t[:, n % 2, :], psum[:, n, :], gr[:, n % 4, :],
                                      ALU.mult).then_inc(e_free[n], 1)
                    dve.wait_ge(e_free[n], 3 * c + 3)
                    dve.tensor_tensor(m_a[:, n, :], m_a[:, n, :], e_t[:, n % 2, :], ALU.add).then_inc(m_r, 1)
                    if n >= 1:
                        low(n - 1)
                low(KD - 1)
                def root(b):
                    st = lambda k: o_st[:, b, k:k + 1]
                    base = 24 * c + 6 * b
                    dve.wait_ge(osq, 8 * c + (2 * b + 2))
                    dve.tensor_tensor(st(0), o_sq[:, b, 0:1], o_sq[:, b, 1:2], ALU.add).then_inc(o_step, 1)
                    dve.wait_ge(o_step, base + 1)
                    dve.tensor_scalar(st(0), st(0), 1.0 / D, EPS, ALU.mult, ALU.add).then_inc(o_step, 1)
                    dve.wait_ge(o_root, 4 * c + (b + 1))
                    dve.reciprocal(st(2), st(1)).then_inc(o_step, 1)
                    dve.wait_ge(o_step, base + 3)
                    dve.scalar_tensor_tensor(out=st(3), in0=st(2), scalar=-0.5, in1=st(2), op0=ALU.mult,
                                             op1=ALU.mult).then_inc(o_step, 1)
                    dve.wait_ge(o_step, base + 4)
                    dve.tensor_tensor(st(3), st(3), st(0), ALU.mult).then_inc(o_step, 1)
                    dve.wait_ge(o_step, base + 5)
                    dve.scalar_tensor_tensor(out=st(2), in0=st(3), scalar=1.5, in1=st(2), op0=ALU.add,
                                             op1=ALU.mult).then_inc(o_step, 1)

                def gated(b):
                    dve.wait_ge(o_step, 24 * c + 6 * b + 6)
                    dve.wait_ge(out_done[b % 2], 32 * c + 16 * (b // 2 + 1))
                    for f in range(2):
                        half = slice(f * CH, (f + 1) * CH)
                        dve.scalar_tensor_tensor(out=o_t[:, b % 2, half], in0=psum[:, 2 * b + f, :],
                                                 scalar=o_st[:, b, 2:3], in1=gg[:, half], op0=ALU.mult,
                                                 op1=ALU.mult).then_inc(e_free[2 * b + f], 1)

                if last:
                    for b in range(4):
                        root(b)
                        gated(b)
                else:
                    root(0)
                    gated(0)
                    root(1)
                    gated(1)
                    residual(dve, c, 0)
                    root(2)
                    residual(dve, c, 1)
                    root(3)
                    for b in (2, 3):
                        gated(b)
                        residual(dve, c, b)

            with dve.Fori(0, NCH - 1) as c:
                merge(c, False)
            merge(NCH - 1, True)

        @blk.tensor
        def _(pe):
            pe.wait_ge(ready, 7)
            def ada(k):
                for n, ks in enumerate(WA_LOADS):
                    if k == ks[0]:
                        pe.wait_ge(wa_in[n], 16)
                for j in range(4):
                    last = pe.matmul(psum[:, 4 + j, :], c_b[:, k, :], wa[:, k, chunk(j)], start=k == 0,
                                     stop=k == KD - 1)
                    if k == KD - 1:
                        last.then_inc(ada_ready, 1)

            pe.wait_ge(cb_step, 1)
            ada(0)
            ada(1)
            for s in range(NCH):
                pe.wait_ge(sq_added, 2 * KD - 2 if s >= 2 else 2 * KD - 3)
                pe.matmul(psum[:, s, :], ones[:], sq_sum[:, chunk(s)], start=True, stop=True).then_inc(ssq_ready, 1)
            ada(2)
            ada(3)
            for b in range(SB):
                pe.wait_ge(diag_ready, b + 1)
                last = pe.matmul(psum[:, b // 4, block(b % 4)], ones[:], diag[:, b, :], start=True, stop=True,
                                 skip_group_check=True)
                if b % 4 == 3:
                    last.then_inc(r_bc, 1)
            for k in range(4, KD):
                ada(k)

            def w_tile(p, k, n=P):
                return w_hi[:, p, k * n:(k + 1) * n], w_lo[:, p, k * n:(k + 1) * n]

            def unit(p, kk, x_hi, x_lo, full, free, tile_n, free_n, before=None):
                pe.wait_ge(wlo, tile_n)
                for s in range(NCH):
                    pe.wait_ge(free[4 * p + s], free_n)
                    for k in range(kk):
                        if before:
                            before(s, k)
                        last = accumulate(pe, psum[:, 4 * p + s, :],
                                          parts(*w_tile(p, k), x_hi[:, k, chunk(s)], x_lo[:, k, chunk(s)]),
                                          start=k == 0, stop=k == kk - 1)
                    last.then_inc(full, 1)

            def h_chunk(s, k):
                if k in H_LO_POOL:
                    pe.wait_ge(hlo_g, len(H_LO_POOL) * s + H_LO_POOL.index(k) + 1)
                else:
                    pe.wait_ge(hlo_v, len(H_LO_VEC) * s + H_LO_VEC.index(k) + 1)

            for t in range(N_LAT):
                unit(t % 2, KD, h_hi, h_lo, p_full, p_free, t + 1, t // 2 + 1, h_chunk if t == 0 else None)
            for n, src in enumerate((vs, cv)):
                for s in range(NCH):
                    pe.wait_ge(p_free[4 * n + s], U_SSQ // 2 + 1)
                    pe.wait_ge(lat_add, 4 * (KQ - 2) + s + 1 if n == 0 else 4 * (KQ - 1) + s + 1)
                    pe.matmul(psum[:, 4 * n + s, :], ones[:], src[:, chunk(s)], start=True,
                              stop=True).then_inc(p_full, 1)
            with pe.Fori(0, (N_CONV + N_GATES) // 4) as i:
                for j in range(4):
                    unit(j % 2, KD, h_hi, h_lo, p_full, p_free, 4 * i + (N_LAT + j + 1),
                         2 * i + (U_CONV // 2 + j // 2 + 1))

            for b in range(8):
                pe.wait_ge(p_free[b], N_UNITS // 2 + 1)
            pe.wait_ge(cb_step, 3 + 2 * KD)
            for k in range(KD):
                t = T_ADA + k
                pe.wait_ge(wlo, t + 1)
                if t >= T_SHARED:
                    pe.wait_ge(wlo_v, t - T_SHARED + 1)
                for f in range(2):
                    last = accumulate(pe, psum[:, 6 + f, :],
                                      parts(c_b_hi[:, k, :], c_b_lo[:, k, :], w_hi[:, t % 2, chunk(f)],
                                            w_lo[:, t % 2, chunk(f)]), start=k == 0, stop=k == KD - 1)
                last.then_inc(g_gate, 1)

            def qn_chunk(s, k):
                if k == KQ - 1:
                    pe.wait_ge(nrm_lo_g, s + 1)
                else:
                    pe.wait_ge(nrm_lo, (KQ - 1) * s + k + 1)

            for g in range(G_V):
                unit(g % 2, KQ, qn_hi, qn_lo, g_full, g_free, T_QR + g + 1, g // 2 + 1, qn_chunk if g == 0 else None)
            pe.wait_ge(wlo, T_V + KKV)
            for g in range(G_V, G_K):
                for s in range(NCH):
                    b, f = 2 * (g - G_V) + s // 2, s % 2
                    pe.wait_ge(nrm_lo, (KQ - 1) * NCH + (KKV - 1) * (b // 4 + 1))
                    pe.wait_ge(nrm_lo_g, NCH + b // 4 + 1)
                    bank = 4 * (g % 2) + s
                    pe.wait_ge(g_free[bank], g // 2 + 1)
                    pairs = []
                    for k in range(KKV):
                        pairs += parts(kn_hi[:, k, block(b)], kn_lo[:, k, block(b)],
                                       w_hi[:, k, chunk(f)], w_lo[:, k, chunk(f)])
                    accumulate(pe, psum[:, bank, :], pairs).then_inc(g_full, 1)
            for first, tile, kk, hi, lo in ((G_K, T_K, KKV, kn_hi, kn_lo), (G_Q, T_Q, KQ, qn_hi, qn_lo)):
                with pe.Fori(0, HEADS // 2) as i:
                    for j in range(2):
                        unit(j, kk, hi, lo, g_full, g_free, 2 * i + (tile + j + 1), i + (first // 2 + 1))

            for b in range(4):
                pe.wait_ge(g_free[b], G_UNITS // 2 + 1)
            pe.wait_ge(kr_lo_r, NCH)

            def scores(h, r):
                nb = r // 4 + 1
                pe.wait_ge(fk_lo, NCH * h + nb)
                pe.wait_ge(fq_lo, NCH * h + nb)
                pe.wait_ge(fr_lo, NCH * h + nb)
                for c in range(nb):
                    w = score_width(r, c)
                    cols = slice(c * CH, c * CH + w)
                    bank = psum[:, score_bank(r, c), 0:w]
                    pe.wait_ge(s_free[score_bank(r, c)], BANK_USES * h + (score_use(r, c) + 1))
                    rows = block(r)
                    pe.matmul(bank, q_hi[:, rows], k_lo[:, cols], start=True, stop=False)
                    pe.matmul(bank, q_lo[:, rows], k_hi[:, cols], start=False, stop=False)
                    pe.matmul(bank, qr_s[:, rows], kr_lo[:, cols], start=False, stop=False)
                    pe.matmul(bank, qr_s[:, rows], kr_hi[:, cols], start=False, stop=False)
                    if c == nb - 1:
                        pe.matmul(bank[:, w - P:w], ident_b[:], mask_b[:], start=False, stop=False)
                    pe.matmul(bank, q_hi[:, rows], k_hi[:, cols], start=False, stop=True).then_inc(s_full, 1)

            def head(h, last):
                for item in head_plan(last):
                    if item[0] == "row":
                        scores(h + 1 if item[1] else h, item[2])
                    elif item[0] == "turn":
                        g, j, k = item[1:]
                        slot = k % PT
                        pe.wait_ge(t_free[slot], T_USES[slot] * h + (k // PT + 1))
                        for i in range(max(0, j - 4 * g), 4):
                            if j == 0:
                                pe.wait_ge(p_ready, SB * h + (4 * g + i + 3))
                            ins = pe.transpose(psum[:, 4 + slot, block(i)], prob(4 * g + i)[:, block(j)], ident[:])
                        ins.then_inc(t_full, 1)
                    elif item[0] == "mul":
                        g, j, k = item[1:]
                        slot = k % PT
                        if j == 0:
                            pe.wait_ge(o_ready, 4 * h + (g + 1))
                        pe.wait_ge(fv_lo, NCH * h + (j // 4 + 1))
                        pe.wait_ge(t_free[slot], T_USES[slot] * h + (k // PT + 2))
                        cols = step_cols(g, j)
                        accumulate(pe, psum[:, 7, cols], parts(v_hi[:, block(j)], v_lo[:, block(j)],
                                                               pt_hi[:, slot, cols], pt_lo[:, slot, cols]),
                                   start=j == 0, stop=j == STEPS[g] - 1).then_inc(pv_done, 1)

            for r in range(4):
                scores(0, r)
            for b in range(4, 8):
                pe.wait_ge(g_free[b], G_UNITS // 2 + 1)
            with pe.Fori(0, HEADS - 1) as h:
                head(h, False)
            head(HEADS - 1, True)

            for c in range(NCH):
                pe.wait_ge(s_free[c], BANK_USES * HEADS + 1)
            for s in range(PT):
                pe.wait_ge(t_free[s], T_USES[s] * HEADS + 1)
            pe.wait_ge(o_ready, 4 * HEADS + 1)

            def merge(c):
                for n in range(2 * KD):
                    hi, lo = (y_hi, y_lo) if n < KD else (o_hi, o_lo)
                    pe.wait_ge(wlo, PER_CHUNK * c + (T_MERGE + n + 1))
                    pe.wait_ge(e_free[n % KD], 3 * c + (n // KD + 1))
                    for k in range(KD):
                        if n % KD == 0:
                            pe.wait_ge(e_lo, 16 * c + (n + k + 1))
                        last = accumulate(pe, psum[:, n % KD, :], parts(*w_tile(n % 2, k), hi[:, k, :], lo[:, k, :]),
                                          start=k == 0, stop=k == KD - 1)
                    last.then_inc(e_full, 1)
                for k in range(KD):
                    pe.wait_ge(wlo, PER_CHUNK * c + (T_MERGE + 2 * KD + k + 1))
                    pe.wait_ge(m_lo_r, KD * c + (k + 1))
                    for b in range(4):
                        for f in range(2):
                            if k == 0:
                                pe.wait_ge(e_free[2 * b + f], 3 * c + 3)
                            last = accumulate(pe, psum[:, 2 * b + f, :],
                                              parts(m_hi[:, k, block(b)], m_lo[:, k, block(b)],
                                                    w_hi[:, k % 2, chunk(f)], w_lo[:, k % 2, chunk(f)]),
                                              start=k == 0, stop=k == KD - 1)
                            if k == KD - 1:
                                last.then_inc(o_full, 1)
                    if k < KD - 1:
                        last.then_inc(e_outmm, 1)

            with pe.Fori(0, NCH) as c:
                merge(c)


def kernel(x, c, positions, w_ada, b_ada, g_pre, w_in, conv_w, w_conv_out, g_q, w_uq, g_kv, w_ukv,
           w_mla_out, w_out, g_post):
    import numpy as _np
    import concourse.bacc as _bacc
    from concourse import mybir as _mybir
    from concourse.bass_utils import run_bass_kernel_spmd as _run

    def cols(v, n):
        return _np.ascontiguousarray(v.reshape(n, P).T)

    def tiles(w):
        k, n = w.shape
        return w.reshape(k // P, P, n // P, P).transpose(2, 1, 0, 3).reshape(n // P, P, k)

    x, w_ada, b_ada, w_in, w_uq, w_ukv = (_np.asarray(a) for a in (x[0], w_ada[0], b_ada[0], w_in[0], w_uq[0], w_ukv[0]))
    inv_freq = (_np.float64(ROPE_THETA) ** (-_np.arange(0, ROPE, 2) / ROPE)).astype(_np.float32)
    cst = _np.concatenate([cols(_np.asarray(c[0]), KD), cols(b_ada[:2 * D], 2 * KD), cols(_np.asarray(g_pre[0]), KD),
                           cols(_np.asarray(g_q[0]), KQ), cols(_np.asarray(g_kv[0]), KKV),
                           cols(_np.asarray(conv_w[0]).reshape(-1), CONV_K * KD),
                           _np.tile(inv_freq, 4)[:, None]], axis=1)
    conv = tiles(w_in[:, :4 * D]).reshape(4, KD, P, D)
    lat0 = 4 * D
    rope0 = lat0 + Q_LORA + KV_LORA
    w_rope = w_in[:, rope0:rope0 + ROPE]
    w1 = _np.concatenate([
        tiles(w_in[:, lat0:rope0]),
        tiles(_np.concatenate([w_rope, w_rope], axis=1)),
        conv[[0, 2, 1, 3]].transpose(1, 0, 2, 3).reshape(N_CONV, P, D),
        tiles(w_in[:, rope0 + ROPE:]),
        w_ada[:, 2 * D:].reshape(KD, P, D),
    ])
    uq = w_uq.reshape(Q_LORA, HEADS, NOPE + ROPE)
    ukv = w_ukv.reshape(KV_LORA, HEADS, NOPE + VD)
    arrays = {
        "x": x.reshape(SB, P, D),
        "xt": x.T.reshape(KD, P, SEQ),
        "cst": cst,
        "pos": _np.asarray(positions),
        "b_gate": b_ada[None, 2 * D:],
        "g_post": _np.asarray(g_post),
        "wada": w_ada[:, :2 * D].reshape(KD, P, 2 * D),
        "w1": w1,
        "wqr": tiles(uq[:, :, NOPE:].reshape(Q_LORA, HEADS * ROPE)),
        "wv": ukv[:, :, NOPE:].reshape(KKV, P, HEADS * VD),
        "wk": tiles(ukv[:, :, :NOPE].reshape(KV_LORA, HEADS * NOPE)),
        "wq": tiles(uq[:, :, :NOPE].reshape(Q_LORA, HEADS * NOPE)),
        "wm": _np.concatenate([tiles(_np.asarray(w_conv_out[0])), tiles(_np.asarray(w_mla_out[0])),
                               _np.asarray(w_out[0]).reshape(KD, P, D)]),
    }
    nc = _bacc.Bacc("TRN2", target_bir_lowering=False, num_devices=1)
    args, named = {}, {}
    for name, a in arrays.items():
        a = _np.ascontiguousarray(a)
        named[f"in_{name}"] = a
        args[name] = nc.dram_tensor(f"in_{name}", a.shape, _mybir.dt.from_np(a.dtype), kind="ExternalInput").ap()
    out = nc.dram_tensor("out", (SB, P, D), F32, kind="ExternalOutput").ap()
    build(nc, out=out, **args)
    r = _run(nc, [named], core_ids=[0])
    return r.results[0]["out"].reshape(1, SEQ, D)
```
